# Optimizing a Trainium2 kernel written in Bass

```python
import jax, jax.numpy as jnp
from jax import lax
import numpy as np
import math

D_MODEL = 1024
BATCH = 1
SEQ = 512
DEPTH = 1

CHUNK = 64
Q_BLOCK = 128
HEAD_DIM = 64
N_HEADS_SB = 8
N_HEADS_FOX = 8
D_SB = N_HEADS_SB * HEAD_DIM
D_FOX = N_HEADS_FOX * HEAD_DIM
N_BRANCH = 2
IN_SIZES = (D_SB, D_SB, D_SB, D_SB,
            D_FOX, D_FOX, D_FOX, D_FOX,
            N_HEADS_FOX,
            N_BRANCH * D_MODEL)
D_IN = sum(IN_SIZES)
EPS = 1e-6
NEG_BIG = -1e30


def _rmsnorm(x, g):
    xf = x.astype(jnp.float32)
    inv = lax.rsqrt(jnp.mean(xf * xf, axis=-1, keepdims=True) + EPS)
    return (xf * inv).astype(x.dtype) * g

def _to_heads(t, n_heads):
    b, s, _ = t.shape
    return t.reshape(b, s, n_heads, HEAD_DIM).transpose(0, 2, 1, 3)

def _from_heads(t):
    b, h, s, d = t.shape
    return t.transpose(0, 2, 1, 3).reshape(b, s, h * d)

def _stick_breaking(q, k, v):
    s_len = q.shape[2]
    scale = HEAD_DIM ** -0.5
    outs = []
    for start in range(0, s_len, Q_BLOCK):
        end = start + Q_BLOCK
        qb, kb, vb = q[:, :, start:end], k[:, :, :end], v[:, :, :end]
        z = jnp.einsum('bhtd,bhsd->bhts', qb, kb).astype(jnp.float32) * scale
        t_idx = start + jnp.arange(Q_BLOCK)[:, None]
        s_idx = jnp.arange(end)[None, :]
        mask = s_idx < t_idx
        log_1m = jnp.where(mask, jax.nn.log_sigmoid(-z), 0.0)
        after = lax.cumsum(log_1m, axis=3, reverse=True) - log_1m
        w = jnp.where(mask, jnp.exp(jax.nn.log_sigmoid(z) + after), 0.0)
        outs.append(jnp.einsum('bhts,bhsd->bhtd', w.astype(vb.dtype), vb))
    return jnp.concatenate(outs, axis=2)

def _forgetting_attention(q, k, v, cum_log_f):
    s_len = q.shape[2]
    scale = HEAD_DIM ** -0.5
    outs = []
    for start in range(0, s_len, Q_BLOCK):
        end = start + Q_BLOCK
        qb, kb, vb = q[:, :, start:end], k[:, :, :end], v[:, :, :end]
        z = jnp.einsum('bhtd,bhsd->bhts', qb, kb).astype(jnp.float32) * scale
        z = z + cum_log_f[:, :, start:end, None] - cum_log_f[:, :, None, :end]
        t_idx = start + jnp.arange(Q_BLOCK)[:, None]
        s_idx = jnp.arange(end)[None, :]
        z = jnp.where(s_idx <= t_idx, z, NEG_BIG)
        p = jax.nn.softmax(z, axis=-1)
        outs.append(jnp.einsum('bhts,bhsd->bhtd', p.astype(vb.dtype), vb))
    return jnp.concatenate(outs, axis=2)

def first_inputs(seed: int = 0) -> dict:
    key = jax.random.key(seed)
    ks = jax.random.split(key, 12)
    f32 = jnp.float32
    d = D_MODEL
    x = jax.random.normal(ks[0], (BATCH, SEQ, d), f32)
    c = jax.random.normal(ks[1], (BATCH, d), f32)
    w_ada = jax.random.normal(ks[2], (DEPTH, d, 3 * d), f32) * (0.5 * d ** -0.5)
    b_ada = 0.02 * jax.random.normal(ks[3], (DEPTH, 3 * d), f32)
    norm_g = 1.0 + 0.02 * jax.random.normal(ks[4], (DEPTH, d), f32)
    w_in = jax.random.normal(ks[5], (DEPTH, d, D_IN), f32) * d ** -0.5
    b_forget = jax.random.uniform(ks[6], (DEPTH, N_HEADS_FOX), f32, 1.0, 4.0)
    w_o_sb = jax.random.normal(ks[7], (DEPTH, D_SB, d), f32) * D_SB ** -0.5
    w_o_fox = jax.random.normal(ks[8], (DEPTH, D_FOX, d), f32) * D_FOX ** -0.5
    b_gate = 0.02 * jax.random.normal(ks[9], (DEPTH, N_BRANCH * d), f32)
    w_out = jax.random.normal(ks[10], (DEPTH, d, d), f32) * d ** -0.5
    final_g = 1.0 + 0.02 * jax.random.normal(ks[11], (d,), f32)
    return {"x": x, "c": c, "w_ada": w_ada, "b_ada": b_ada, "norm_g": norm_g,
            "w_in": w_in, "b_forget": b_forget, "w_o_sb": w_o_sb, "w_o_fox": w_o_fox,
            "b_gate": b_gate, "w_out": w_out, "final_g": final_g}

def first_block(x, c, w_ada, b_ada, norm_g, w_in, b_forget, w_o_sb, w_o_fox, b_gate, w_out, final_g):
    b, s, d = x.shape
    split_points = list(np.cumsum(IN_SIZES)[:-1])
    for l in range(DEPTH):
        mod = c @ w_ada[l] + b_ada[l]
        shift, scale, gate = jnp.split(mod, 3, axis=-1)
        h = _rmsnorm(x, norm_g[l]) * (1.0 + scale[:, None, :]) + shift[:, None, :]

        proj = h @ w_in[l]
        (q_a, k_a, v_a, z_a, q_b, k_b, v_b, z_b,
         f_logit, g_logit) = jnp.split(proj, split_points, axis=-1)

        y_a = _from_heads(_stick_breaking(_to_heads(q_a, N_HEADS_SB), _to_heads(k_a, N_HEADS_SB),
                                          _to_heads(v_a, N_HEADS_SB)))
        y_a = (y_a * jax.nn.silu(z_a)) @ w_o_sb[l]

        log_f = jax.nn.log_sigmoid((f_logit + b_forget[l]).astype(jnp.float32))
        cum_log_f = jnp.cumsum(log_f, axis=1).transpose(0, 2, 1)
        y_b = _from_heads(_forgetting_attention(_to_heads(q_b, N_HEADS_FOX), _to_heads(k_b, N_HEADS_FOX),
                                                _to_heads(v_b, N_HEADS_FOX), cum_log_f))
        y_b = (y_b * jax.nn.silu(z_b)) @ w_o_fox[l]

        gates = jax.nn.sigmoid(g_logit + b_gate[l]).reshape(b, s, N_BRANCH, d)
        merged = gates[:, :, 0, :] * y_a + gates[:, :, 1, :] * y_b
        x = x + gate[:, None, :] * (merged @ w_out[l])
    return _rmsnorm(x, final_g)


QBLK = 128
MEM_LEN = 256

POOL_WIDTH = D_MODEL // 4
POOL_GROUPS = 4
POOL_GDIM = POOL_WIDTH // POOL_GROUPS
POOL_WINDOWS = (2, 4, 8, 16)

RWKV_WIDTH = D_MODEL // 4
RWKV_HEAD = 64
RWKV_HEADS = RWKV_WIDTH // RWKV_HEAD
D_DECAY_LORA = 64
D_AAA_LORA = 64
D_GATE_LORA = 128
RWKV_COLS = 3 * RWKV_WIDTH + D_DECAY_LORA + D_AAA_LORA + D_GATE_LORA
RWKV_SPLITS = tuple(int(i) for i in np.cumsum(
    [RWKV_WIDTH, RWKV_WIDTH, RWKV_WIDTH, D_DECAY_LORA, D_AAA_LORA]))
RWKV_GN_EPS = 64e-5

DIFF_WIDTH = D_MODEL // 2
DIFF_HEADS = 4
DIFF_VDIM = DIFF_WIDTH // DIFF_HEADS
DIFF_QK = DIFF_VDIM // 2
DIFF_COLS = 3 * DIFF_WIDTH

P_IN = POOL_WIDTH + RWKV_COLS + DIFF_COLS

XA_HEADS = 4
XA_HEAD = D_MODEL // XA_HEADS
D_FF = 2816
CONV_W = 3


F32 = jnp.float32

def rms_normalize(x, eps=EPS):
    xf = x.astype(F32)
    return xf * lax.rsqrt(jnp.mean(xf * xf, axis=-1, keepdims=True) + eps)

def rmsnorm(x, g):
    return (rms_normalize(x) * g.astype(F32)).astype(x.dtype)

def shift_right(x, n=1):
    return jnp.pad(x, ((0, 0), (n, 0), (0, 0)))[:, :x.shape[1]]

def alibi_slopes(n_heads):
    return jnp.asarray(2.0 ** (-8.0 * (np.arange(n_heads) + 1) / n_heads), dtype=F32)

def pool_mixer(u, w_grp, scale):
    B, S, _ = u.shape
    ug = u.astype(F32).reshape(B, S, POOL_GROUPS, POOL_GDIM)
    t = jnp.arange(S)
    outs = []
    for gi, w in enumerate(POOL_WINDOWS):
        c = jnp.cumsum(ug[:, :, gi], axis=1)
        win_sum = c - shift_right(c, w)
        count = jnp.minimum(t + 1, w).astype(F32)[None, :, None]
        outs.append(win_sum / count - ug[:, :, gi])
    d = jnp.stack(outs, axis=2)
    y = jnp.einsum('bsgc,gcd->bsgd', d, w_grp.astype(F32))
    return (y.reshape(B, S, POOL_WIDTH) * scale.astype(F32)).astype(u.dtype)

def wkv7_scan(r, decay, k, v, a_vec, b_vec):
    B, S, H, N = r.shape

    def step(s, inp):
        r_t, w_t, k_t, v_t, a_t, b_t = inp
        sa = jnp.einsum('bhvk,bhk->bhv', s, a_t)
        s = (s * w_t[:, :, None, :] + sa[..., None] * b_t[:, :, None, :]
             + v_t[..., None] * k_t[:, :, None, :])
        y = jnp.einsum('bhvk,bhk->bhv', s, r_t)
        return s, y

    seq_first = lambda a: jnp.moveaxis(a, 1, 0)
    s0 = jnp.zeros((B, H, N, N), F32)
    _, ys = lax.scan(step, s0, (seq_first(r), seq_first(decay), seq_first(k),
                                seq_first(v), seq_first(a_vec), seq_first(b_vec)))
    return jnp.moveaxis(ys, 0, 1)

def rwkv7_mixer(z, mu, w0, w2, a0, a2, g2, k_k, k_a, r_k, ln_w, ln_b):
    B, S, _ = z.shape
    H, N = RWKV_HEADS, RWKV_HEAD
    zf = z.astype(F32)
    zm = zf + mu.astype(F32) * (shift_right(zf) - zf)
    r, k, v, wd, ad, gd = jnp.split(zm, RWKV_SPLITS, axis=-1)
    w = -jax.nn.softplus(-(w0 + jnp.tanh(wd) @ w2)) - 0.5
    a = jax.nn.sigmoid(a0 + ad @ a2)
    g = jax.nn.sigmoid(gd) @ g2
    heads = lambda t: t.reshape(B, S, H, N)
    r, w, k, v, a = heads(r), heads(w), heads(k), heads(v), heads(a)
    kk = k * k_k.astype(F32).reshape(H, N)
    kk = kk / jnp.maximum(jnp.sqrt(jnp.sum(kk * kk, -1, keepdims=True)), 1e-12)
    k = k * (1.0 + (a - 1.0) * k_a.astype(F32).reshape(H, N))
    decay = jnp.exp(-jnp.exp(w))
    y = wkv7_scan(r, decay, k, v, -kk, kk * a)
    mean = jnp.mean(y, -1, keepdims=True)
    var = jnp.mean(jnp.square(y - mean), -1, keepdims=True)
    y = ((y - mean) * lax.rsqrt(var + RWKV_GN_EPS)).reshape(B, S, RWKV_WIDTH)
    y = y * ln_w.astype(F32) + ln_b.astype(F32)
    bonus = jnp.sum(r * k * r_k.astype(F32), -1, keepdims=True) * v
    y = y + bonus.reshape(B, S, RWKV_WIDTH)
    return (y * g).astype(z.dtype)

def diff_attention(z, q_norm, k_norm, lq1, lk1, lq2, lk2, subln, lambda_init):
    B, S, _ = z.shape
    H = DIFF_HEADS
    q, k, v = jnp.split(z.astype(F32), 3, axis=-1)
    q = rms_normalize(q.reshape(B, S, H, 2, DIFF_QK)) * q_norm.astype(F32)
    k = rms_normalize(k.reshape(B, S, H, 2, DIFF_QK)) * k_norm.astype(F32)
    v = v.reshape(B, S, H, DIFF_VDIM)
    lam = (jnp.exp(jnp.sum(lq1.astype(F32) * lk1.astype(F32)))
           - jnp.exp(jnp.sum(lq2.astype(F32) * lk2.astype(F32))) + lambda_init)
    slopes = alibi_slopes(H)
    nblk = S // QBLK
    qb = q.reshape(B, nblk, QBLK, H, 2, DIFF_QK).transpose(1, 0, 2, 3, 4, 5)
    kpos = jnp.arange(S)
    kchunk = kpos // CHUNK
    scale = DIFF_QK ** -0.5

    def block(args):
        q_blk, start = args
        qpos = start + jnp.arange(QBLK)
        s = jnp.einsum('bqhcd,bkhcd->bhcqk', q_blk, k) * scale
        dist = jnp.abs(qpos[:, None] - kpos[None, :]).astype(F32)
        bias = -slopes[:, None, None, None] * dist
        visible = kchunk[None, :] <= (qpos // CHUNK)[:, None]
        s = jnp.where(visible, s + bias, -jnp.inf)
        p = jax.nn.softmax(s, axis=-1)
        p = p[:, :, 0] - lam * p[:, :, 1]
        return jnp.einsum('bhqk,bkhd->bqhd', p, v)

    starts = jnp.arange(nblk) * QBLK
    o = lax.map(block, (qb, starts))
    o = jnp.moveaxis(o, 0, 1).reshape(B, S, H, DIFF_VDIM)
    o = rms_normalize(o) * subln.astype(F32) * (1.0 - lambda_init)
    return o.reshape(B, S, DIFF_WIDTH).astype(z.dtype)

def memory_cross_attention(xn, memn, wq, wk, wv, wo, q_norm, k_norm):
    B, S, _ = xn.shape
    M = memn.shape[1]
    q = rms_normalize((xn @ wq).reshape(B, S, XA_HEADS, XA_HEAD)) * q_norm.astype(F32)
    k = rms_normalize((memn @ wk).reshape(B, M, XA_HEADS, XA_HEAD)) * k_norm.astype(F32)
    v = (memn @ wv).reshape(B, M, XA_HEADS, XA_HEAD).astype(F32)
    s = jnp.einsum('bshd,bmhd->bhsm', q, k) * (XA_HEAD ** -0.5)
    p = jax.nn.softmax(s, axis=-1)
    o = jnp.einsum('bhsm,bmhd->bshd', p, v).reshape(B, S, D_MODEL).astype(xn.dtype)
    return o @ wo

def conv_ffn(xn, w_up, conv_w, conv_b, w_down):
    h = xn @ w_up
    a, b = jnp.split(h, 2, axis=-1)
    rhs = conv_w.reshape(CONV_W, 1, D_FF).astype(a.dtype)
    c = lax.conv_general_dilated(a, rhs, window_strides=(1,), padding=[(CONV_W - 1, 0)],
                                 dimension_numbers=('NWC', 'WIO', 'NWC'),
                                 feature_group_count=D_FF) + conv_b
    return (jax.nn.gelu(c, approximate=False) * b) @ w_down

def second_inputs(seed: int = 0) -> dict:
    key = jax.random.key(seed)
    ks = iter(jax.random.split(key, 40))
    nrm = lambda shape, s: jax.random.normal(next(ks), shape, F32) * s
    gain = lambda shape: 1.0 + 0.02 * jax.random.normal(next(ks), shape, F32)
    L = DEPTH
    return {
        "x": nrm((BATCH, SEQ, D_MODEL), 1.0),
        "mem": nrm((BATCH, MEM_LEN, D_MODEL), 1.0),
        "mix_norm_g": gain((L, D_MODEL)),
        "w_in": nrm((L, D_MODEL, P_IN), D_MODEL ** -0.5),
        "pool_w": nrm((L, POOL_GROUPS, POOL_GDIM, POOL_GDIM), POOL_GDIM ** -0.5),
        "pool_scale": gain((L, POOL_WIDTH)),
        "rwkv_mu": jax.random.uniform(next(ks), (L, RWKV_COLS), F32),
        "rwkv_w0": jax.random.uniform(next(ks), (L, RWKV_WIDTH), F32, -5.0, -1.0),
        "rwkv_w2": nrm((L, D_DECAY_LORA, RWKV_WIDTH), 0.5 * D_DECAY_LORA ** -0.5),
        "rwkv_a0": nrm((L, RWKV_WIDTH), 0.1),
        "rwkv_a2": nrm((L, D_AAA_LORA, RWKV_WIDTH), 0.5 * D_AAA_LORA ** -0.5),
        "rwkv_g2": nrm((L, D_GATE_LORA, RWKV_WIDTH), D_GATE_LORA ** -0.5),
        "rwkv_k_k": 0.85 + nrm((L, RWKV_WIDTH), 0.05),
        "rwkv_k_a": 1.0 + nrm((L, RWKV_WIDTH), 0.05),
        "rwkv_r_k": nrm((L, RWKV_HEADS, RWKV_HEAD), 0.1),
        "rwkv_ln_w": gain((L, RWKV_WIDTH)),
        "rwkv_ln_b": nrm((L, RWKV_WIDTH), 0.02),
        "diff_q_norm": gain((L, 2, DIFF_QK)),
        "diff_k_norm": gain((L, 2, DIFF_QK)),
        "diff_lq1": nrm((L, DIFF_QK), 0.1),
        "diff_lk1": nrm((L, DIFF_QK), 0.1),
        "diff_lq2": nrm((L, DIFF_QK), 0.1),
        "diff_lk2": nrm((L, DIFF_QK), 0.1),
        "diff_subln": gain((L, DIFF_VDIM)),
        "w_out": nrm((L, D_MODEL, D_MODEL), D_MODEL ** -0.5),
        "xa_norm_g": gain((L, D_MODEL)),
        "mem_norm_g": gain((L, D_MODEL)),
        "xa_wq": nrm((L, D_MODEL, D_MODEL), D_MODEL ** -0.5),
        "xa_wk": nrm((L, D_MODEL, D_MODEL), D_MODEL ** -0.5),
        "xa_wv": nrm((L, D_MODEL, D_MODEL), D_MODEL ** -0.5),
        "xa_wo": nrm((L, D_MODEL, D_MODEL), D_MODEL ** -0.5),
        "xa_q_norm": gain((L, XA_HEAD)),
        "xa_k_norm": gain((L, XA_HEAD)),
        "ffn_norm_g": gain((L, D_MODEL)),
        "ffn_w_up": nrm((L, D_MODEL, 2 * D_FF), D_MODEL ** -0.5),
        "ffn_conv_w": nrm((L, CONV_W, D_FF), CONV_W ** -0.5),
        "ffn_conv_b": nrm((L, D_FF), 0.02),
        "ffn_w_down": nrm((L, D_FF, D_MODEL), D_FF ** -0.5),
    }

def second_block(x, mem, mix_norm_g, w_in, pool_w, pool_scale,
              rwkv_mu, rwkv_w0, rwkv_w2, rwkv_a0, rwkv_a2, rwkv_g2,
              rwkv_k_k, rwkv_k_a, rwkv_r_k, rwkv_ln_w, rwkv_ln_b,
              diff_q_norm, diff_k_norm, diff_lq1, diff_lk1, diff_lq2, diff_lk2, diff_subln,
              w_out, xa_norm_g, mem_norm_g, xa_wq, xa_wk, xa_wv, xa_wo, xa_q_norm, xa_k_norm,
              ffn_norm_g, ffn_w_up, ffn_conv_w, ffn_conv_b, ffn_w_down):
    h = x
    for l in range(DEPTH):
        lambda_init = 0.8 - 0.6 * math.exp(-0.3 * l)
        z = rmsnorm(h, mix_norm_g[l]) @ w_in[l]
        z_pool = z[..., :POOL_WIDTH]
        z_rwkv = z[..., POOL_WIDTH:POOL_WIDTH + RWKV_COLS]
        z_diff = z[..., POOL_WIDTH + RWKV_COLS:]
        y_pool = pool_mixer(z_pool, pool_w[l], pool_scale[l])
        y_rwkv = rwkv7_mixer(z_rwkv, rwkv_mu[l], rwkv_w0[l], rwkv_w2[l], rwkv_a0[l],
                             rwkv_a2[l], rwkv_g2[l], rwkv_k_k[l], rwkv_k_a[l],
                             rwkv_r_k[l], rwkv_ln_w[l], rwkv_ln_b[l])
        y_diff = diff_attention(z_diff, diff_q_norm[l], diff_k_norm[l], diff_lq1[l],
                                diff_lk1[l], diff_lq2[l], diff_lk2[l], diff_subln[l],
                                lambda_init)
        y = jnp.concatenate([y_pool, y_rwkv, y_diff], axis=-1)
        h = h + y @ w_out[l]
        h = h + memory_cross_attention(rmsnorm(h, xa_norm_g[l]), rmsnorm(mem, mem_norm_g[l]),
                                       xa_wq[l], xa_wk[l], xa_wv[l], xa_wo[l],
                                       xa_q_norm[l], xa_k_norm[l])
        h = h + conv_ffn(rmsnorm(h, ffn_norm_g[l]), ffn_w_up[l], ffn_conv_w[l],
                         ffn_conv_b[l], ffn_w_down[l])
    return h


def setup_inputs(seed=0):
    out = dict(first_inputs(seed))
    for name, value in second_inputs(seed + 1).items():
        if name != "x":
            out[name + "_2"] = value
    return out


def reference(
    x, c, w_ada, b_ada, norm_g, w_in, b_forget, w_o_sb, w_o_fox, b_gate, w_out, final_g, mem_2,
    mix_norm_g_2, w_in_2, pool_w_2, pool_scale_2, rwkv_mu_2, rwkv_w0_2, rwkv_w2_2, rwkv_a0_2,
    rwkv_a2_2, rwkv_g2_2, rwkv_k_k_2, rwkv_k_a_2, rwkv_r_k_2, rwkv_ln_w_2, rwkv_ln_b_2,
    diff_q_norm_2, diff_k_norm_2, diff_lq1_2, diff_lk1_2, diff_lq2_2, diff_lk2_2, diff_subln_2,
    w_out_2, xa_norm_g_2, mem_norm_g_2, xa_wq_2, xa_wk_2, xa_wv_2, xa_wo_2, xa_q_norm_2,
    xa_k_norm_2, ffn_norm_g_2, ffn_w_up_2, ffn_conv_w_2, ffn_conv_b_2, ffn_w_down_2,
):
    x = first_block(
        x, c, w_ada, b_ada, norm_g, w_in, b_forget, w_o_sb, w_o_fox, b_gate, w_out, final_g,
    )
    return second_block(
        x, mem_2, mix_norm_g_2, w_in_2, pool_w_2, pool_scale_2, rwkv_mu_2, rwkv_w0_2, rwkv_w2_2,
        rwkv_a0_2, rwkv_a2_2, rwkv_g2_2, rwkv_k_k_2, rwkv_k_a_2, rwkv_r_k_2, rwkv_ln_w_2,
        rwkv_ln_b_2, diff_q_norm_2, diff_k_norm_2, diff_lq1_2, diff_lk1_2, diff_lq2_2,
        diff_lk2_2, diff_subln_2, w_out_2, xa_norm_g_2, mem_norm_g_2, xa_wq_2, xa_wk_2, xa_wv_2,
        xa_wo_2, xa_q_norm_2, xa_k_norm_2, ffn_norm_g_2, ffn_w_up_2, ffn_conv_w_2, ffn_conv_b_2,
        ffn_w_down_2,
    )


_drawn_inputs = setup_inputs


def setup_inputs(seed=0):
    import zlib

    import numpy as np

    out = dict(_drawn_inputs(seed))
    spreads = {}
    factors = {'norm_g': 5.339,
     'b_gate': 8.0,
     'mix_norm_g_2': 2.917,
     'pool_scale_2': 7.451,
     'rwkv_w2_2': 6.956,
     'rwkv_a0_2': 5.845,
     'rwkv_k_k_2': 6.152,
     'rwkv_k_a_2': 4.048,
     'rwkv_ln_w_2': 8.0,
     'rwkv_ln_b_2': 8.0,
     'diff_q_norm_2': 6.779,
     'diff_k_norm_2': 6.87,
     'diff_lk1_2': 4.647,
     'diff_lk2_2': 5.248,
     'diff_subln_2': 5.928,
     'xa_norm_g_2': 8.0,
     'mem_norm_g_2': 8.0,
     'xa_q_norm_2': 8.0,
     'xa_k_norm_2': 8.0,
     'ffn_norm_g_2': 12.575,
     'ffn_conv_b_2': 17.718}
    for name, (base, spread) in spreads.items():
        noise = np.random.default_rng([zlib.crc32(name.encode()), seed]).standard_normal(out[name].shape)
        drawn = base * np.exp(spread * noise) if base else spread * noise
        out[name] = __import__('jax').numpy.asarray(drawn.astype(out[name].dtype))
    for name, factor in factors.items():
        out[name] = (out[name] * factor).astype(out[name].dtype)
    return out
```

```python
from contextlib import ExitStack

import numpy as np

import concourse.bass as bass
from concourse import mybir

F32 = mybir.dt.float32
F32R = mybir.dt.float32r
ACT = mybir.ActivationFunctionType
ALU = mybir.AluOpType

P = 128
T = 512
D = 1024
KD = D // P
NB = T // P
HEAD = 64
HEADS = 8
FFN = 2816
KF = FFN // P
MEM = 256
DIFF_HEADS = 4
XA_HEADS = 4
CHUNK = 64
NCH = T // CHUNK
POOL_WINDOWS = (2, 4, 8, 16)
PAD = 16
EPS = 1e-6
GN_EPS = 64e-5
NEG = -1e30
ARENA = 25000
MIX_AT, DIST_AT = 21536, 0
LAMBDA_INIT = 0.2


RAW = 3
HI = 2
CHUNK_F = KD * 256
ADA = 6
STREAM = 85
DOWN_K = KF // 2
DOWN = 2 * KD

PARAM_COLS = {}
_at = 0
for _n, _c in (("c", 8), ("b_ada", 24), ("norm_g", 8), ("b_gate", 16), ("final_g", 8), ("mix_g", 8),
               ("pool_scale", 2), ("mu", 8), ("w0", 2), ("a0", 2), ("k_k", 2), ("k_a", 2), ("r_k", 2),
               ("ln_w", 2), ("ln_b", 2), ("dq_g", 1), ("dk_g", 1), ("lq", 2), ("lk", 2), ("subln", 1),
               ("xa_g", 8), ("mem_g", 8), ("xq_g", 2), ("xk_g", 2), ("ffn_g", 8), ("conv_w", 66),
               ("conv_b", 22), ("b_forget", 1), ("w_f", 64), ("lora", 256), ("g2", 256), ("pool_w", 256)):
    PARAM_COLS[_n] = (_at, _c)
    _at += _c
NPARAM = _at
NCOLS = PARAM_COLS["w_f"][0]

CONST_COLS = {}
_at = 0
for _n, _c in (("ident", 128), ("ones", 128), ("blk", 128), ("mask_strict", 128), ("mask_incl", 128),
               ("tri_lower", 128), ("tri_upper", 128), ("tri_incl", 128), ("ident64", 64),
               ("head_row", 1024), ("eps", 1), ("gn_eps", 1),
               ("inv_count", 1024), ("lower", 6 * 128), ("upper", 6 * 128), ("restart", 512),
               ("dist", 4 * 512)):
    CONST_COLS[_n] = (_at, _c)
    _at += _c
NCONST = _at
MIX_COL, DIFF_COL = CONST_COLS["inv_count"][0], CONST_COLS["dist"][0]


def shape_constants():
    i = np.arange(P)
    t, s = i[:, None], i[None, :]
    same = (t // CHUNK) == (s // CHUNK)
    out = np.zeros((P, NCONST), np.float32)

    def put(name, value):
        a, n = CONST_COLS[name]
        out[:, a:a + n] = np.asarray(value, np.float32).reshape(P, n)

    put("ident", np.eye(P))
    put("ones", np.ones((P, P)))
    put("blk", same / HEAD)
    put("mask_strict", np.where(s < t, 0.0, NEG))
    put("mask_incl", np.where(s <= t, 0.0, NEG))
    lower = []
    for lv in range(6):
        b = 1 << lv
        lower.append((t // (2 * b) == s // (2 * b)) & (t // b % 2 == 1) & (s // b % 2 == 0))
    put("lower", np.stack(lower, 1))
    put("upper", np.stack([m.T for m in lower], 1))
    put("tri_lower", same & (s < t))
    put("tri_upper", same & (s > t))
    put("tri_incl", same & (s >= t))
    put("ident64", (t % CHUNK) == np.arange(CHUNK)[None, :])
    tok = np.arange(T)
    inv = np.zeros((P, 2, T))
    for g, w in enumerate(POOL_WINDOWS):
        inv[HEAD * (g % 2):HEAD * (g % 2 + 1), g // 2] = 1.0 / np.minimum(tok + 1, w).astype(np.float32)
    put("inv_count", inv)
    put("restart", np.broadcast_to(tok % CHUNK != 0, (P, T)))
    rows = np.zeros((P, HEADS, P))
    for h in range(HEADS):
        rows[h, h] = 1.0
    put("head_row", rows)
    put("eps", np.full((P, 1), EPS))
    put("gn_eps", np.full((P, 1), GN_EPS))
    j = np.arange(T)[None, :] - (T - P)
    dist = -np.abs(t - j).astype(np.float64)
    seen = (j < 0) | (j // CHUNK <= t // CHUNK)
    put("dist", np.stack([np.where(seen, dist * 2.0 ** (-8.0 * (h + 1) / DIFF_HEADS), NEG)
                          for h in range(DIFF_HEADS)], 1))
    return out


def build(nc, x_in, mem_in, params_in, consts_in, ada_in, stream_in, down_in, out):
    with ExitStack() as ctx:

        sems = {}

        def sem(name):
            if name not in sems:
                sems[name] = ctx.enter_context(nc.semaphore(name))
            return sems[name]

        class Ring:

            def __init__(self, name, banks):
                self.banks = banks
                self.filled = sem(f"{name}_filled")
                self.moved = [sem(f"{name}{b}_moved") for b in range(len(banks))]
                self.ids = {}

            def take(self, pe, key):
                n = self.ids[key] = len(self.ids)
                b = n % len(self.banks)
                if n >= len(self.banks):
                    pe.wait_ge(self.moved[b], n // len(self.banks))
                return self.banks[b]

            def full(self, eng, key):
                eng.wait_ge(self.filled, self.ids[key] + 1)
                return self.banks[self.ids[key] % len(self.banks)]

            def bank(self, key):
                return self.banks[self.ids[key] % len(self.banks)]

            def out(self, key):
                return self.moved[self.ids[key] % len(self.banks)]

            def wait_out(self, eng, key):
                n = self.ids[key]
                eng.wait_ge(self.moved[n % len(self.banks)], n // len(self.banks) + 1)

        def view(v, dims):
            if len(dims) == 2:
                return v.rearrange("p (a b) -> p a b", a=dims[0])
            if len(dims) == 3:
                return v.rearrange("p (a b c) -> p a b c", a=dims[0], b=dims[1])
            return v

        def sb(name, *dims, kind=F32):
            n = int(np.prod(dims))
            return view(ctx.enter_context(nc.sbuf_tensor(name, [P, n], kind))[:, :], dims)

        def sb_both(name, *dims):
            with nc.sbuf_tensor(name, [P, int(np.prod(dims))], F32) as plain:
                pass
            return view(plain[:, :], dims), sb(name + "_low", *dims, kind=F32R)

        w_raw, w_lo = sb_both("weights", RAW, CHUNK_F)
        w_hi = sb("weights_high", HI, CHUNK_F, kind=F32R)
        consts = sb("consts", MIX_COL)
        params = sb("params", NPARAM)
        nparams = sb("nparams", NCOLS)
        wf_hi = sb("w_f_high", 64, kind=F32R)
        wf_lo = sb("w_f_low", 64, kind=F32R)
        xres = sb("xres", KD, T)
        h_raw, h_lo = sb_both("h", KD, T)
        h_hi = sb("h_high", KD, T, kind=F32R)
        sq = sb("sq", 2, T)
        acc = sb("acc", T)
        rms = sb("rms", T)
        mod = sb("mod", 24)
        gmod = sb("gmod", 8)
        small = sb("small", 64)
        dq8 = sb("dq8", 2)
        with nc.sbuf_tensor("arena", [P, ARENA], F32) as arena:
            pass

        def at(a, *dims):
            n = int(np.prod(dims))
            assert a + n <= ARENA, (a, n)
            return view(arena[:, a:a + n], dims)

        def at_r(name, a, *dims):
            n = int(np.prod(dims))
            assert a + n <= ARENA, (a, n)
            with ExitStack() as held:
                if a:
                    held.enter_context(nc.sbuf_tensor(name + "_below", [P, a], F32))
                part = held.enter_context(nc.sbuf_tensor(name, [P, n], F32R))
            return view(part[:, :], dims)

        def par(name, j=0, n=1):
            a = PARAM_COLS[name][0] + j
            return params[:, a:a + n]

        def npar(name, j=0):
            a = PARAM_COLS[name][0] + j
            return nparams[:, a:a + 1]

        def con(name, *dims):
            a, n = CONST_COLS[name]
            if a >= DIFF_COL:
                v = at(DIST_AT, n)
            elif a >= MIX_COL:
                v = at(MIX_AT + a - MIX_COL, n)
            else:
                v = consts[:, a:a + n]
            return view(v, dims)

        ident, ones_m, blk = con("ident"), con("ones"), con("blk")

        def ones(n, rows=P):
            return ones_m[0:rows, 0:1].broadcast_to([rows, n])

        ada_w = at(0, ADA, 2, KD * 256).rearrange("p i c (k n) -> p i c k n", k=KD)
        qa, ka, va = at(0, 4, T), at(2048, 4, T), at(4096, 4, T)
        qb, kb, vb = at(6144, 4, T), at(8192, 4, T), at(10240, 4, T)
        gated_raw = at(12288, 8, T)
        gated = {"a": gated_raw[:, 0:4, :], "b": gated_raw[:, 4:8, :]}
        gated_lo, gated_hi = at_r("gated_low", 12288, 8, T), at_r("gated_high", 0, 8, T)
        gates = at(4096, 16, T)
        nF = at(16384, T)
        nF_bc = at(16896, 2, T)
        W1 = 17920
        ebuf, spb, rbuf, wbuf, ptb = at(W1, 3, T), at(W1 + 1536, 2, T), at(W1 + 2560, 2, T), \
            at(W1 + 3584, 3, T), at(W1 + 5120, 3, T)
        negb, expb = at(W1, 3, T), at(W1 + 1536, 3, T)
        tmp1 = negb
        zm = at(0, 8, T)
        POOL_AT = 4096
        pool_u = at(POOL_AT, 2, PAD + T)
        POOL_W = PAD + T
        ycat03 = at(5152, 4, T)
        dqk, dv = at(7200, 8, T), at(11296, 4, T)
        W2 = 13344
        dneg, dexp, dpt = at(W2, 4, T), at(W2 + 2048, 6, T), at(W2 + 5120, 3, T)
        dsq, drinv = at(W2 + 6656, 3, T), at(W2 + 8192, 2, T)
        R0 = 7200
        kvec, avec, decay, rdec, kdec, bdec, adec, rst, bonus, gout = (at(R0 + 512 * i, T) for i in range(10))
        tA, tB = at(R0 + 5120, T), at(R0 + 5632, T)
        vnat, bnat, knat, anat = (at(R0 + 6144 + 512 * i, 4, P) for i in range(4))
        MAT = R0 + 8192
        Am, AmT, Tm, Wm, Om, OmT = ([at(MAT + 1024 * i + 512 * hh, 4, P) for hh in range(2)] for i in range(6))
        AakT, ArbT, ArkT = Am, AmT, Om
        U0 = at(POOL_AT, 2, 4, HEAD)
        Mt, H0 = view(kvec, (NCH, CHUNK)), view(avec, (NCH, CHUNK))
        Qm = view(at(R0 + 6144 + 512 * 3, 512), (2, 4, HEAD))
        X1, St = view(decay, (2, 4, HEAD)), view(decay, (NCH, CHUNK))
        zraw = at(R0, 3, T + 1)
        kx, vx = at(7200, 8, MEM), at(9248, 2, D)
        memx, memn_raw, memn_lo = at(13344, 8, MEM), at(15392, 8, MEM), at_r("memory_low", 15392, 8, MEM)
        memn_hi = at_r("memory_high", 11296, 8, MEM)
        qx = at(17440, 8, T)
        W3 = 21536
        xneg, xexp, xpt = at(W3, 3, MEM), at(W3 + 768, 3, MEM), at(W3 + 1536, 3, MEM)
        xsq, xrinv = at(4096, 4, T), at(6144, 2, T)
        gact_raw, gact_lo, gact_hi = at(0, KF, T), at_r("gact_low", 0, KF, T), \
            at_r("gact_high", KF * T, KF, T)
        conv_in = at(2 * KF * T, 3, T + 2)

        bank = [ctx.enter_context(nc.psum_tensor(f"bank{b}", [P, T], F32))[:, :] for b in range(8)]
        M = Ring("main", bank[0:4])
        TR = Ring("turn", bank[4:6])
        PV = Ring("mix", bank[6:8])

        loaded = [sem(f"weights{s}_loaded") for s in range(RAW)]
        used = [sem(f"weights{s}_used") for s in range(RAW)]
        chunk_end = []

        block = ctx.enter_context(nc.Block())

        def rwkv_pe(pe, j, mm, turn):
            lora, g2 = par("lora", P * j, P), par("g2", P * j, P)
            if j == 1:
                pe.wait_ge(sem("rwkv_out"), 1)
            o = M.take(pe, ("rw", j))
            mm(o, lora[0:64, :], zm[0:64, 6, :], True, True, M.filled)
            o = M.take(pe, ("ra", j))
            mm(o, lora[64:128, :], zm[64:128, 6, :], True, True, M.filled)
            o = M.take(pe, ("rg", j))
            mm(o, g2, zm[:, 7, :], True, True, M.filled)
            pe.wait_ge(sem("kk_squares"), j + 1)
            o = M.take(pe, ("kk", j))
            mm(o, blk, tA, True, True, M.filled)
            pe.wait_ge(sem("rk_ready"), j + 1)
            o = M.take(pe, ("bonus", j))
            mm(o, blk, rst, True, True, M.filled)
            for i, src in enumerate((zm[:, 4 + j, :], kdec, bdec, adec)):
                pe.wait_ge(sem("decayed"), 4 * j + 4)
                o = TR.take(pe, ("nat", j, i))
                for c in range(NB):
                    turn(o[:, P * c:P * (c + 1)], src[:, P * c:P * (c + 1)], TR.filled if c == NB - 1 else None)

            def products(name, lhs, rhs):
                for hh in range(2):
                    lo = HEAD * hh
                    o = M.take(pe, (name, j, hh))
                    for c in range(NB):
                        cols = slice(P * c, P * (c + 1))
                        mm(o[:, cols], lhs[lo:lo + HEAD, cols], rhs[lo:lo + HEAD, cols], True, True,
                           M.filled if c == NB - 1 else None)

            def square(name, hh, lhs, rhs):
                o = M.take(pe, name)
                for c in range(NB):
                    mm(o[:, P * c:P * (c + 1)], lhs[hh][:, c, :], rhs[hh][:, c, :], True, True,
                       M.filled if c == NB - 1 else None)

            products("A", adec, bdec)
            products("AT", bdec, adec)
            for lv in range(1, 6):
                for hh in range(2):
                    pe.wait_ge(sem("corner"), 2 * (2 * (5 * j + lv - 1) + hh) + 2)
                    if lv == 1:
                        pe.wait_ge(sem("inverse"), 4 * j + 2 * hh + 2)
                    else:
                        M.wait_out(pe, ("dT", j, lv - 1, hh))
                        M.wait_out(pe, ("dW", j, lv - 1, hh))
                    if lv < 5:
                        square(("Z", j, lv, hh), hh, OmT, Tm)
                    square(("ZT", j, lv, hh), hh, Om, Wm)
                for hh in range(2):
                    if lv < 5:
                        M.wait_out(pe, ("Z", j, lv, hh))
                        square(("dT", j, lv, hh), hh, Wm, Om)
                    M.wait_out(pe, ("ZT", j, lv, hh))
                    square(("dW", j, lv, hh), hh, Tm, OmT)
            products("Aak", kdec, adec)
            products("Arb", bdec, rdec)
            products("Ark", kdec, rdec)
            for i in range(4):
                TR.wait_out(pe, ("nat", j, i))
            o = M.take(pe, ("X1", j))
            for hh in range(2):
                M.wait_out(pe, ("Aak", j, hh))
                for c in range(NB):
                    mm(o[:, HEAD * (NB * hh + c):HEAD * (NB * hh + c + 1)], AakT[hh][:, c, :],
                       vnat[:, c, HEAD * hh:HEAD * (hh + 1)], True, True, M.filled if hh and c == NB - 1 else None)
            for hh in range(2):
                M.wait_out(pe, ("dW", j, 5, hh))
            o = M.take(pe, ("Q", j))
            for hh in range(2):
                for c in range(NB):
                    mm(o[:, HEAD * (NB * hh + c):HEAD * (NB * hh + c + 1)], Wm[hh][:, c, :],
                       anat[:, c, HEAD * hh:HEAD * (hh + 1)], True, True, M.filled if hh and c == NB - 1 else None)
            M.wait_out(pe, ("X1", j))
            o = M.take(pe, ("U0", j))
            for hh in range(2):
                for c in range(NB):
                    mm(o[:, HEAD * (NB * hh + c):HEAD * (NB * hh + c + 1)], Wm[hh][:, c, :],
                       X1[:, hh, c, :], True, True, M.filled if hh and c == NB - 1 else None)
            M.wait_out(pe, ("Q", j))
            for odd in range(2):
                rows = slice(CHUNK * odd, CHUNK * (odd + 1))
                o = M.take(pe, ("Mt", j, odd))
                for c in range(NB):
                    for hh in range(2):
                        cols = slice(HEAD * hh, HEAD * (hh + 1))
                        mm(o[cols, CHUNK * c:CHUNK * (c + 1)], Qm[rows, hh, c, :], bnat[rows, c, cols],
                           True, True, M.filled if (c == NB - 1 and hh) else None)
            M.wait_out(pe, ("U0", j))
            for odd in range(2):
                rows = slice(CHUNK * odd, CHUNK * (odd + 1))
                o = M.take(pe, ("H0", j, odd))
                for c in range(NB):
                    for hh in range(2):
                        cols = slice(HEAD * hh, HEAD * (hh + 1))
                        out_ = o[cols, CHUNK * c:CHUNK * (c + 1)]
                        mm(out_, bnat[rows, c, cols], U0[rows, hh, c, :], True, False)
                        mm(out_, knat[rows, c, cols], vnat[rows, c, cols], False, True,
                           M.filled if (c == NB - 1 and hh) else None)
            for hh in range(2):
                M.wait_out(pe, ("Arb", j, hh))
                M.wait_out(pe, ("Ark", j, hh))
            o = M.take(pe, ("R", j))
            for hh in range(2):
                rows = slice(HEAD * hh, HEAD * (hh + 1))
                for c in range(NB):
                    mm(o[rows, P * c:P * (c + 1)], Qm[:, hh, c, :], ArbT[hh][:, c, :], True, True,
                       M.filled if hh and c == NB - 1 else None)
            y = PV.take(pe, ("yr", j))
            for hh in range(2):
                rows = slice(HEAD * hh, HEAD * (hh + 1))
                for c in range(NB):
                    mm(y[rows, P * c:P * (c + 1)], U0[:, hh, c, :], ArbT[hh][:, c, :], c == 0, False, skip=True)
                    mm(y[rows, P * c:P * (c + 1)], vnat[:, c, rows], ArkT[hh][:, c, :], False, False, skip=True)
            for odd in range(2):
                M.wait_out(pe, ("Mt", j, odd))
            M.wait_out(pe, ("R", j))
            for c in range(1, NCH):
                if c == 1:
                    pe.wait_ge(sem("state"), j + 1)
                else:
                    TR.wait_out(pe, ("S", j, c - 1))
                if c < NCH - 1:
                    o = TR.take(pe, ("S", j, c))
                    for hh in range(2):
                        rows = slice(HEAD * hh, HEAD * (hh + 1))
                        mm(o[rows, 0:CHUNK], Mt[rows, c, :], St[rows, c, :], True, True, TR.filled if hh else None)
                for hh in range(2):
                    rows = slice(HEAD * hh, HEAD * (hh + 1))
                    mm(y[rows, CHUNK * c:CHUNK * (c + 1)], St[rows, c, :], rst[rows, CHUNK * c:CHUNK * (c + 1)],
                       False, c == NCH - 1, PV.filled if (c == NCH - 1 and hh) else None, skip=True)
            PV.wait_out(pe, ("yr", j))
            o = M.take(pe, ("ymean", j))
            mm(o, blk, tA, True, True, M.filled)
            pe.wait_ge(sem("ysq_ready"), j + 1)
            o = M.take(pe, ("yvar", j))
            mm(o, blk, tB, True, True, M.filled)

        @block.tensor
        def _(pe):
            free_slot = []

            def mm(o, lhsT, rhs, start, stop, signal=None, skip=False):
                ins = nc.tensor.matmul(o, lhsT, rhs, start=start, stop=stop, skip_group_check=skip)
                if signal is not None:
                    ins.then_inc(signal, 1)
                elif free_slot:
                    ins.then_inc(used[free_slot.pop()], 1)

            def turn(o, i, signal=None):
                ins = nc.tensor.transpose(o, i, ident)
                if signal is not None:
                    ins.then_inc(signal, 1)

            def next_chunk(k, cols):
                c = len(chunk_end)
                pe.wait_ge(sem("weights_split"), c + 1)
                chunk_end.append(("used", c % RAW, c // RAW + 1))
                return c % RAW, [v[:, 0:k * cols].rearrange("p (k n) -> p k n", k=k)
                                 for v in (w_hi[:, c % HI, :], w_lo[:, c % RAW, :])]

            def mm3(o, left, right, first, last, signal=None):
                mm(o, left[0], right[0], first, False)
                mm(o, left[0], right[1], False, False)
                mm(o, left[1], right[0], False, last, signal)

            def project(key, tiles, nk, rhs, n, ready=None, cols=256, after=None):
                for m in range(tiles):
                    per = cols // P
                    if m % per == 0:
                        slot, w = next_chunk(nk, cols)
                    o = M.take(pe, (key, m))
                    for k in range(nk):
                        if m == 0 and ready is not None:
                            ready(k)
                        mm3(o[:, 0:n], [p_[:, k, P * (m % per):P * (m % per + 1)] for p_ in w], rhs(k),
                            k == 0, k == nk - 1, M.filled if k == nk - 1 else None)
                    if m % per == per - 1:
                        free_slot.append(slot)
                        chunk_end[-1] = (key, m)
                    if after is not None:
                        after(m)

            def project_rows(key, chunks_n, lhs, blocks, ready=None):
                for c in range(chunks_n):
                    slot, w = next_chunk(KD, 256)
                    for b in range(blocks):
                        o = M.take(pe, (key, c, b))
                        for k in range(KD):
                            if c == 0 and b == 0 and ready is not None:
                                ready(k)
                            mm3(o[:, 0:256], lhs(k, b), [p_[:, k, :] for p_ in w], k == 0, k == KD - 1,
                                M.filled if k == KD - 1 else None)
                    free_slot.append(slot)
                    chunk_end[-1] = (key, c, blocks - 1)

            def norm_sum(n, width):
                pe.wait_ge(sem("squares_added"), KD * (n + 1))
                o = M.take(pe, ("norm", n))
                mm(o[:, 0:width], ones_m, acc[:, 0:width], True, True, M.filled)

            def h_ready(n):
                return lambda k: pe.wait_ge(sem("h_ready"), KD * n + k + 1)

            pe.wait_ge(sem("consts_loaded"), 16)
            pe.wait_ge(sem("params_loaded"), 16)
            norm_sum(0, T)
            pe.wait_ge(sem("lam_products"), 1)
            o = M.take(pe, "lam")
            mm(o[:, 0:2], ones_m, small[:, 0:2], True, True, M.filled)
            o = M.take(pe, "mod")
            for i in range(ADA):
                pe.wait_ge(sem("ada_sums"), i + 1)
                for c in range(2):
                    for mi in range(2):
                        m = 4 * i + 2 * c + mi
                        mm(o[:, m:m + 1], ada_w[:, i, c, 0, P * mi:P * (mi + 1)], ones_m[:, 0:1], True, True,
                           M.filled if m == 23 else None)

            h = lambda k: (h_hi[:, k, :], h_lo[:, k, :])
            hrow = lambda k, b: (h_hi[:, k, P * b:P * (b + 1)], h_lo[:, k, P * b:P * (b + 1)])
            project("qa", 4, KD, h, T, h_ready(0))
            project("ka", 4, KD, h, T)
            project_rows("va", 2, hrow, NB)
            project("za", 4, KD, h, T)
            project("qb", 4, KD, h, T)
            project("kb", 4, KD, h, T)
            project_rows("vb", 2, hrow, NB)
            project("zb", 4, KD, h, T)
            o = M.take(pe, "f")
            pe.wait_ge(sem("wf_split"), 1)
            wf = [v.rearrange("p (k n) -> p k n", k=KD) for v in (wf_hi, wf_lo)]
            for k in range(KD):
                mm3(o[0:HEADS, :], [v[:, k, :] for v in wf], h(k), k == 0, k == KD - 1,
                    M.filled if k == KD - 1 else None)

            def head_rows(hd):
                return HEAD * (hd % 2), HEAD * (hd % 2) + HEAD

            def transposes(key, src, blocks):
                o = TR.take(pe, key)
                for i in range(blocks):
                    turn(o[:, P * i:P * (i + 1)], src[:, P * i:P * (i + 1)], TR.filled if i == blocks - 1 else None)

            def attend(tag, q, kk, v, mask, lag, weights_done, weights):
                N = HEADS * NB
                for c in range(2):
                    for b in range(NB):
                        M.wait_out(pe, ("v" + tag, c, b))
                for i in range(N + lag + 1):
                    if i < N:
                        hd, b = divmod(i, NB)
                        if tag == "b" and b == 0:
                            if hd == 0:
                                pe.wait_ge(sem("nF_ready"), 1)
                            o = M.take(pe, ("nF", hd))
                            mm(o, con("head_row", HEADS, P)[0:HEADS, hd, :], nF[0:HEADS, :], True, True, M.filled)
                        if b == 0 and hd % 2 == 0:
                            M.wait_out(pe, ("q" + tag, hd // 2))
                            M.wait_out(pe, ("k" + tag, hd // 2))
                        lo, hi = head_rows(hd)
                        o = M.take(pe, (tag, i))
                        end = P * (b + 1)
                        mm(o[:, 0:end], q[lo:hi, hd // 2, P * b:end], kk[lo:hi, hd // 2, 0:end], True, False)
                        mm(o[:, P * b:end], ident, mask, False, True, M.filled)
                    n = i - lag
                    if 0 <= n < N:
                        pe.wait_ge(weights_done, n + 1)
                        transposes(("T" + tag, n), weights(n), n % NB + 1)
                    n = i - lag - 1
                    if 0 <= n < N:
                        hd, b = divmod(n, NB)
                        lo, hi = head_rows(hd)
                        TR.wait_out(pe, ("T" + tag, n))
                        if b == 0 and hd % 2 == 0:
                            y = PV.take(pe, ("y" + tag, hd // 2))
                        last = b == NB - 1 and hd % 2 == 1
                        for s in range(b + 1):
                            mm(y[lo:hi, P * b:P * (b + 1)], v[:, s, HEAD * hd:HEAD * (hd + 1)],
                               ptb[:, n % 3, P * s:P * (s + 1)], s == 0, s == b,
                               PV.filled if last and s == b else None)

            attend("a", qa, ka, va, con("mask_strict"), 3, sem("stick_w"), lambda n: wbuf[:, n % 3, :])
            attend("b", qb, kb, vb, con("mask_incl"), 2, sem("fox_w"), lambda n: expb[:, n % 3, :])

            project("g", 16, KD, h, T)
            for tag, first in (("oa", 0), ("ob", 4)):
                project(tag, KD, 4, lambda k: (gated_hi[:, first + k, :], gated_lo[:, first + k, :]), T,
                        lambda k: pe.wait_ge(sem("gated_split"), first + k + 1), cols=512)
            project("wo", KD, KD, h, T, lambda k: pe.wait_ge(sem("merged"), k + 1))
            norm_sum(1, T)
            norm_sum(2, T)

            project("zr", 8, KD, h, T, h_ready(1))
            project("zp", 2, KD, h, T)
            for j in range(2):
                pe.wait_ge(sem("pooled"), j + 1)
                o = M.take(pe, ("pool", j))
                mm(o, par("pool_w", P * j, P), ycat03[:, j, :], True, True, M.filled)
            pe.wait_ge(sem("lora_in"), 2)
            for j in range(2):
                rwkv_pe(pe, j, mm, turn)

            def dq_sum(j):
                if 0 <= j < 8:
                    pe.wait_ge(sem("dsq_ready"), j + 1)
                    o = M.take(pe, ("dn", j))
                    mm(o, blk, dsq[:, j % 3, :], True, True, M.filled)

            project("dq", 8, KD, h, T, after=lambda m: dq_sum(m - 1))
            dq_sum(7)
            project_rows("dv", 2, hrow, NB)
            for c in range(2):
                for b in range(NB):
                    M.wait_out(pe, ("dv", c, b))
            N = DIFF_HEADS * NB
            for i in range(N + 6):
                if i < N:
                    hd, b = divmod(i, NB)
                    end = P * (b + 1)
                    if b == 0:
                        pe.wait_ge(sem("dqk_ready"), 8)
                    for cp in range(2):
                        lo, hi = head_rows(cp)
                        o = M.take(pe, ("d", i, cp))
                        mm(o[:, 0:end], dqk[lo:hi, hd, P * b:end], dqk[lo:hi, 4 + hd, 0:end], True, True, M.filled)
                n = i - 2
                if 0 <= n < N:
                    pe.wait_ge(sem("diff_w"), n + 1)
                    transposes(("Td", n), dexp[:, 2 * (n % 3), :], n % NB + 1)
                n = i - 3
                if 0 <= n < N:
                    hd, b = divmod(n, NB)
                    TR.wait_out(pe, ("Td", n))
                    if b == 0:
                        y = PV.take(pe, ("yd", hd))
                    for s in range(b + 1):
                        mm(y[:, P * b:P * (b + 1)], dv[:, s, P * hd:P * (hd + 1)], dpt[:, n % 3, P * s:P * (s + 1)],
                           s == 0, s == b, PV.filled if (b == NB - 1 and s == b) else None)
                n = i - 5
                if 0 <= n < N and n % NB == NB - 1:
                    hd = n // NB
                    pe.wait_ge(sem("osq_ready"), hd + 1)
                    o = M.take(pe, ("on", hd))
                    mm(o, ones_m, dsq[:, hd % 2, :], True, True, M.filled)
            project("wo2", KD, KD, h, T, lambda k: pe.wait_ge(sem("mixers_split"), k + 1), after=lambda m: norm_sum(3, MEM) if m == 3 else None)

            def head_sum(name, hd, width):
                if 0 <= hd < XA_HEADS:
                    pe.wait_ge(sem(f"x{name}sq_ready"), 2 * hd + 2)
                    o = M.take(pe, (name + "n", hd))
                    for i in range(2):
                        mm(o[:, 0:width], ones_m, xsq[:, (2 * hd + i) % 4, 0:width], i == 0, i == 1,
                           M.filled if i else None)

            def head_sum_after(name, width):
                return lambda m: head_sum(name, m // 2 - 1, width) if m % 2 == 0 else None

            project("kx", KD, KD, lambda k: (memn_hi[:, k, :], memn_lo[:, k, :]), MEM, h_ready(2), after=head_sum_after("k", MEM))
            head_sum("k", XA_HEADS - 1, MEM)
            norm_sum(4, T)
            project_rows("vx", 4, lambda k, b: [v[:, k, P * b:P * (b + 1)] for v in (memn_hi, memn_lo)], 2)
            project("xq", KD, KD, h, T, h_ready(3), after=head_sum_after("q", T))
            head_sum("q", XA_HEADS - 1, T)
            pe.wait_ge(sem("kx_ready"), 8)
            for c in range(4):
                for b in range(2):
                    M.wait_out(pe, ("vx", c, b))
            N = XA_HEADS * NB
            for i in range(N + 3):
                if i < N:
                    hd, b = divmod(i, NB)
                    if b == 0:
                        pe.wait_ge(sem("qx_ready"), 2 * hd + 2)
                    o = M.take(pe, ("x", i))
                    for k in range(2):
                        mm(o[:, 0:MEM], qx[:, 2 * hd + k, P * b:P * (b + 1)], kx[:, 2 * hd + k, :], k == 0, k == 1,
                           M.filled if k else None)
                n = i - 2
                if 0 <= n < N:
                    pe.wait_ge(sem("xa_w"), n + 1)
                    transposes(("Tx", n), xexp[:, n % 3, :], 2)
                n = i - 3
                if 0 <= n < N:
                    hd, b = divmod(n, NB)
                    TR.wait_out(pe, ("Tx", n))
                    o = PV.take(pe, ("yx", n))
                    for j in range(2):
                        for s in range(2):
                            mm(o[:, P * j:P * (j + 1)], vx[:, s, 256 * hd + P * j:256 * hd + P * (j + 1)],
                               xpt[:, n % 3, P * s:P * (s + 1)], s == 0, s == 1, PV.filled if j and s else None)
            project("xo", KD, KD, h, T, lambda k: pe.wait_ge(sem("xa_split"), k + 1))
            norm_sum(5, T)

            for j in range(KF // 2):
                for half in range(2):
                    slot, w = next_chunk(KD, 256)
                    for mi in range(2):
                        o = M.take(pe, ("up", 2 * j + mi, half))
                        for k in range(KD):
                            if j == 0 and half == 0 and mi == 0:
                                h_ready(4)(k)
                            mm3(o, [p_[:, k, P * mi:P * (mi + 1)] for p_ in w], h(k), k == 0, k == KD - 1,
                                M.filled if k == KD - 1 else None)
                    free_slot.append(slot)
                    chunk_end[-1] = ("up", 2 * j + 1, half)
            for m in range(KD):
                o = M.take(pe, ("down", m))
                for part in range(2):
                    slot, w = next_chunk(DOWN_K, P)
                    for k in range(DOWN_K):
                        kf = DOWN_K * part + k
                        if m == 0:
                            pe.wait_ge(sem("gact_split"), kf + 1)
                        mm3(o, [p_[:, k, :] for p_ in w], (gact_hi[:, kf, :], gact_lo[:, kf, :]),
                            kf == 0, kf == KF - 1, M.filled if kf == KF - 1 else None)
                    free_slot.append(slot)
            assert len(chunk_end) == STREAM + DOWN

        @block.scalar
        def _(act):
            links = [0]

            def link(ins):
                links[0] += 1
                ins.then_inc(sem("act_link"), 1)
                act.wait_ge(sem("act_link"), links[0])

            chunks = [0]

            def split_weights():
                c = chunks[0]
                chunks[0] += 1
                if c >= len(chunk_end):
                    return
                act.wait_ge(loaded[c % RAW], 16 * (c // RAW + 1))
                if c >= HI:
                    end = chunk_end[c - HI]
                    if end[0] == "used":
                        act.wait_ge(used[end[1]], end[2])
                    else:
                        M.full(act, end)
                n = CHUNK_F if c < STREAM else DOWN_K * P
                nc.scalar.activation(w_hi[:, c % HI, 0:n], w_raw[:, c % RAW, 0:n], ACT.Copy)\
                    .then_inc(sem("weights_hi"), 1)

            def split_after(m):
                if m % 2 == 1:
                    split_weights()

            def high(hi, raw, done):
                nc.scalar.activation(hi, raw, ACT.Copy).then_inc(done, 1)

            def high_h(n):
                for k in range(KD):
                    act.wait_ge(sem("h_raw"), KD * n + k + 1)
                    high(h_hi[:, k, :], h_raw[:, k, :], sem("h_hi"))

            def squares(n, src, width, ready, after=None):
                for k in range(KD):
                    i = KD * n + k
                    if k and after is not None:
                        after(k - 1)
                    ready(k)
                    if i >= 2:
                        act.wait_ge(sem("squares_added"), i - 1)
                    nc.scalar.activation(sq[:, i % 2, 0:width], src[:, k, 0:width], ACT.Square)\
                        .then_inc(sem("squares"), 1)
                if after is not None:
                    after(KD - 1)

            def inverse_rms(n, width):
                o = M.full(act, ("norm", n))
                nc.scalar.activation(rms[:, 0:width], o[:, 0:width], ACT.Ln, scale=1.0 / D, bias=con("eps"))\
                    .then_inc(M.out(("norm", n)), 1)
                M.wait_out(act, ("norm", n))
                nc.scalar.activation(rms[:, 0:width], rms[:, 0:width], ACT.Exp, scale=-0.5).then_inc(sem("rms_ready"), 1)

            def move(key, dst, src=None, ring_=M, scale=None):
                o = ring_.full(act, key)
                s_ = o if src is None else src(o)
                if scale is None:
                    nc.scalar.activation(dst, s_, ACT.Copy).then_inc(ring_.out(key), 1)
                elif isinstance(scale, float):
                    nc.scalar.activation(dst, s_, ACT.Copy, scale=scale).then_inc(ring_.out(key), 1)
                else:
                    nc.scalar.activation(dst, s_, ACT.Identity, scale=scale).then_inc(ring_.out(key), 1)

            nc.scalar.preload_act_table_set("natural_log_exp_and_others")
            act.wait_ge(sem("x_loaded"), 16)
            squares(0, xres, T, lambda k: None)
            act.wait_ge(sem("consts_loaded"), 16)
            inverse_rms(0, T)
            o = M.full(act, "lam")
            nc.scalar.activation(small[:, 2:4], o[:, 0:2], ACT.Exp).then_inc(M.out("lam"), 1)

            act.wait_ge(sem("negated"), 1)
            high(wf_hi, par("w_f", 0, 64), sem("wf_hi"))
            for _ in range(HI):
                split_weights()
            high_h(0)

            def silu(tag, base):
                for m in range(4):
                    o = M.full(act, ("z" + tag, m))
                    if base + m >= 2:
                        i = base + m - 2
                        M.wait_out(act, ("za" if i < 4 else "zb", i % 4))
                    nc.scalar.activation(tmp1[:, m % 2, :], o, ACT.Exp, scale=-1.0).then_inc(sem("silu_exp"), 1)
                    split_after(m)

            def rows_out(key, dst):
                for c in range(2):
                    for b in range(NB):
                        move((key, c, b), dst[:, b, 256 * c:256 * (c + 1)], lambda o: o[:, 0:256])
                    split_weights()

            for m in range(4):
                move(("qa", m), qa[:, m, :], scale=HEAD ** -0.5)
                split_after(m)
            for _ in range(2):
                split_weights()
            rows_out("va", va)
            silu("a", 0)
            for m in range(4):
                move(("qb", m), qb[:, m, :], scale=HEAD ** -0.5)
                split_after(m)
            for _ in range(2):
                split_weights()
            rows_out("vb", vb)
            silu("b", 4)
            o = M.full(act, "f")
            fx, fa = nF_bc[0:HEADS, 0, :], nF_bc[0:HEADS, 1, :]
            nc.scalar.activation(fx, o[0:HEADS, :], ACT.Identity, scale=-1.0, bias=npar("b_forget")[0:HEADS, :])\
                .then_inc(M.out("f"), 1)
            M.wait_out(act, "f")
            link(nc.scalar.activation(fa, fx, ACT.Abs))
            link(nc.scalar.activation(fa, fa, ACT.Exp, scale=-1.0))
            nc.scalar.activation(fa, fa, ACT.Ln, bias=1.0).then_inc(sem("f_ln"), 1)

            M.wait_out(act, ("zb", 3))
            N = HEADS * NB
            for i in range(N + 1):
                if i < N:
                    end = P * (i % NB + 1)
                    e = ebuf[:, i % 3, 0:end]
                    o = M.full(act, ("a", i))
                    if i >= 3:
                        act.wait_ge(sem("stick_sp"), i - 2)
                    link(nc.scalar.activation(e, o[:, 0:end], ACT.Abs))
                    link(nc.scalar.activation(e, e, ACT.Exp, scale=-1.0))
                    nc.scalar.activation(e, e, ACT.Ln, bias=1.0).then_inc(sem("stick_ln"), 1)
                if i >= 1:
                    n = i - 1
                    end = P * (n % NB + 1)
                    M.wait_out(act, ("a", n))
                    w = wbuf[:, n % 3, 0:end]
                    nc.scalar.activation(w, w, ACT.Exp).then_inc(sem("stick_w"), 1)

            for i in range(N + 3):
                if i < N:
                    hd, b = divmod(i, NB)
                    end = P * (b + 1)
                    if b == 0:
                        if hd >= 2:
                            M.wait_out(act, ("b", NB * (hd - 1) - 1))
                        else:
                            act.wait_ge(sem("nF_ready"), 1)
                        move(("nF", hd), nF_bc[:, hd % 2, :])
                    M.wait_out(act, ("b", i))
                    if i >= 3:
                        TR.full(act, ("Tb", i - 3))
                        act.wait_ge(sem("fox_w"), i - 2)
                    nc.scalar.activation(expb[:, i % 3, 0:end], negb[:, i % 3, 0:end], ACT.Exp, scale=-1.0,
                                         bias=small[:, 8 + i % 3:9 + i % 3],
                                         accum_out=small[:, 11 + i % 3:12 + i % 3]).then_inc(sem("fox_exp"), 1)
                n = i - 2
                if 0 <= n < N:
                    end = P * (n % NB + 1)
                    move(("Tb", n), ptb[:, n % 3, 0:end], lambda o: o[:, 0:end], TR)

            for m in range(8):
                PV.wait_out(act, ("yb" if m >= 4 else "ya", m % 4))
                high(gated_hi[:, m, :], gated_raw[:, m, :], sem("gated_hi"))
            act.dma_start(at(MIX_AT, DIFF_COL - MIX_COL), consts_in[:, MIX_COL:DIFF_COL]).then_inc(sem("mix_loaded"), 16)
            for m in range(16):
                o = M.full(act, ("g", m))
                nc.scalar.activation(gates[:, m, :], o, ACT.Exp, scale=-1.0, bias=npar("b_gate", m))\
                    .then_inc(M.out(("g", m)), 1)
                split_after(m)
            for _ in range(2):
                split_weights()
            for m in range(KD):
                act.wait_ge(sem("merged_raw"), m + 1)
                high(h_hi[:, m, :], h_raw[:, m, :], sem("merged_hi"))
                if m % 4 == 3:
                    split_weights()

            squares(1, xres, T, lambda k: M.wait_out(act, ("wo", k)), split_after)
            inverse_rms(1, T)
            squares(2, xres, T, lambda k: act.wait_ge(sem("x2_ready"), k + 1))
            inverse_rms(2, T)
            high_h(1)

            act.wait_ge(sem("pads_zero"), 1)
            for m in range(8):
                if m >= 3:
                    act.wait_ge(sem("zm"), m - 2)
                move(("zr", m), zraw[:, m % 3, 1:T + 1])
                split_after(m)
            for j in range(2):
                move(("zp", j), pool_u[:, j, PAD:PAD + T])
            split_weights()
            act.wait_ge(sem("zm"), 8)
            nc.scalar.activation(tA[0:64, :], zm[0:64, 6, :], ACT.Exp, scale=2.0).then_inc(sem("lora_exp"), 1)
            nc.scalar.activation(tB, zm[:, 7, :], ACT.Exp, scale=-1.0).then_inc(sem("lora_exp"), 1)
            for j in range(2):
                move(("pool", j), ycat03[:, j, :], scale=par("pool_scale", j))
            for j in range(2):
                for key, dst, bias in (("rw", decay, npar("w0", j)), ("ra", avec, npar("a0", j))):
                    o = M.full(act, (key, j))
                    nc.scalar.activation(dst, o, ACT.Exp, scale=-1.0, bias=bias).then_inc(M.out((key, j)), 1)
                move(("rg", j), gout)
                act.wait_ge(sem("kk0"), j + 1)
                nc.scalar.activation(tA, adec, ACT.Square).then_inc(sem("kk_squares"), 1)
                act.wait_ge(sem("kk_floor"), j + 1)
                nc.scalar.activation(tB, tB, ACT.Sqrt).then_inc(sem("kk_norm"), 1)
                nc.scalar.preload_act_table_set("natural_log_exp_and_others")
                act.wait_ge(sem("L_ready"), 2 * j + 2)
                nc.scalar.activation(rdec, tA, ACT.Exp).then_inc(sem("exps"), 1)
                nc.scalar.activation(kdec, tA, ACT.Exp, scale=-1.0).then_inc(sem("exps"), 1)
                nc.scalar.activation(decay, decay, ACT.Exp).then_inc(sem("exps"), 1)
                nc.scalar.activation(small[:, 24:32], tA[:, CHUNK - 1::CHUNK], ACT.Exp).then_inc(sem("exps"), 1)
                for i, dst in enumerate((vnat, knat, bnat, anat)):
                    move(("nat", j, i), dst, lambda o: o.rearrange("p (a b) -> p a b", a=4), TR)
                for lv in range(1, 5):
                    for hh in range(2):
                        M.full(act, ("ZT", j, lv, hh))
                        move(("Z", j, lv, hh), Om[hh], lambda o: o.rearrange("p (a b) -> p a b", a=4))
                flat = lambda v: v.rearrange("p a b c -> p (a b c)")
                move(("X1", j), flat(X1))
                move(("U0", j), flat(U0))
                move(("yr", j), tA, None, PV)
                M.wait_out(act, ("ymean", j))
                nc.scalar.activation(tB, tA, ACT.Square).then_inc(sem("ysq_ready"), 1)
                o = M.full(act, ("yvar", j))
                nc.scalar.activation(tB, o, ACT.Ln, bias=con("gn_eps")).then_inc(M.out(("yvar", j)), 1)
                M.wait_out(act, ("yvar", j))
                nc.scalar.activation(tB, tB, ACT.Exp, scale=-0.5).then_inc(sem("y_rstd"), 1)

            def dq_inverse(j):
                o = M.full(act, ("dn", j))
                if j >= 2:
                    act.wait_ge(sem("dqk_ready"), j - 1)
                nc.scalar.activation(drinv[:, j % 2, :], o, ACT.Ln, bias=con("eps")).then_inc(M.out(("dn", j)), 1)
                M.wait_out(act, ("dn", j))
                nc.scalar.activation(drinv[:, j % 2, :], drinv[:, j % 2, :], ACT.Exp, scale=-0.5)\
                    .then_inc(sem("drinv"), 1)

            act.wait_ge(sem("rwkv_out"), 2)
            act.dma_start(at(DIST_AT, NCONST - DIFF_COL), consts_in[:, DIFF_COL:]).then_inc(sem("dist_loaded"), 16)
            for j in range(8):
                move(("dq", j), dqk[:, j, :])
                split_after(j)
                M.wait_out(act, ("dq", j))
                if j >= 3:
                    M.full(act, ("dn", j - 3))
                nc.scalar.activation(dsq[:, j % 3, :], dqk[:, j, :], ACT.Square).then_inc(sem("dsq_ready"), 1)
                if j >= 1:
                    dq_inverse(j - 1)
            dq_inverse(7)
            rows_out("dv", dv)
            for m in range(4):
                high(h_hi[:, m, :], ycat03[:, m, :], sem("mixers_hi"))
            N = DIFF_HEADS * NB
            for i in range(N + 6):
                if i < N:
                    end = P * (i % NB + 1)
                    if i >= 3:
                        TR.full(act, ("Td", i - 3))
                    for cp in range(2):
                        M.wait_out(act, ("d", i, cp))
                        c = 2 * (i % 2) + cp
                        nc.scalar.activation(dexp[:, 2 * (i % 3) + cp, 0:end], dneg[:, c, 0:end], ACT.Exp, scale=-1.0,
                                             bias=small[:, 32 + c:33 + c], accum_out=small[:, 36 + c:37 + c])\
                            .then_inc(sem("diff_exp"), 1)
                n = i - 2
                if 0 <= n < N:
                    end = P * (n % NB + 1)
                    move(("Td", n), dpt[:, n % 3, 0:end], lambda o: o[:, 0:end], TR)
                n = i - 4
                if 0 <= n < N and n % NB == NB - 1:
                    hd = n // NB
                    o = PV.full(act, ("yd", hd))
                    nc.scalar.activation(dsq[:, hd % 2, :], o, ACT.Square).then_inc(sem("osq_ready"), 1)
                n = i - 5
                if 0 <= n < N and n % NB == NB - 1:
                    hd = n // NB
                    o = M.full(act, ("on", hd))
                    if hd >= 2:
                        PV.wait_out(act, ("yd", hd - 2))
                    nc.scalar.activation(drinv[:, hd % 2, :], o, ACT.Ln, scale=1.0 / P, bias=con("eps"))\
                        .then_inc(M.out(("on", hd)), 1)
                    M.wait_out(act, ("on", hd))
                    nc.scalar.activation(drinv[:, hd % 2, :], drinv[:, hd % 2, :], ACT.Exp, scale=-0.5)\
                        .then_inc(sem("oinv"), 1)
                    PV.wait_out(act, ("yd", hd))
                    high(h_hi[:, 4 + hd, :], h_raw[:, 4 + hd, :], sem("mixers_hi"))

            act.dma_start(memx, mem_in).then_inc(sem("mem_loaded"), 16)
            act.wait_ge(sem("mem_loaded"), 16)
            squares(3, memx, MEM, lambda k: None)
            inverse_rms(3, MEM)

            def between(k):
                split_after(k)
                if k == 4:
                    for i in range(KD):
                        act.wait_ge(sem("h_raw"), KD * 2 + i + 1)
                        high(memn_hi[:, i, :], memn_raw[:, i, :], sem("h_hi"))

            squares(4, xres, T, lambda k: M.wait_out(act, ("wo2", k)), between)

            def heads_norm(name, dst, width):
                def inverse(hd):
                    if not 0 <= hd < XA_HEADS:
                        return
                    key = (name + "n", hd)
                    o = M.full(act, key)
                    if hd >= 2:
                        act.wait_ge(sem(f"{name}x_ready"), 2 * (hd - 1))
                    r = xrinv[:, hd % 2, 0:width]
                    nc.scalar.activation(r, o[:, 0:width], ACT.Ln, scale=1.0 / 256, bias=con("eps"))\
                        .then_inc(M.out(key), 1)
                    M.wait_out(act, key)
                    nc.scalar.activation(r, r, ACT.Exp, scale=-0.5).then_inc(sem(f"x{name}inv"), 1)

                for m in range(KD):
                    key = ({"k": "kx", "q": "xq"}[name], m)
                    move(key, dst[:, m, 0:width], lambda o: o[:, 0:width])
                    M.wait_out(act, key)
                    if m >= 4:
                        M.full(act, (name + "n", m // 2 - 2))
                    nc.scalar.activation(xsq[:, m % 4, 0:width], dst[:, m, 0:width], ACT.Square)\
                        .then_inc(sem(f"x{name}sq_ready"), 1)
                    split_after(m)
                    if m % 2 == 0:
                        inverse(m // 2 - 1)
                inverse(XA_HEADS - 1)

            heads_norm("k", kx, MEM)
            inverse_rms(4, T)
            for c in range(4):
                for b in range(2):
                    move(("vx", c, b), vx[:, b, 256 * c:256 * (c + 1)], lambda o: o[:, 0:256])
                split_weights()
                for k in (2 * c, 2 * c + 1):
                    act.wait_ge(sem("h_raw"), KD * 3 + k + 1)
                    high(h_hi[:, k, :], h_raw[:, k, :], sem("h_hi"))
            act.wait_ge(sem("kx_ready"), 8)
            heads_norm("q", qx, T)
            N = XA_HEADS * NB
            for i in range(N + 5):
                if i < N:
                    M.wait_out(act, ("x", i))
                    if i >= 3:
                        TR.full(act, ("Tx", i - 3))
                        act.wait_ge(sem("xa_w"), i - 2)
                    nc.scalar.activation(xexp[:, i % 3, :], xneg[:, i % 3, :], ACT.Exp, scale=-1.0,
                                         bias=small[:, 8 + i % 3:9 + i % 3],
                                         accum_out=small[:, 11 + i % 3:12 + i % 3]).then_inc(sem("xa_exp"), 1)
                n = i - 2
                if 0 <= n < N:
                    move(("Tx", n), xpt[:, n % 3, :], lambda o: o[:, 0:MEM], TR)
                n = i - 4
                if 0 <= n < N and n % NB == NB - 1:
                    PV.wait_out(act, ("yx", n))
                    for m in (2 * (n // NB), 2 * (n // NB) + 1):
                        high(h_hi[:, m, :], h_raw[:, m, :], sem("xa_hi"))
            squares(5, xres, T, lambda k: M.wait_out(act, ("xo", k)), split_after)
            inverse_rms(5, T)
            nc.scalar.preload_act_table_set("gelu_and_others")
            high_h(4)

            act.wait_ge(sem("conv_zero"), 1)
            for j in range(KF // 2 + 1):
                if j:
                    split_weights()
                if j < KF // 2:
                    for mi in range(2):
                        m = 2 * j + mi
                        if m >= 3:
                            act.wait_ge(sem("conv"), m - 2)
                        move(("up", m, 0), conv_in[:, m % 3, 2:T + 2])
                    split_weights()
                if j:
                    for m in (2 * j - 2, 2 * j - 1):
                        M.wait_out(act, ("up", m, 1))
                        high(gact_hi[:, m, :], gact_raw[:, m, :], sem("gact_hi"))
                if j < KF // 2:
                    for mi in range(2):
                        m = 2 * j + mi
                        act.wait_ge(sem("conv"), m + 1)
                        nc.scalar.activation(gact_raw[:, m, :], gact_raw[:, m, :], ACT.Gelu).then_inc(sem("gelu"), 1)
            for _ in range(DOWN):
                split_weights()
            assert chunks[0] == STREAM + DOWN + HI

        @block.vector
        def _(dve):
            links = [0]
            tt, ts, stt = nc.vector.tensor_tensor, nc.vector.tensor_scalar, nc.vector.scalar_tensor_tensor

            def link(ins):
                links[0] += 1
                ins.then_inc(sem("dve_link"), 1)
                dve.wait_ge(sem("dve_link"), links[0])

            def add_square(n, k, width):
                i = KD * n + k
                dve.wait_ge(sem("squares"), i + 1)
                s_ = sq[:, i % 2, 0:width]
                if k == 0:
                    if n:
                        M.full(dve, ("norm", n - 1))
                    nc.vector.tensor_copy(acc[:, 0:width], s_).then_inc(sem("squares_added"), 1)
                else:
                    dve.wait_ge(sem("squares_added"), i)
                    tt(acc[:, 0:width], acc[:, 0:width], s_, ALU.add).then_inc(sem("squares_added"), 1)

            def low(lo, raw, hi, done):
                return tt(lo, raw, hi.bitcast(F32), ALU.subtract).then_inc(done, 1)

            def scaled(n, src, dst, g, width, done):
                dve.wait_ge(sem("rms_ready"), n + 1)
                for k in range(KD):
                    stt(dst[:, k, 0:width], src[:, k, 0:width], par(g, k), rms[:, 0:width], ALU.mult, ALU.mult)\
                        .then_inc(done, 1)

            def low_h(n, k, lo, raw, hi):
                dve.wait_ge(sem("h_hi"), KD * n + k + 1)
                low(lo[:, k, :], raw[:, k, :], hi[:, k, :], sem("h_ready"))

            def scaled_h(norm, n, g):
                dve.wait_ge(sem("rms_ready"), norm + 1)
                for k in range(KD + 2):
                    if k < KD:
                        stt(h_raw[:, k, :], xres[:, k, :], par(g, k), rms[:, :], ALU.mult, ALU.mult)\
                            .then_inc(sem("h_raw"), 1)
                    if k >= 2:
                        low_h(n, k - 2, h_lo, h_raw, h_hi)

            dve.wait_ge(sem("params_loaded"), 16)
            ts(nparams[:, :], params[:, 0:NCOLS], -1.0, None, ALU.mult).then_inc(sem("negated"), 1)
            tt(small[:, 0:2], par("lq", 0, 2), par("lk", 0, 2), ALU.mult).then_inc(sem("lam_products"), 1)
            ts(dq8[:, 0:1], par("dq_g"), HEAD ** -0.5, None, ALU.mult)
            link(ts(dq8[:, 1:2], par("subln"), 1.0 - LAMBDA_INIT, None, ALU.mult))
            for k in range(KD):
                add_square(0, k, T)
            for i in range(ADA):
                dve.wait_ge(sem(f"ada{i}_loaded"), 16)
                total = ada_w[:, i, :, 0, :]
                link(ts(total, total, par("c", 0), None, ALU.mult))
                for k in range(1, KD):
                    ins = stt(total, ada_w[:, i, :, k, :], par("c", k), total, ALU.mult, ALU.add)
                    if k < KD - 1:
                        link(ins)
                ins.then_inc(sem("ada_sums"), 1)
            dve.wait_ge(sem("wf_hi"), 1)
            tt(wf_lo, par("w_f", 0, 64), wf_hi.bitcast(F32), ALU.subtract).then_inc(sem("wf_split"), 1)
            M.wait_out(dve, "lam")
            link(tt(small[:, 4:5], small[:, 2:3], small[:, 3:4], ALU.subtract))
            link(ts(small[:, 5:6], small[:, 4:5], LAMBDA_INIT, -1.0, ALU.add, ALU.mult))
            nlam = small[:, 5:6]
            o = M.full(dve, "mod")
            tt(mod[:, :], o[:, 0:24], par("b_ada", 0, 24), ALU.add).then_inc(M.out("mod"), 1)
            M.wait_out(dve, "mod")
            link(stt(gmod[:, :], mod[:, 8:16], 1.0, par("norm_g", 0, 8), ALU.add, ALU.mult))
            dve.wait_ge(sem("rms_ready"), 1)
            for k in range(KD + 3):
                if k < KD:
                    stt(h_raw[:, k, :], xres[:, k, :], gmod[:, k:k + 1], rms[:, :], ALU.mult, ALU.mult)\
                        .then_inc(sem("h_scaled"), 1)
                if 1 <= k <= KD:
                    dve.wait_ge(sem("h_scaled"), k)
                    ts(h_raw[:, k - 1, :], h_raw[:, k - 1, :], mod[:, k - 1:k], None, ALU.add).then_inc(sem("h_raw"), 1)
                if k >= 3:
                    low_h(0, k - 3, h_lo, h_raw, h_hi)

            def move(key, dst, src=None, ring_=M):
                o = ring_.full(dve, key)
                nc.vector.tensor_copy(dst, o if src is None else src(o)).then_inc(ring_.out(key), 1)

            def silu(tag, base):
                for m in range(4):
                    o = M.full(dve, ("z" + tag, m))
                    e = tmp1[:, m % 2, :]
                    dve.wait_ge(sem("silu_exp"), base + m + 1)
                    link(ts(e, e, 1.0, None, ALU.add))
                    link(nc.vector.reciprocal(e, e))
                    tt(gated[tag][:, m, :], o, e, ALU.mult).then_inc(M.out(("z" + tag, m)), 1)

            for m in range(4):
                move(("ka", m), ka[:, m, :])
            silu("a", 0)
            for m in range(4):
                move(("kb", m), kb[:, m, :])
            silu("b", 4)
            fx, fa = nF_bc[0:HEADS, 0, :], nF_bc[0:HEADS, 1, :]
            dve.wait_ge(sem("f_ln"), 1)
            link(stt(fx, fx, 0.0, fa, ALU.max, ALU.add))
            nc.vector.tensor_tensor_scan(nF[0:HEADS, :], ones(T, HEADS), fx, 0.0, ALU.mult, ALU.add)\
                .then_inc(sem("nF_ready"), 1)

            N = HEADS * NB
            for i in range(N + 6):
                if i < N:
                    end = P * (i % NB + 1)
                    o = M.full(dve, ("a", i))
                    sp, r = spb[:, i % 2, 0:end], rbuf[:, i % 2, 0:end]
                    dve.wait_ge(sem("stick_ln"), i + 1)
                    stt(sp, o[:, 0:end], 0.0, ebuf[:, i % 3, 0:end], ALU.max, ALU.add).then_inc(sem("stick_sp"), 1)
                    dve.wait_ge(sem("stick_sp"), i + 1)
                    link(nc.vector.tensor_tensor_scan(r[:, ::-1], ones(end), sp[:, ::-1], 0.0, ALU.mult, ALU.add))
                    if i >= 3:
                        TR.full(dve, ("Ta", i - 3))
                    tt(wbuf[:, i % 3, 0:end], o[:, 0:end], r, ALU.subtract).then_inc(M.out(("a", i)), 1)
                n = i - 3
                if 0 <= n < N:
                    end = P * (n % NB + 1)
                    move(("Ta", n), ptb[:, n % 3, 0:end], lambda o: o[:, 0:end], TR)
                n = i - 5
                if 0 <= n < N and n % 8 == 7:
                    o = PV.full(dve, ("ya", n // 8))
                    g = gated["a"][:, n // 8, :]
                    tt(g, o, g, ALU.mult).then_inc(PV.out(("ya", n // 8)), 1)

            def soft(key, i, slot, width, bias, scale, neg, lowest):
                o = M.full(dve, key)
                nc.vector.tensor_tensor_reduce(neg[:, slot, 0:width], o[:, 0:width], bias, -scale, 3.0e38,
                                               ALU.add, ALU.min, lowest).then_inc(M.out(key), 1)

            for i in range(N + 5):
                if i < N:
                    hd, b = divmod(i, NB)
                    end = P * (b + 1)
                    if b == 0:
                        M.wait_out(dve, ("nF", hd))
                    if i >= 3:
                        dve.wait_ge(sem("fox_exp"), i - 2)
                    soft(("b", i), i, i % 3, end, nF_bc[:, hd % 2, 0:end], 1.0, negb, small[:, 8 + i % 3:9 + i % 3])
                n = i - 1
                if 0 <= n < N:
                    end = P * (n % NB + 1)
                    dve.wait_ge(sem("fox_exp"), n + 1)
                    link(nc.vector.reciprocal(small[:, 14 + n % 3:15 + n % 3], small[:, 11 + n % 3:12 + n % 3]))
                    w = expb[:, n % 3, 0:end]
                    ts(w, w, small[:, 14 + n % 3:15 + n % 3], None, ALU.mult).then_inc(sem("fox_w"), 1)
                n = i - 4
                if 0 <= n < N and n % 8 == 7:
                    o = PV.full(dve, ("yb", n // 8))
                    g = gated["b"][:, n // 8, :]
                    tt(g, o, g, ALU.mult).then_inc(PV.out(("yb", n // 8)), 1)

            for m in range(16):
                M.wait_out(dve, ("g", m))
                link(ts(gates[:, m, :], gates[:, m, :], 1.0, None, ALU.add))
                nc.vector.reciprocal(gates[:, m, :], gates[:, m, :]).then_inc(sem("gates"), 1)
                if m < 8:
                    dve.wait_ge(sem("gated_hi"), m + 1)
                    low(gated_lo[:, m, :], gated_raw[:, m, :], gated_hi[:, m, :], sem("gated_split"))
            dve.wait_ge(sem("gates"), 16)
            for m in range(KD):
                o = M.full(dve, ("oa", m))
                tt(gates[:, m, :], o, gates[:, m, :], ALU.mult).then_inc(M.out(("oa", m)), 1)
            for m in range(KD + 1):
                if m < KD:
                    o = M.full(dve, ("ob", m))
                    tt(gates[:, KD + m, :], o, gates[:, KD + m, :], ALU.mult).then_inc(M.out(("ob", m)), 1)
                    M.wait_out(dve, ("ob", m))
                    M.wait_out(dve, ("oa", m))
                    tt(h_raw[:, m, :], gates[:, m, :], gates[:, KD + m, :], ALU.add).then_inc(sem("merged_raw"), 1)
                if m:
                    dve.wait_ge(sem("merged_hi"), m)
                    low(h_lo[:, m - 1, :], h_raw[:, m - 1, :], h_hi[:, m - 1, :], sem("merged"))

            def residual(key, n, extra=None, gate=None):
                for m in range(KD + 1):
                    if m < KD:
                        o = M.full(dve, (key, m))
                        if gate is not None:
                            ins = stt(xres[:, m, :], o, gate(m), xres[:, m, :], ALU.mult, ALU.add)
                        else:
                            ins = tt(xres[:, m, :], o, xres[:, m, :], ALU.add)
                        ins.then_inc(M.out((key, m)), 1)
                        if extra is not None:
                            extra(m)
                    if m >= 1 and n is not None:
                        add_square(n, m - 1, T)

            residual("wo", 1, gate=lambda m: mod[:, 16 + m:17 + m])
            scaled(1, xres, xres, "final_g", T, sem("x2_ready"))
            for k in range(KD):
                add_square(2, k, T)
            dve.wait_ge(sem("x2_ready"), KD)
            scaled_h(2, 1, "mix_g")

            for m in range(8):
                M.wait_out(dve, ("zr", m))
                z = zraw[:, m % 3, :]
                if m:
                    dve.wait_ge(sem("zm"), m)
                link(tt(tA, z[:, 0:T], z[:, 1:T + 1], ALU.subtract))
                stt(zm[:, m, :], tA, par("mu", m), z[:, 1:T + 1], ALU.mult, ALU.add).then_inc(sem("zm"), 1)
            win = [at(MAT, POOL_W), at(MAT + 1024, POOL_W)]
            inv_count = con("inv_count", 2, T)
            dve.wait_ge(sem("mix_loaded"), 16)
            for j in range(2):
                M.wait_out(dve, ("zp", j))
                u = pool_u[:, j, :]
                link(tt(win[0][:, 1:], u[:, 1:], u[:, :-1], ALU.add))
                link(tt(win[1][:, 3:], win[0][:, 3:], win[0][:, 1:-2], ALU.add))
                if j == 1:
                    link(tt(win[0][:, 7:], win[1][:, 7:], win[1][:, 3:-4], ALU.add))
                    link(tt(win[1][64:, 15:], win[0][64:, 15:], win[0][64:, 7:-8], ALU.add))
                for half in range(2):
                    rows = slice(64 * half, 64 * half + 64)
                    d = ycat03[rows, j, :]
                    link(tt(d, win[half][rows, PAD:], inv_count[rows, j, :], ALU.mult))
                    ins = tt(d, d, u[rows, PAD:], ALU.subtract)
                ins.then_inc(sem("pooled"), 1)
            dve.wait_ge(sem("lora_exp"), 2)
            link(ts(tA[0:64, :], tA[0:64, :], 1.0, None, ALU.add))
            link(nc.vector.reciprocal(tA[0:64, :], tA[0:64, :]))
            ts(zm[0:64, 6, :], tA[0:64, :], -2.0, 1.0, ALU.mult, ALU.add).then_inc(sem("lora_in"), 1)
            link(ts(tB, tB, 1.0, None, ALU.add))
            nc.vector.reciprocal(zm[:, 7, :], tB).then_inc(sem("lora_in"), 1)

            for j in range(2):
                r_, k_, v_ = zm[:, j, :], zm[:, 2 + j, :], zm[:, 4 + j, :]
                ts(adec, k_, par("k_k", j), None, ALU.mult).then_inc(sem("kk0"), 1)
                M.wait_out(dve, ("rw", j))
                link(ts(decay, decay, 1.0, -float(np.exp(0.5)), ALU.add, ALU.mult))
                link(nc.vector.reciprocal(decay, decay))
                M.wait_out(dve, ("ra", j))
                link(ts(avec, avec, 1.0, None, ALU.add))
                link(nc.vector.reciprocal(avec, avec))
                o = M.full(dve, ("kk", j))
                ts(tB, o, float(HEAD), 1e-24, ALU.mult, ALU.max).then_inc(M.out(("kk", j)), 1)
                M.wait_out(dve, ("kk", j))
                nc.vector.engine_nop().then_inc(sem("kk_floor"), 1)
                link(ts(kvec, avec, 1.0, par("k_a", j), ALU.subtract, ALU.mult))
                link(stt(kvec, kvec, 1.0, k_, ALU.add, ALU.mult))
                stt(rst, r_, par("r_k", j), kvec, ALU.mult, ALU.mult).then_inc(sem("rk_ready"), 1)
                nc.vector.tensor_tensor_scan(tA, con("restart"), decay, 0.0, ALU.mult, ALU.add)\
                    .then_inc(sem("L_ready"), 1)
                dve.wait_ge(sem("L_ready"), 2 * j + 1)
                tt(decay, tA, decay, ALU.subtract).then_inc(sem("L_ready"), 1)
                dve.wait_ge(sem("kk_norm"), j + 1)
                link(nc.vector.reciprocal(tB, tB))
                link(tt(adec, adec, tB, ALU.mult))
                link(tt(bdec, avec, adec, ALU.mult))
                dve.wait_ge(sem("exps"), 4 * j + 4)
                tt(rdec, rdec, r_, ALU.mult).then_inc(sem("decayed"), 1)
                tt(bdec, bdec, kdec, ALU.mult).then_inc(sem("decayed"), 1)
                tt(kdec, kdec, kvec, ALU.mult).then_inc(sem("decayed"), 1)
                stt(adec, adec, -1.0, decay, ALU.mult, ALU.mult).then_inc(sem("decayed"), 1)
                o = M.full(dve, ("bonus", j))
                stt(bonus, o, float(HEAD), v_, ALU.mult, ALU.mult).then_inc(M.out(("bonus", j)), 1)

                def spread(m):
                    return m.unsqueeze(1).broadcast_to([P, NB, P])

                four = lambda o: o.rearrange("p (a b) -> p a b", a=4)

                def masked(name, dst, mask):
                    for hh in range(2):
                        o = M.full(dve, (name, j, hh))
                        tt(dst[hh], four(o), spread(mask), ALU.mult).then_inc(M.out((name, j, hh)), 1)

                masked("A", Am, con("tri_lower"))
                masked("AT", AmT, con("tri_upper"))
                low0, up0 = con("lower", 6, P)[:, 0, :], con("upper", 6, P)[:, 0, :]
                for hh in range(2):
                    M.wait_out(dve, ("AT", j, hh))
                    tt(Tm[hh], Am[hh], spread(low0), ALU.mult)
                    link(tt(Wm[hh], AmT[hh], spread(up0), ALU.mult))
                    tt(Tm[hh], Tm[hh], spread(ident), ALU.add).then_inc(sem("inverse"), 1)
                    tt(Wm[hh], Wm[hh], spread(ident), ALU.add).then_inc(sem("inverse"), 1)
                for lv in range(1, 6):
                    for hh in range(2):
                        move(("ZT", j, lv, hh), OmT[hh], four)
                    for hh in range(2):
                        dw = M.full(dve, ("dW", j, lv, hh))
                        if lv == 1 and hh == 0:
                            dve.wait_ge(sem("inverse"), 4 * j + 4)
                        if lv > 1:
                            M.wait_out(dve, ("dT", j, lv - 1, hh))
                            M.wait_out(dve, ("dW", j, lv - 1, hh))
                        if lv < 5:
                            dt_ = M.full(dve, ("dT", j, lv, hh))
                            tt(Tm[hh], four(dt_), Tm[hh], ALU.add).then_inc(M.out(("dT", j, lv, hh)), 1)
                        tt(Wm[hh], four(dw), Wm[hh], ALU.add).then_inc(M.out(("dW", j, lv, hh)), 1)
                masked("Aak", AakT, con("tri_upper"))
                masked("Arb", ArbT, con("tri_incl"))
                masked("Ark", ArkT, con("tri_incl"))
                move(("Q", j), Qm.rearrange("p a b c -> p (a b c)"))
                half = lambda o: o[:, 0:256].rearrange("p (a b) -> p a b", a=NB)
                for odd in range(2):
                    o = M.full(dve, ("Mt", j, odd))
                    tt(Mt[:, odd::2, :], half(o), con("ident64").unsqueeze(1).broadcast_to([P, NB, CHUNK]), ALU.add)\
                        .then_inc(M.out(("Mt", j, odd)), 1)
                for odd in range(2):
                    o = M.full(dve, ("H0", j, odd))
                    tt(H0[:, odd::2, :], half(o), small[:, 24 + odd:32:2].unsqueeze(2).broadcast_to([P, NB, CHUNK]),
                       ALU.mult).then_inc(M.out(("H0", j, odd)), 1)
                for odd in range(2):
                    M.wait_out(dve, ("H0", j, odd))
                nc.vector.tensor_copy(St[:, 1, :], H0[:, 0, :]).then_inc(sem("state"), 1)
                o = M.full(dve, ("R", j))
                tt(rst, o, rdec, ALU.add).then_inc(M.out(("R", j)), 1)
                for c in range(1, NCH - 1):
                    o = TR.full(dve, ("S", j, c))
                    stt(St[:, c + 1, :], o[:, 0:CHUNK], small[:, 24 + c:25 + c], H0[:, c, :], ALU.mult, ALU.add)\
                        .then_inc(TR.out(("S", j, c)), 1)
                o = M.full(dve, ("ymean", j))
                PV.wait_out(dve, ("yr", j))
                tt(tA, tA, o, ALU.subtract).then_inc(M.out(("ymean", j)), 1)
                dve.wait_ge(sem("y_rstd"), j + 1)
                link(tt(tA, tA, tB, ALU.mult))
                link(ts(tA, tA, par("ln_w", j), par("ln_b", j), ALU.mult, ALU.add))
                link(tt(tA, tA, bonus, ALU.add))
                tt(ycat03[:, 2 + j, :], tA, gout, ALU.mult).then_inc(sem("rwkv_out"), 1)

            dve.wait_ge(sem("dist_loaded"), 16)
            for j in range(8):
                dve.wait_ge(sem("drinv"), j + 1)
                g = dq8[:, 0:1] if j < 4 else par("dk_g")
                stt(dqk[:, j, :], dqk[:, j, :], g, drinv[:, j % 2, :], ALU.mult, ALU.mult).then_inc(sem("dqk_ready"), 1)
            for m in range(4):
                dve.wait_ge(sem("mixers_hi"), m + 1)
                low(h_lo[:, m, :], ycat03[:, m, :], h_hi[:, m, :], sem("mixers_split"))
            dist = con("dist", DIFF_HEADS, T)
            N = DIFF_HEADS * NB
            for i in range(N + 6):
                if i < N:
                    hd, b = divmod(i, NB)
                    end = P * (b + 1)
                    for cp in range(2):
                        if i >= 2:
                            dve.wait_ge(sem("diff_exp"), 2 * (i - 2) + cp + 1)
                        c = 2 * (i % 2) + cp
                        soft(("d", i, cp), i, c, end, dist[:, hd, T - end:T], 1.0, dneg, small[:, 32 + c:33 + c])
                n = i - 1
                if 0 <= n < N:
                    end = P * (n % NB + 1)
                    dve.wait_ge(sem("diff_exp"), 2 * n + 2)
                    c = 2 * (n % 2)
                    e0, e1 = (dexp[:, 2 * (n % 3) + cp, 0:end] for cp in range(2))
                    link(nc.vector.reciprocal(small[:, 40:42], small[:, 36 + c:38 + c]))
                    ts(small[:, 42:43], small[:, 41:42], nlam, None, ALU.mult)
                    link(ts(e0, e0, small[:, 40:41], None, ALU.mult))
                    stt(e0, e1, small[:, 42:43], e0, ALU.mult, ALU.add).then_inc(sem("diff_w"), 1)
                n = i - 5
                if 0 <= n < N and n % NB == NB - 1:
                    hd = n // NB
                    o = PV.full(dve, ("yd", hd))
                    dve.wait_ge(sem("oinv"), hd + 1)
                    stt(h_raw[:, 4 + hd, :], o, dq8[:, 1:2], drinv[:, hd % 2, :], ALU.mult, ALU.mult)\
                        .then_inc(PV.out(("yd", hd)), 1)
                    dve.wait_ge(sem("mixers_hi"), 5 + hd)
                    low(h_lo[:, 4 + hd, :], h_raw[:, 4 + hd, :], h_hi[:, 4 + hd, :], sem("mixers_split"))

            for k in range(KD):
                add_square(3, k, MEM)

            def mem_norm(m):
                if m == 3:
                    scaled(3, memx, memn_raw, "mem_g", MEM, sem("h_raw"))
                if m == 6:
                    for k in range(KD):
                        low_h(2, k, memn_lo, memn_raw, memn_hi)

            residual("wo2", 4, mem_norm)

            def heads_scaled(name, dst, g, width):
                for m in range(KD):
                    dve.wait_ge(sem(f"x{name}inv"), m // 2 + 1)
                    stt(dst[:, m, 0:width], dst[:, m, 0:width], par(g, m % 2), xrinv[:, m // 2 % 2, 0:width],
                        ALU.mult, ALU.mult).then_inc(sem(f"{name}x_ready"), 1)

            heads_scaled("k", kx, "xk_g", MEM)
            scaled_h(4, 3, "xa_g")
            heads_scaled("q", qx, "xq_g", T)
            N = XA_HEADS * NB
            zeros = small[:, 63:64].broadcast_to([P, MEM])
            for i in range(N + 5):
                if i < N:
                    if i >= 3:
                        dve.wait_ge(sem("xa_exp"), i - 2)
                    soft(("x", i), i, i % 3, MEM, zeros, 256 ** -0.5, xneg, small[:, 8 + i % 3:9 + i % 3])
                n = i - 1
                if 0 <= n < N:
                    dve.wait_ge(sem("xa_exp"), n + 1)
                    link(nc.vector.reciprocal(small[:, 14 + n % 3:15 + n % 3], small[:, 11 + n % 3:12 + n % 3]))
                    w = xexp[:, n % 3, :]
                    ts(w, w, small[:, 14 + n % 3:15 + n % 3], None, ALU.mult).then_inc(sem("xa_w"), 1)
                n = i - 3
                if 0 <= n < N:
                    hd, b = divmod(n, NB)
                    move(("yx", n), h_raw[:, 2 * hd:2 * hd + 2, P * b:P * (b + 1)],
                         lambda o: o[:, 0:2 * P].rearrange("p (j n) -> p j n", j=2), PV)
                n = i - 4
                if 0 <= n < N and n % NB == NB - 1:
                    for m in (2 * (n // NB), 2 * (n // NB) + 1):
                        dve.wait_ge(sem("xa_hi"), m + 1)
                        low(h_lo[:, m, :], h_raw[:, m, :], h_hi[:, m, :], sem("xa_split"))
            residual("xo", 5)
            scaled_h(5, 4, "ffn_g")

            for j in range(KF // 2 + 1):
                if j < KF // 2:
                    for mi in range(2):
                        m = 2 * j + mi
                        M.wait_out(dve, ("up", m, 0))
                        a, c = conv_in[:, m % 3, :], gact_raw[:, m, :]
                        link(ts(c, a[:, 0:T], par("conv_w", m), par("conv_b", m), ALU.mult, ALU.add))
                        link(stt(c, a[:, 1:T + 1], par("conv_w", KF + m), c, ALU.mult, ALU.add))
                        stt(c, a[:, 2:T + 2], par("conv_w", 2 * KF + m), c, ALU.mult, ALU.add).then_inc(sem("conv"), 1)
                if j:
                    for m in (2 * j - 2, 2 * j - 1):
                        dve.wait_ge(sem("gact_hi"), m + 1)
                        low(gact_lo[:, m, :], gact_raw[:, m, :], gact_hi[:, m, :], sem("gact_split"))
                if j < KF // 2:
                    for mi in range(2):
                        m = 2 * j + mi
                        dve.wait_ge(sem("gelu"), m + 1)
                        o = M.full(dve, ("up", m, 1))
                        tt(gact_raw[:, m, :], o, gact_raw[:, m, :], ALU.mult).then_inc(M.out(("up", m, 1)), 1)
            residual("down", None)

        @block.gpsimd
        def _(pool):
            def low_weights(first, last):
                for c in range(first, last):
                    n = CHUNK_F if c < STREAM else DOWN_K * P
                    raw, lo = w_raw[:, c % RAW, 0:n], w_lo[:, c % RAW, 0:n]
                    pool.wait_ge(sem("weights_hi"), c + 1)
                    nc.gpsimd.tensor_tensor(lo, raw, w_hi[:, c % HI, 0:n].bitcast(F32), ALU.subtract)\
                        .then_inc(sem("weights_split"), 1)

            nc.gpsimd.memset(small[:, 63:64], 0.0).then_inc(sem("fills"), 1)
            mixers = chunk_end.index(("zr", 1))
            low_weights(0, mixers + HI)
            pool.wait_ge(sem("x2_ready"), 1)
            for s in range(3):
                nc.gpsimd.memset(zraw[:, s, 0:1], 0.0)
            for j in range(2):
                ins = nc.gpsimd.memset(pool_u[:, j, 0:PAD], 0.0)
            ins.then_inc(sem("pads_zero"), 1)
            diff = chunk_end.index(("dq", 1))
            low_weights(mixers + HI, diff + HI)
            pool.wait_ge(sem("mix_loaded"), 16)
            lower, upper = con("lower", 6, P), con("upper", 6, P)
            for j in range(2):
                for lv in range(1, 6):
                    for hh in range(2):
                        if lv == 1:
                            M.wait_out(pool, ("AT", j, hh))
                        else:
                            M.full(pool, ("dW", j, lv - 1, hh))
                        nc.gpsimd.tensor_tensor(Om[hh], Am[hh], lower[:, lv, :].unsqueeze(1).broadcast_to([P, NB, P]),
                                                ALU.mult).then_inc(sem("corner"), 1)
                        nc.gpsimd.tensor_tensor(OmT[hh], AmT[hh], upper[:, lv, :].unsqueeze(1).broadcast_to([P, NB, P]),
                                                ALU.mult).then_inc(sem("corner"), 1)
            up = chunk_end.index(("up", 1, 0))
            low_weights(diff + HI, up + HI)
            pool.wait_ge(sem("h_raw"), 4 * KD + 1)
            for s in range(3):
                ins = nc.gpsimd.memset(conv_in[:, s, 0:2], 0.0)
            ins.then_inc(sem("conv_zero"), 1)
            low_weights(up + HI, STREAM + DOWN)

        @block.sync
        def _(sp):
            sp.dma_start(xres[:, :, :], x_in).then_inc(sem("x_loaded"), 16)
            sp.dma_start(params[:, :], params_in).then_inc(sem("params_loaded"), 16)
            sp.dma_start(consts[:, :], consts_in[:, 0:MIX_COL]).then_inc(sem("consts_loaded"), 16)
            for i in range(ADA):
                sp.dma_start(at(4096 * i, 2, CHUNK_F), ada_in[2 * i:2 * i + 2].rearrange("c p n -> p c n"))\
                    .then_inc(sem(f"ada{i}_loaded"), 16)
            for c in range(RAW):
                sp.dma_start(w_raw[:, c, :], stream_in[c]).then_inc(loaded[c], 16)
            rounds = STREAM // RAW
            with sp.Fori(1, rounds) as i:
                for s in range(RAW):
                    sp.wait_ge(used[s], i)
                    sp.dma_start(w_raw[:, s, :], stream_in[bass.ds(i * RAW + s, 1), :, :].rearrange("a p n -> p (a n)"))\
                        .then_inc(loaded[s], 16)
            for c in range(rounds * RAW, STREAM):
                sp.wait_ge(used[c % RAW], c // RAW)
                sp.dma_start(w_raw[:, c % RAW, :], stream_in[c]).then_inc(loaded[c % RAW], 16)
            width = DOWN_K * P
            rounds = DOWN // RAW
            with sp.Fori(0, rounds) as i:
                for s in range(RAW):
                    slot = (STREAM + s) % RAW
                    sp.wait_ge(used[slot], i + (STREAM + s) // RAW)
                    sp.dma_start(w_raw[:, slot, 0:width],
                                 down_in[bass.ds(i * RAW + s, 1), :, :].rearrange("a p n -> p (a n)"))\
                        .then_inc(loaded[slot], 16)
            for c in range(rounds * RAW, DOWN):
                slot = (STREAM + c) % RAW
                sp.wait_ge(used[slot], (STREAM + c) // RAW)
                sp.dma_start(w_raw[:, slot, 0:width], down_in[c]).then_inc(loaded[slot], 16)
            for m in range(KD):
                M.wait_out(sp, ("down", m))
                sp.dma_start(out[:, m, :], xres[:, m, :]).then_inc(sem("stored"), 16)
            sp.wait_ge(sem("stored"), 16 * KD)


def columns(v, n):
    return np.asarray(v, np.float32).reshape(n, P).T


def lay_params(a):
    out = np.zeros((P, NPARAM), np.float32)

    def put(name, value):
        i, n = PARAM_COLS[name]
        out[0:value.shape[0], i:i + n] = value

    for name, key in (("c", "c"), ("b_ada", "b_ada"), ("norm_g", "norm_g"), ("b_gate", "b_gate"),
                      ("final_g", "final_g"), ("mix_g", "mix_norm_g_2"), ("pool_scale", "pool_scale_2"),
                      ("mu", "rwkv_mu_2"), ("w0", "rwkv_w0_2"), ("a0", "rwkv_a0_2"), ("k_k", "rwkv_k_k_2"),
                      ("k_a", "rwkv_k_a_2"), ("r_k", "rwkv_r_k_2"), ("ln_w", "rwkv_ln_w_2"),
                      ("ln_b", "rwkv_ln_b_2"), ("dq_g", "diff_q_norm_2"), ("dk_g", "diff_k_norm_2"),
                      ("subln", "diff_subln_2"), ("xa_g", "xa_norm_g_2"), ("mem_g", "mem_norm_g_2"),
                      ("xq_g", "xa_q_norm_2"), ("xk_g", "xa_k_norm_2"), ("ffn_g", "ffn_norm_g_2"),
                      ("conv_w", "ffn_conv_w_2"), ("conv_b", "ffn_conv_b_2")):
        put(name, columns(a[key], PARAM_COLS[name][1]))
    for name, keys in (("lq", ("diff_lq1_2", "diff_lq2_2")), ("lk", ("diff_lk1_2", "diff_lk2_2"))):
        two = np.zeros((HEAD, 2), np.float32)
        for i, key in enumerate(keys):
            two[:, i] = np.asarray(a[key]).reshape(-1)
        put(name, two)
    put("b_forget", np.asarray(a["b_forget"]).reshape(HEADS, 1))
    w_f = np.asarray(a["w_in"])[0][:, 4096:4096 + HEADS]
    put("w_f", w_f.reshape(KD, P, HEADS).transpose(1, 0, 2).reshape(P, -1))
    put("lora", np.concatenate([np.asarray(a["rwkv_w2_2"])[0], np.asarray(a["rwkv_a2_2"])[0]], 0))
    put("g2", np.asarray(a["rwkv_g2_2"])[0])
    w = np.asarray(a["pool_w_2"])[0]
    blocks = np.zeros((P, 2, P), np.float32)
    for g in range(4):
        r = HEAD * (g % 2)
        blocks[r:r + HEAD, g // 2, r:r + HEAD] = w[g]
    put("pool_w", blocks.reshape(P, -1))
    return out


def lay_chunks(w, cols):
    k, n = w.shape
    return w.reshape(k // P, P, n // cols, cols).transpose(2, 1, 0, 3).reshape(n // cols, P, -1)


def lay_stream(a):
    w_in, w_in2, up = (np.asarray(a[k])[0] for k in ("w_in", "w_in_2", "ffn_w_up_2"))
    parts = []
    for i in (0, 1, 2, 3, 4, 5, 6, 7):
        parts.append(lay_chunks(w_in[:, 512 * i:512 * (i + 1)], 256))
    parts.append(lay_chunks(w_in[:, 4096 + HEADS:], 256))
    parts.append(lay_chunks(np.asarray(a["w_o_sb"])[0], 512))
    parts.append(lay_chunks(np.asarray(a["w_o_fox"])[0], 512))
    parts.append(lay_chunks(np.asarray(a["w_out"])[0], 256))
    parts.append(lay_chunks(w_in2[:, 256:1280], 256))
    parts.append(lay_chunks(w_in2[:, 0:256], 256))
    parts.append(lay_chunks(w_in2[:, 1280:], 256))
    for key in ("w_out_2", "xa_wk_2", "xa_wv_2", "xa_wq_2", "xa_wo_2"):
        parts.append(lay_chunks(np.asarray(a[key])[0], 256))
    halves = [lay_chunks(up[:, FFN * i:FFN * (i + 1)], 256) for i in range(2)]
    parts.append(np.stack(halves, 1).reshape(2 * halves[0].shape[0], P, -1))
    return np.ascontiguousarray(np.concatenate(parts, 0))


def lay_down(w):
    return np.ascontiguousarray(
        w.reshape(2, DOWN_K, P, KD, P).transpose(3, 0, 2, 1, 4).reshape(DOWN, P, DOWN_K * P))


def kernel(**inputs):
    from concourse import bacc as _bacc
    from concourse.bass_utils import run_bass_kernel_spmd as _run

    a = {k: np.asarray(v) for k, v in inputs.items()}
    rows = lambda v: np.ascontiguousarray(v.T.reshape(KD, P, -1).transpose(1, 0, 2))
    arrays = {
        "x": rows(a["x"][0]),
        "mem": rows(a["mem_2"][0]),
        "params": lay_params(a),
        "consts": shape_constants(),
        "ada": lay_chunks(np.asarray(a["w_ada"])[0], 256),
        "stream": lay_stream(a),
        "down": lay_down(a["ffn_w_down_2"][0]),
    }
    nc = _bacc.Bacc("TRN2", target_bir_lowering=False, num_devices=1)
    ins = [nc.dram_tensor("in_" + n, list(v.shape), F32, kind="ExternalInput").ap() for n, v in arrays.items()]
    out = nc.dram_tensor("out", [P, KD, T], F32, kind="ExternalOutput").ap()
    build(nc, *ins, out)
    r = _run(nc, [{"in_" + n: v for n, v in arrays.items()}], core_ids=[0])
    got = r.results[0]["out"]
    return np.ascontiguousarray(got.transpose(1, 0, 2).reshape(D, T).T)[None]
```

```python
from contextlib import ExitStack

import numpy as np

import concourse.bass as bass
from concourse import mybir

F32 = mybir.dt.float32
F32R = mybir.dt.float32r
BF16 = mybir.dt.bfloat16
ACT = mybir.ActivationFunctionType
ALU = mybir.AluOpType

P = 128
T = 512
D = 1024
KD = D // P
NB = T // P
HEAD = 64
HEADS = 8
FFN = 2816
KF = FFN // P
MEM = 256
DIFF_HEADS = 4
SIDE_G = 11
WBUF = 5
XA_HEADS = 4
CHUNK = 64
NCH = T // CHUNK
POOL_WINDOWS = (2, 4, 8, 16)
PAD = 16
EPS = 1e-6
GN_EPS = 64e-5
NEG = -1e30
ARENA = 24800
MIX_AT, DIST_AT = 21536, 7200
LAMBDA_INIT = 0.2


RAW = 3
HI = 2
CHUNK_F = KD * 256
ADA, ADA_FIRST = 6, 4
STREAM = 85
DOWN_K = KF // 2
DOWN = 2 * KD

PARAM_COLS = {}
_at = 0
for _n, _c in (("c", 8), ("b_ada", 24), ("norm_g", 8), ("b_gate", 16), ("final_g", 8), ("mix_g", 8),
               ("pool_scale", 2), ("mu", 8), ("w0", 2), ("a0", 2), ("k_k", 2), ("k_a", 2), ("r_k", 2),
               ("ln_w", 2), ("ln_b", 2), ("dq_g", 1), ("dk_g", 1), ("lq", 2), ("lk", 2), ("subln", 1),
               ("xa_g", 8), ("mem_g", 8), ("xq_g", 2), ("xk_g", 2), ("ffn_g", 8), ("conv_w", 66),
               ("conv_b", 22), ("b_forget", 1), ("w_f", 64), ("lora", 256), ("g2", 256), ("pool_w", 256)):
    PARAM_COLS[_n] = (_at, _c)
    _at += _c
NPARAM = _at
NCOLS = PARAM_COLS["w_f"][0]

CONST_COLS = {}
_at = 0
for _n, _c in (("ident", 128), ("ones", 128), ("blk", 128), ("mask_strict", 128), ("mask_incl", 128),
               ("tri_lower", 128), ("tri_upper", 128), ("tri_incl", 128), ("ident64", 64),
               ("head_row", 1024), ("eps", 1), ("gn_eps", 1), ("neg_half", 1),
               ("inv_count", 1024), ("lower", 6 * 128), ("upper", 6 * 128), ("restart", 512),
               ("dist", 4 * 512)):
    CONST_COLS[_n] = (_at, _c)
    _at += _c
NCONST = _at
MIX_COL, DIFF_COL = CONST_COLS["inv_count"][0], CONST_COLS["dist"][0]


def shape_constants():
    i = np.arange(P)
    t, s = i[:, None], i[None, :]
    same = (t // CHUNK) == (s // CHUNK)
    out = np.zeros((P, NCONST), np.float32)

    def put(name, value):
        a, n = CONST_COLS[name]
        out[:, a:a + n] = np.asarray(value, np.float32).reshape(P, n)

    put("ident", np.eye(P))
    put("ones", np.ones((P, P)))
    put("blk", same / HEAD)
    put("mask_strict", np.where(s < t, 0.0, NEG))
    put("mask_incl", np.where(s <= t, 0.0, NEG))
    lower = []
    for lv in range(6):
        b = 1 << lv
        lower.append((t // (2 * b) == s // (2 * b)) & (t // b % 2 == 1) & (s // b % 2 == 0))
    put("lower", np.stack(lower, 1))
    put("upper", np.stack([m.T for m in lower], 1))
    put("tri_lower", same & (s < t))
    put("tri_upper", same & (s > t))
    put("tri_incl", same & (s >= t))
    put("ident64", (t % CHUNK) == np.arange(CHUNK)[None, :])
    tok = np.arange(T)
    inv = np.zeros((P, 2, T))
    for g, w in enumerate(POOL_WINDOWS):
        inv[HEAD * (g % 2):HEAD * (g % 2 + 1), g // 2] = 1.0 / np.minimum(tok + 1, w).astype(np.float32)
    put("inv_count", inv)
    put("restart", np.broadcast_to(tok % CHUNK != 0, (P, T)))
    rows = np.zeros((P, HEADS, P))
    for h in range(HEADS):
        rows[h, h] = 1.0
    put("head_row", rows)
    put("eps", np.full((P, 1), EPS))
    put("gn_eps", np.full((P, 1), GN_EPS))
    put("neg_half", np.full((P, 1), -0.5))
    j = np.arange(T)[None, :] - (T - P)
    dist = -np.abs(t - j).astype(np.float64)
    seen = (j < 0) | (j // CHUNK <= t // CHUNK)
    put("dist", np.stack([np.where(seen, dist * 2.0 ** (-8.0 * (h + 1) / DIFF_HEADS), NEG)
                          for h in range(DIFF_HEADS)], 1))
    return out


def build(nc, x_in, mem_in, params_in, consts_in, ada_in, stream_in, down_in, out, x2_kept):
    with ExitStack() as ctx:

        sems = {}

        def sem(name):
            if name not in sems:
                sems[name] = ctx.enter_context(nc.semaphore(name))
            return sems[name]

        class Ring:

            def __init__(self, name, banks):
                self.filled = sem(f"{name}_filled")
                self.ids = {}
                self.use(banks)

            def use(self, banks):
                self.banks = banks
                self.turn = 0

            def take(self, pe, key):
                b = self.banks[self.turn % len(self.banks)]
                self.turn += 1
                if tiles[b]:
                    pe.wait_ge(moved[b], tiles[b])
                tiles[b] += 1
                self.ids[key] = len(self.ids), b, tiles[b]
                return bank[b]

            def full(self, eng, key):
                eng.wait_ge(self.filled, self.ids[key][0] + 1)
                return bank[self.ids[key][1]]

            def out(self, key):
                return moved[self.ids[key][1]]

            def wait_out(self, eng, key):
                eng.wait_ge(moved[self.ids[key][1]], self.ids[key][2])

        def view(v, dims):
            if len(dims) == 2:
                return v.rearrange("p (a b) -> p a b", a=dims[0])
            if len(dims) == 3:
                return v.rearrange("p (a b c) -> p a b c", a=dims[0], b=dims[1])
            return v

        def sb(name, *dims, kind=F32):
            n = int(np.prod(dims))
            return view(ctx.enter_context(nc.sbuf_tensor(name, [P, n], kind))[:, :], dims)

        def sb_both(name, *dims):
            with nc.sbuf_tensor(name, [P, int(np.prod(dims))], F32) as plain:
                pass
            return view(plain[:, :], dims), sb(name + "_low", *dims, kind=F32R)

        w_raw, w_lo = sb_both("weights", RAW, CHUNK_F)
        w_hi = sb("weights_high", HI, CHUNK_F, kind=F32R)
        consts = sb("consts", MIX_COL)
        params = sb("params", NPARAM)
        nparams = sb("nparams", NCOLS)
        wf_hi = sb("w_f_high", 64, kind=F32R)
        wf_lo = sb("w_f_low", 64, kind=F32R)
        xres = sb("xres", KD, T)
        h_raw, h_lo = sb_both("h", KD, T)
        h_hi = sb("h_high", KD, T, kind=F32R)
        sq = sb("sq", 2, T)
        acc = sb("acc", T)
        rms = sb("rms", T)
        mod = sb("mod", 24)
        gmod = sb("gmod", 8)
        gmix = sb("gmix", 8)
        small = sb("small", 64)
        dq8 = sb("dq8", 2)
        masks = sb("masks", 3, P, kind=BF16)
        with nc.sbuf_tensor("arena", [P, ARENA], F32) as arena:
            pass

        def at(a, *dims):
            n = int(np.prod(dims))
            assert a + n <= ARENA, (a, n)
            return view(arena[:, a:a + n], dims)

        def at_r(name, a, *dims):
            n = int(np.prod(dims))
            assert a + n <= ARENA, (a, n)
            with ExitStack() as held:
                if a:
                    held.enter_context(nc.sbuf_tensor(name + "_below", [P, a], F32))
                part = held.enter_context(nc.sbuf_tensor(name, [P, n], F32R))
            return view(part[:, :], dims)

        def par(name, j=0, n=1):
            a = PARAM_COLS[name][0] + j
            return params[:, a:a + n]

        def npar(name, j=0):
            a = PARAM_COLS[name][0] + j
            return nparams[:, a:a + 1]

        def con(name, *dims):
            a, n = CONST_COLS[name]
            if a >= DIFF_COL:
                v = at(DIST_AT, n)
            elif a >= MIX_COL:
                v = at(MIX_AT + a - MIX_COL, n)
            else:
                v = consts[:, a:a + n]
            return view(v, dims)

        ident, ones_m, blk = con("ident"), con("ones"), con("blk")

        def ones(n, rows=P):
            return ones_m[0:rows, 0:1].broadcast_to([rows, n])

        ada_w = at(0, ADA, 2, KD * 256).rearrange("p i c (k n) -> p i c k n", k=KD)
        qa, ka, va = at(0, 4, T), at(2048, 4, T), at(4096, 4, T)
        qb, kb, vb = at(6144, 4, T), at(8192, 4, T), at(10240, 4, T)
        W1 = 17920
        gated_raw = at(12288, 8, T)
        gated = {"a": gated_raw[:, 0:4, :], "b": gated_raw[:, 4:8, :]}
        gated_lo, gated_hi = at_r("gated_low", 12288, 8, T), \
            [v[:, m, :] for v in (at_r("gated_high_a", W1 + 3072, 4, T), at_r("gated_high_b", 6144, 4, T))
             for m in range(4)]
        gates = [at(512 * m if m < 12 else 10240 + 512 * (m - 12), T) for m in range(16)]
        merged_raw, merged_lo = at(16384, 8, T), at_r("merged_low", 16384, 8, T)
        merged_hi = [v[:, m, :] for v in (at_r("merged_high_a", 8192, 4, T), at_r("merged_high_b", W1 + 3072, 4, T))
                     for m in range(4)]
        nF = at(16384, T)
        nF_bc = at(16896, 2, T)
        ebuf, spb, wbuf, ptb = at(W1, 3, T), at(W1 + 1536, 2, T), at(W1 + 2560, WBUF, T), at(W1 + 5120, 3, T)
        z_gate = at(16896, 2, T)
        negb, expb = at(W1, 3, T), at(W1 + 1536, 3, T)
        zm = at(0, 8, T)
        POOL_AT = 4096
        pool_u = at(POOL_AT, 2, PAD + T)
        POOL_W = PAD + T
        ycat03 = at(5152, 4, T)
        dqk = xres
        qk_sq, qk_rinv = sq, [acc, rms]
        zscale, rms2 = sq[:, 0, :], sq[:, 1, :]
        dv = [zm[:, 0, :], zm[:, 2, :], zm[:, 4, :], at(POOL_AT + 512, T)]
        W2 = 13344
        dneg, dexp, dpt = at(W2, 4, T), at(W2 + 2048, 6, T), at(W2 + 5120, 3, T)
        dsq, drinv = at(W2 + 6656, 3, T), at(W2 + 8192, 2, T)
        R0 = 7200
        kvec, avec, decay, rdec, kdec, bdec, adec, rst, bonus, gout = (at(R0 + 512 * i, T) for i in range(10))
        tA, tB = at(R0 + 5120, T), at(R0 + 5632, T)
        vnat, bnat, knat, anat = (at(R0 + 6144 + 512 * i, 4, P) for i in range(4))
        MAT = R0 + 8192
        Am, AmT, Tm, Wm, Om, OmT = ([at(MAT + 1024 * i + 512 * hh, 4, P) for hh in range(2)] for i in range(6))
        AakT, ArbT, ArkT = Am, AmT, Om
        U0 = at(POOL_AT, 2, 4, HEAD)
        Mt, H0 = view(kvec, (NCH, CHUNK)), view(avec, (NCH, CHUNK))
        Qm = view(at(R0 + 6144 + 512 * 3, 512), (2, 4, HEAD))
        X1, St = view(decay, (2, 4, HEAD)), view(decay, (NCH, CHUNK))
        zraw = at(R0, 3, T + 1)
        kx, vx = at(7200, 8, MEM), at(9248, 2, D)
        memx, memn_raw, memn_lo = at(13344, 8, MEM), at(15392, 8, MEM), at_r("memory_low", 15392, 8, MEM)
        memn_hi = at_r("memory_high", 11296, 8, MEM)
        qx = at(17440, 8, T)
        W3 = 21536
        xneg, xexp, xpt = at(W3, 3, MEM), at(W3 + 768, 3, MEM), at(W3 + 1536, 3, MEM)
        xsq, xrinv = at(4096, 4, T), at(6144, 2, T)
        gact_raw, gact_lo, gact_hi = at(0, KF, T), at_r("gact_low", 0, KF, T), \
            at_r("gact_high", KF * T, KF, T)
        conv_in = at(2 * KF * T, 3, T + 2)

        bank = [ctx.enter_context(nc.psum_tensor(f"bank{b}", [P, T], F32))[:, :] for b in range(8)]
        moved = [sem(f"bank{b}_moved") for b in range(8)]
        tiles = [0] * 8
        M = Ring("main", [0, 1, 2, 3])
        F = Ring("side", [3])
        TR = Ring("turn", [4, 5])
        PV = Ring("mix", [6, 7])

        loaded = [sem(f"weights{s}_loaded") for s in range(RAW)]
        used = [sem(f"weights{s}_used") for s in range(RAW)]
        chunk_end = []

        block = ctx.enter_context(nc.Block())

        def rwkv_pe(pe, j, mm, turn, fill, level_done):
            lora, g2 = par("lora", P * j, P), par("g2", P * j, P)
            if j == 1:
                pe.wait_ge(sem("rwkv_out"), 1)
            o = M.take(pe, ("rw", j))
            mm(o, lora[0:64, :], zm[0:64, 6, :], True, True, M.filled)
            o = M.take(pe, ("ra", j))
            mm(o, lora[64:128, :], zm[64:128, 6, :], True, True, M.filled)
            o = M.take(pe, ("rg", j))
            mm(o, g2, zm[:, 7, :], True, True, M.filled)
            fill(0)
            pe.wait_ge(sem("kk_squares"), j + 1)
            o = M.take(pe, ("kk", j))
            mm(o, blk, tA, True, True, M.filled)
            fill(1)
            pe.wait_ge(sem("rk_ready"), j + 1)
            o = M.take(pe, ("bonus", j))
            mm(o, blk, rst, True, True, M.filled)
            fill(2)
            for i, src in enumerate((zm[:, 4 + j, :], kdec, bdec, adec)):
                pe.wait_ge(sem("decayed"), 4 * j + 4)
                o = TR.take(pe, ("nat", j, i))
                for c in range(NB):
                    turn(o[:, P * c:P * (c + 1)], src[:, P * c:P * (c + 1)], TR.filled if c == NB - 1 else None)

            def products(name, lhs, rhs):
                for hh in range(2):
                    lo = HEAD * hh
                    o = M.take(pe, (name, j, hh))
                    for c in range(NB):
                        cols = slice(P * c, P * (c + 1))
                        mm(o[:, cols], lhs[lo:lo + HEAD, cols], rhs[lo:lo + HEAD, cols], True, True,
                           M.filled if c == NB - 1 else None)

            def square(name, hh, lhs, rhs):
                o = M.take(pe, name)
                for c in range(NB):
                    mm(o[:, P * c:P * (c + 1)], lhs[hh][:, c, :], rhs[hh][:, c, :], True, True,
                       M.filled if c == NB - 1 else None)

            products("A", adec, bdec)
            products("AT", bdec, adec)
            for lv in range(1, 6):
                for hh in range(2):
                    pe.wait_ge(sem("corner"), 2 * (2 * (5 * j + lv - 1) + hh) + 2)
                    if lv == 1:
                        pe.wait_ge(sem("inverse"), 4 * j + 2 * hh + 2)
                    else:
                        M.wait_out(pe, ("dT", j, lv - 1, hh))
                        M.wait_out(pe, ("dW", j, lv - 1, hh))
                    if lv < 5:
                        square(("Z", j, lv, hh), hh, OmT, Tm)
                    square(("ZT", j, lv, hh), hh, Om, Wm)
                for hh in range(2):
                    if lv < 5:
                        M.wait_out(pe, ("Z", j, lv, hh))
                        square(("dT", j, lv, hh), hh, Wm, Om)
                    M.wait_out(pe, ("ZT", j, lv, hh))
                    square(("dW", j, lv, hh), hh, Tm, OmT)
                level_done(lv)
            products("Aak", kdec, adec)
            products("Arb", bdec, rdec)
            products("Ark", kdec, rdec)
            for i in range(4):
                TR.wait_out(pe, ("nat", j, i))
            o = M.take(pe, ("X1", j))
            for hh in range(2):
                M.wait_out(pe, ("Aak", j, hh))
                for c in range(NB):
                    mm(o[:, HEAD * (NB * hh + c):HEAD * (NB * hh + c + 1)], AakT[hh][:, c, :],
                       vnat[:, c, HEAD * hh:HEAD * (hh + 1)], True, True, M.filled if hh and c == NB - 1 else None)
            for hh in range(2):
                M.wait_out(pe, ("dW", j, 5, hh))
            o = M.take(pe, ("Q", j))
            for hh in range(2):
                for c in range(NB):
                    mm(o[:, HEAD * (NB * hh + c):HEAD * (NB * hh + c + 1)], Wm[hh][:, c, :],
                       anat[:, c, HEAD * hh:HEAD * (hh + 1)], True, True, M.filled if hh and c == NB - 1 else None)
            M.wait_out(pe, ("X1", j))
            o = M.take(pe, ("U0", j))
            for hh in range(2):
                for c in range(NB):
                    mm(o[:, HEAD * (NB * hh + c):HEAD * (NB * hh + c + 1)], Wm[hh][:, c, :],
                       X1[:, hh, c, :], True, True, M.filled if hh and c == NB - 1 else None)
            M.wait_out(pe, ("Q", j))
            for odd in range(2):
                rows = slice(CHUNK * odd, CHUNK * (odd + 1))
                o = M.take(pe, ("Mt", j, odd))
                for c in range(NB):
                    for hh in range(2):
                        cols = slice(HEAD * hh, HEAD * (hh + 1))
                        mm(o[cols, CHUNK * c:CHUNK * (c + 1)], Qm[rows, hh, c, :], bnat[rows, c, cols],
                           True, True, M.filled if (c == NB - 1 and hh) else None)
            M.wait_out(pe, ("U0", j))
            for odd in range(2):
                rows = slice(CHUNK * odd, CHUNK * (odd + 1))
                o = M.take(pe, ("H0", j, odd))
                for c in range(NB):
                    for hh in range(2):
                        cols = slice(HEAD * hh, HEAD * (hh + 1))
                        out_ = o[cols, CHUNK * c:CHUNK * (c + 1)]
                        mm(out_, bnat[rows, c, cols], U0[rows, hh, c, :], True, False)
                        mm(out_, knat[rows, c, cols], vnat[rows, c, cols], False, True,
                           M.filled if (c == NB - 1 and hh) else None)
            for hh in range(2):
                M.wait_out(pe, ("Arb", j, hh))
                M.wait_out(pe, ("Ark", j, hh))
            o = M.take(pe, ("R", j))
            for hh in range(2):
                rows = slice(HEAD * hh, HEAD * (hh + 1))
                for c in range(NB):
                    mm(o[rows, P * c:P * (c + 1)], Qm[:, hh, c, :], ArbT[hh][:, c, :], True, True,
                       M.filled if hh and c == NB - 1 else None)
            y = PV.take(pe, ("yr", j))
            for hh in range(2):
                rows = slice(HEAD * hh, HEAD * (hh + 1))
                for c in range(NB):
                    mm(y[rows, P * c:P * (c + 1)], U0[:, hh, c, :], ArbT[hh][:, c, :], c == 0, False, skip=True)
                    mm(y[rows, P * c:P * (c + 1)], vnat[:, c, rows], ArkT[hh][:, c, :], False, False, skip=True)
            for odd in range(2):
                M.wait_out(pe, ("Mt", j, odd))
            M.wait_out(pe, ("R", j))
            for c in range(1, NCH):
                if c == 1:
                    pe.wait_ge(sem("state"), j + 1)
                else:
                    TR.wait_out(pe, ("S", j, c - 1))
                if c < NCH - 1:
                    o = TR.take(pe, ("S", j, c))
                    for hh in range(2):
                        rows = slice(HEAD * hh, HEAD * (hh + 1))
                        mm(o[rows, 0:CHUNK], Mt[rows, c, :], St[rows, c, :], True, True, TR.filled if hh else None)
                for hh in range(2):
                    rows = slice(HEAD * hh, HEAD * (hh + 1))
                    mm(y[rows, CHUNK * c:CHUNK * (c + 1)], St[rows, c, :], rst[rows, CHUNK * c:CHUNK * (c + 1)],
                       False, c == NCH - 1, PV.filled if (c == NCH - 1 and hh) else None, skip=True)
            PV.wait_out(pe, ("yr", j))
            o = M.take(pe, ("ymean", j))
            mm(o, blk, tA, True, True, M.filled)
            pe.wait_ge(sem("ysq_ready"), j + 1)
            o = M.take(pe, ("yvar", j))
            mm(o, blk, tB, True, True, M.filled)

        @block.tensor
        def _(pe):
            free_slot = []

            def mm(o, lhsT, rhs, start, stop, signal=None, skip=False):
                ins = nc.tensor.matmul(o, lhsT, rhs, start=start, stop=stop, skip_group_check=skip)
                if signal is not None:
                    ins.then_inc(signal, 1)
                elif free_slot:
                    ins.then_inc(used[free_slot.pop()], 1)

            def turn(o, i, signal=None):
                ins = nc.tensor.transpose(o, i, ident)
                if signal is not None:
                    ins.then_inc(signal, 1)

            def next_chunk(k, cols):
                c = len(chunk_end)
                pe.wait_ge(sem("weights_split"), c + 1)
                chunk_end.append(("used", c % RAW, c // RAW + 1))
                return c % RAW, [v[:, 0:k * cols].rearrange("p (k n) -> p k n", k=k)
                                 for v in (w_hi[:, c % HI, :], w_lo[:, c % RAW, :])]

            def mm3(o, left, right, first, last, signal=None):
                mm(o, left[0], right[0], first, False)
                mm(o, left[0], right[1], False, False)
                mm(o, left[1], right[0], False, last, signal)

            chunk = [None]

            def project(key, tiles, nk, rhs, n, ready=None, cols=256, after=None, first=0):
                for m in range(first, first + tiles):
                    per = cols // P
                    if m % per == 0:
                        chunk[0] = next_chunk(nk, cols)
                    slot, w = chunk[0]
                    o = M.take(pe, (key, m))
                    for k in range(nk):
                        if m == first and ready is not None:
                            ready(k)
                        mm3(o[:, 0:n], [p_[:, k, P * (m % per):P * (m % per + 1)] for p_ in w], rhs(k),
                            k == 0, k == nk - 1, M.filled if k == nk - 1 else None)
                    if m % per == per - 1:
                        free_slot.append(slot)
                        chunk_end[-1] = (key, m)
                    if after is not None:
                        after(m)

            part_bank = [None]

            def project_part(key, m, first, last):
                if first == 0:
                    if m % 2 == 0:
                        chunk[0] = next_chunk(KD, 256)
                    part_bank[0] = F.take(pe, (key, m))
                slot, w = chunk[0]
                for k in range(first, last):
                    mm3(part_bank[0], [p_[:, k, P * (m % 2):P * (m % 2 + 1)] for p_ in w], h(k),
                        k == 0, k == KD - 1, F.filled if k == KD - 1 else None)
                if last == KD and m % 2 == 1:
                    free_slot.append(slot)
                    chunk_end[-1] = (key, m)

            def project_rows(key, first, last, lhs, blocks):
                for i in range(first, last):
                    c, b = divmod(i, blocks)
                    if b == 0:
                        chunk[0] = next_chunk(KD, 256)
                    slot, w = chunk[0]
                    o = M.take(pe, (key, c, b))
                    for k in range(KD):
                        mm3(o[:, 0:256], lhs(k, b), [p_[:, k, :] for p_ in w], k == 0, k == KD - 1,
                            M.filled if k == KD - 1 else None)
                    if b == blocks - 1:
                        free_slot.append(slot)
                        chunk_end[-1] = (key, c, b)

            def norm_sum(n, width, ring=M):
                pe.wait_ge(sem("squares_added"), KD * (n + 1))
                o = ring.take(pe, ("norm", n))
                mm(o[:, 0:width], ones_m, acc[:, 0:width], True, True, ring.filled)

            def h_ready(n):
                return lambda k: pe.wait_ge(sem("h_ready"), KD * n + k + 1)

            pe.wait_ge(sem("consts_loaded"), 16)
            pe.wait_ge(sem("params_loaded"), 16)
            norm_sum(0, T)
            pe.wait_ge(sem("lam_products"), 1)
            o = M.take(pe, "lam")
            mm(o[:, 0:2], ones_m, small[:, 0:2], True, True, M.filled)
            o = M.take(pe, "mod")

            def ada_columns(o, first, last):
                for i in range(first, last):
                    pe.wait_ge(sem("ada_sums"), i + 1)
                    for c in range(2):
                        for mi in range(2):
                            m = 2 * c + mi
                            at_ = 4 * (i - first) + m
                            mm(o[:, at_:at_ + 1], ada_w[:, i, c, 0, P * mi:P * (mi + 1)], ones_m[:, 0:1], True, True,
                               M.filled if i == last - 1 and m == 3 else None)

            ada_columns(o, 0, ADA_FIRST)

            h = lambda k: (h_hi[:, k, :], h_lo[:, k, :])
            hrow = lambda k, b: (h_hi[:, k, P * b:P * (b + 1)], h_lo[:, k, P * b:P * (b + 1)])
            project("qa", 4, KD, h, T, h_ready(0))
            o = M.take(pe, "gate")
            ada_columns(o, ADA_FIRST, ADA)
            project("ka", 4, KD, h, T)
            project_rows("va", 0, 2 * NB, hrow, NB)
            project("za", 4, KD, h, T)
            project("qb", 4, KD, h, T)
            project("kb", 4, KD, h, T)
            o = M.take(pe, "f")
            pe.wait_ge(sem("wf_split"), 1)
            wf = [v.rearrange("p (k n) -> p k n", k=KD) for v in (wf_hi, wf_lo)]
            for k in range(KD):
                mm3(o[0:HEADS, :], [v[:, k, :] for v in wf], h(k), k == 0, k == KD - 1,
                    M.filled if k == KD - 1 else None)

            def head_rows(hd):
                return HEAD * (hd % 2), HEAD * (hd % 2) + HEAD

            def transposes(key, src, blocks):
                o = TR.take(pe, key)
                for i in range(blocks):
                    turn(o[:, P * i:P * (i + 1)], src[:, P * i:P * (i + 1)], TR.filled if i == blocks - 1 else None)

            def attend(tag, q, kk, v, mask, lag, weights_done, weights, fill):
                N = HEADS * NB
                for c in range(2):
                    for b in range(NB):
                        M.wait_out(pe, ("v" + tag, c, b))
                if tag == "a":
                    pe.wait_ge(sem("masks"), 3)
                for i in range(N + lag + 2):
                    if i < N:
                        hd, b = divmod(i, NB)
                        if tag == "b" and b == 0:
                            if hd == 0:
                                pe.wait_ge(sem("nF_ready"), 1)
                            o = M.take(pe, ("nF", hd))
                            mm(o, con("head_row", HEADS, P)[0:HEADS, hd, :], nF[0:HEADS, :], True, True, M.filled)
                        if b == 0 and hd % 2 == 0:
                            M.wait_out(pe, ("q" + tag, hd // 2))
                            M.wait_out(pe, ("k" + tag, hd // 2))
                        lo, hi = head_rows(hd)
                        o = M.take(pe, (tag, i))
                        end = P * (b + 1)
                        mm(o[:, 0:end], q[lo:hi, hd // 2, P * b:end], kk[lo:hi, hd // 2, 0:end], True, False)
                        mm(o[:, P * b:end], masks[:, 0, :], mask, False, True, M.filled)
                    n = i - lag
                    if 0 <= n < N:
                        pe.wait_ge(weights_done, n + 1)
                        transposes(("T" + tag, n), weights(n), n % NB + 1)
                    n = i - lag - 2
                    if 0 <= n < N:
                        hd, b = divmod(n, NB)
                        lo, hi = head_rows(hd)
                        TR.wait_out(pe, ("T" + tag, n))
                        if b == 0 and hd % 2 == 0:
                            y = PV.take(pe, ("y" + tag, hd // 2))
                        last = b == NB - 1 and hd % 2 == 1
                        for s in range(b + 1):
                            mm(y[lo:hi, P * b:P * (b + 1)], v[:, s, HEAD * hd:HEAD * (hd + 1)],
                               ptb[:, n % 3, P * s:P * (s + 1)], s == 0, s == b,
                               PV.filled if last and s == b else None)
                    fill(i)

            PARTS = ((0, 3), (3, 6), (6, KD))

            def fill_a(i):
                if i % 2 == 1 and i < 16:
                    project_rows("vb", i // 2, i // 2 + 1, hrow, NB)
                elif 16 <= i < 32 and i % 4 < 3:
                    project_part("zb", (i - 16) // 4, *PARTS[i % 4])
                elif i >= 32:
                    project_part("g", (i - 32) // 3, *PARTS[(i - 32) % 3])

            def fill_b(i):
                if i % 4 < 3:
                    project_part("g", 2 + i // 4, *PARTS[i % 4])

            M.use([0, 1, 2])
            attend("a", qa, ka, va, masks[:, 1, :], 4, sem("stick_w"), lambda n: wbuf[:, n % WBUF, :], fill_a)
            attend("b", qb, kb, vb, masks[:, 2, :], 2, sem("fox_w"), lambda n: expb[:, n % 3, :], fill_b)

            M.use([0, 1, 2, 3])
            project("g", 16 - SIDE_G, KD, h, T, first=SIDE_G)
            for tag, first in (("oa", 0), ("ob", 4)):
                project(tag, KD, 4, lambda k: (gated_hi[first + k], gated_lo[:, first + k, :]), T,
                        lambda k: pe.wait_ge(sem("gated_split"), first + k + 1), cols=512)
            project("wo", KD, KD, lambda k: (merged_hi[k], merged_lo[:, k, :]), T,
                    lambda k: pe.wait_ge(sem("merged"), k + 1))

            project("zr", 1, KD, h, T, h_ready(1))
            norm_sum(1, T, PV)
            project("zr", 2, KD, h, T, first=1)
            norm_sum(2, T, PV)
            project("zr", 5, KD, h, T, first=3)
            project("zp", 2, KD, h, T)
            pe.wait_ge(sem("zscale"), 1)
            o = PV.take(pe, "zcols")
            for b in range(NB):
                mm(o[:, b:b + 1], zscale[:, P * b:P * (b + 1)], ident[:, 0:1], True, True,
                   PV.filled if b == NB - 1 else None)
            project("dq", 2, KD, h, T)
            for j in range(2):
                pe.wait_ge(sem("pooled"), j + 1)
                o = M.take(pe, ("pool", j))
                mm(o, par("pool_w", P * j, P), ycat03[:, j, :], True, True, M.filled)
            project("dq", 2, KD, h, T, first=2)
            pe.wait_ge(sem("lora_in"), 2)

            def dq_sums(lv):
                for t in range(2 * lv - 2, 2 * lv):
                    if t < 8:
                        pe.wait_ge(sem("qk_squares"), t + 1)
                        o = M.take(pe, ("dn", t))
                        mm(o, blk, qk_sq[:, t % 2, :], True, True, M.filled)

            rwkv_pe(pe, 0, mm, turn, lambda i: project("dq", (1, 2, 1)[i], KD, h, T, first=(4, 5, 7)[i]),
                    lambda lv: None)
            rwkv_pe(pe, 1, mm, turn, lambda i: project_rows("dv", (0, 2, 6)[i], (2, 6, 8)[i], hrow, NB), dq_sums)
            N = DIFF_HEADS * NB
            for i in range(N + 7):
                if i < N:
                    hd, b = divmod(i, NB)
                    end = P * (b + 1)
                    if b == 0:
                        pe.wait_ge(sem("dqk_ready"), 8)
                    for cp in range(2):
                        lo, hi = head_rows(cp)
                        o = M.take(pe, ("d", i, cp))
                        mm(o[:, 0:end], dqk[lo:hi, hd, P * b:end], dqk[lo:hi, 4 + hd, 0:end], True, True, M.filled)
                n = i - 2
                if 0 <= n < N:
                    pe.wait_ge(sem("diff_w"), n + 1)
                    transposes(("Td", n), dexp[:, 2 * (n % 3), :], n % NB + 1)
                n = i - 4
                if 0 <= n < N:
                    hd, b = divmod(n, NB)
                    TR.wait_out(pe, ("Td", n))
                    if b == 0:
                        y = PV.take(pe, ("yd", hd))
                    for s in range(b + 1):
                        mm(y[:, P * b:P * (b + 1)], dv[s][:, P * hd:P * (hd + 1)], dpt[:, n % 3, P * s:P * (s + 1)],
                           s == 0, s == b, PV.filled if (b == NB - 1 and s == b) else None)
                n = i - 6
                if 0 <= n < N and n % NB == NB - 1:
                    hd = n // NB
                    pe.wait_ge(sem("osq_ready"), hd + 1)
                    o = M.take(pe, ("on", hd))
                    mm(o, ones_m, dsq[:, hd % 2, :], True, True, M.filled)
            project("wo2", KD, KD, h, T, lambda k: pe.wait_ge(sem("mixers_split"), k + 1), after=lambda m: norm_sum(3, MEM) if m == 3 else None)

            def head_sum(name, hd, width):
                if 0 <= hd < XA_HEADS:
                    pe.wait_ge(sem(f"x{name}sq_ready"), 2 * hd + 2)
                    o = M.take(pe, (name + "n", hd))
                    for i in range(2):
                        mm(o[:, 0:width], ones_m, xsq[:, (2 * hd + i) % 4, 0:width], i == 0, i == 1,
                           M.filled if i else None)

            def head_sum_after(name, width):
                return lambda m: head_sum(name, m // 2 - 1, width) if m % 2 == 0 else None

            project("kx", KD, KD, lambda k: (memn_hi[:, k, :], memn_lo[:, k, :]), MEM, h_ready(2), after=head_sum_after("k", MEM))
            head_sum("k", XA_HEADS - 1, MEM)
            norm_sum(4, T)
            project_rows("vx", 0, 4 * 2, lambda k, b: [v[:, k, P * b:P * (b + 1)] for v in (memn_hi, memn_lo)], 2)
            project("xq", KD, KD, h, T, h_ready(3), after=head_sum_after("q", T))
            head_sum("q", XA_HEADS - 1, T)
            pe.wait_ge(sem("kx_ready"), 8)
            for c in range(4):
                for b in range(2):
                    M.wait_out(pe, ("vx", c, b))
            N = XA_HEADS * NB
            for i in range(N + 4):
                if i < N:
                    hd, b = divmod(i, NB)
                    if b == 0:
                        pe.wait_ge(sem("qx_ready"), 2 * hd + 2)
                    o = M.take(pe, ("x", i))
                    for k in range(2):
                        mm(o[:, 0:MEM], qx[:, 2 * hd + k, P * b:P * (b + 1)], kx[:, 2 * hd + k, :], k == 0, k == 1,
                           M.filled if k else None)
                n = i - 2
                if 0 <= n < N:
                    pe.wait_ge(sem("xa_w"), n + 1)
                    transposes(("Tx", n), xexp[:, n % 3, :], 2)
                n = i - 4
                if 0 <= n < N:
                    hd, b = divmod(n, NB)
                    TR.wait_out(pe, ("Tx", n))
                    o = PV.take(pe, ("yx", n))
                    for j in range(2):
                        for s in range(2):
                            mm(o[:, P * j:P * (j + 1)], vx[:, s, 256 * hd + P * j:256 * hd + P * (j + 1)],
                               xpt[:, n % 3, P * s:P * (s + 1)], s == 0, s == 1, PV.filled if j and s else None)
            project("xo", KD, KD, h, T, lambda k: pe.wait_ge(sem("xa_split"), k + 1))
            norm_sum(5, T)

            for j in range(KF // 2):
                for half in range(2):
                    slot, w = next_chunk(KD, 256)
                    for mi in range(2):
                        o = M.take(pe, ("up", 2 * j + mi, half))
                        for k in range(KD):
                            if j == 0 and half == 0 and mi == 0:
                                h_ready(4)(k)
                            mm3(o, [p_[:, k, P * mi:P * (mi + 1)] for p_ in w], h(k), k == 0, k == KD - 1,
                                M.filled if k == KD - 1 else None)
                    free_slot.append(slot)
                    chunk_end[-1] = ("up", 2 * j + 1, half)
            for m in range(KD):
                o = M.take(pe, ("down", m))
                for part in range(2):
                    slot, w = next_chunk(DOWN_K, P)
                    for k in range(DOWN_K):
                        kf = DOWN_K * part + k
                        if m == 0:
                            pe.wait_ge(sem("gact_split"), kf + 1)
                        mm3(o, [p_[:, k, :] for p_ in w], (gact_hi[:, kf, :], gact_lo[:, kf, :]),
                            kf == 0, kf == KF - 1, M.filled if kf == KF - 1 else None)
                    free_slot.append(slot)
            assert len(chunk_end) == STREAM + DOWN

        @block.scalar
        def _(act):
            links = [0]

            def link(ins):
                links[0] += 1
                ins.then_inc(sem("act_link"), 1)
                act.wait_ge(sem("act_link"), links[0])

            chunks = [0]

            def full(key):
                return (F if key in F.ids else M).full(act, key)

            def split_weights():
                c = chunks[0]
                chunks[0] += 1
                if c >= len(chunk_end):
                    return
                act.wait_ge(loaded[c % RAW], 16 * (c // RAW + 1))
                if c >= HI:
                    end = chunk_end[c - HI]
                    if end[0] == "used":
                        act.wait_ge(used[end[1]], end[2])
                    else:
                        full(end)
                n = CHUNK_F if c < STREAM else DOWN_K * P
                nc.scalar.activation(w_hi[:, c % HI, 0:n], w_raw[:, c % RAW, 0:n], ACT.Copy)\
                    .then_inc(sem("weights_hi"), 1)

            def split_after(m):
                if m % 2 == 1:
                    split_weights()

            def high(hi, raw, done):
                nc.scalar.activation(hi, raw, ACT.Copy).then_inc(done, 1)

            def high_h(n):
                for k in range(KD):
                    act.wait_ge(sem("h_raw"), KD * n + k + 1)
                    high(h_hi[:, k, :], h_raw[:, k, :], sem("h_hi"))

            def squares(n, src, width, ready, after=None):
                for k in range(KD):
                    i = KD * n + k
                    if k and after is not None:
                        after(k - 1)
                    ready(k)
                    if i >= 2:
                        act.wait_ge(sem("squares_added"), i - 1)
                    nc.scalar.activation(sq[:, i % 2, 0:width], src[:, k, 0:width], ACT.Square)\
                        .then_inc(sem("squares"), 1)
                if after is not None:
                    after(KD - 1)

            def inverse_rms(n, width, ring=M, to=rms):
                o = ring.full(act, ("norm", n))
                nc.scalar.activation(to[:, 0:width], o[:, 0:width], ACT.Ln, scale=1.0 / D, bias=con("eps"))\
                    .then_inc(ring.out(("norm", n)), 1)
                ring.wait_out(act, ("norm", n))
                nc.scalar.activation(to[:, 0:width], to[:, 0:width], ACT.Exp, scale=-0.5).then_inc(sem("rms_ready"), 1)

            def move(key, dst, src=None, ring_=M, scale=None):
                o = ring_.full(act, key)
                s_ = o if src is None else src(o)
                if scale is None:
                    nc.scalar.activation(dst, s_, ACT.Copy).then_inc(ring_.out(key), 1)
                elif isinstance(scale, float):
                    nc.scalar.activation(dst, s_, ACT.Copy, scale=scale).then_inc(ring_.out(key), 1)
                else:
                    nc.scalar.activation(dst, s_, ACT.Identity, scale=scale).then_inc(ring_.out(key), 1)

            nc.scalar.preload_act_table_set("natural_log_exp_and_others")
            act.wait_ge(sem("x_loaded"), 16)
            squares(0, xres, T, lambda k: None)
            act.wait_ge(sem("consts_loaded"), 16)
            inverse_rms(0, T)
            o = M.full(act, "lam")
            nc.scalar.activation(small[:, 2:4], o[:, 0:2], ACT.Exp).then_inc(M.out("lam"), 1)

            act.wait_ge(sem("negated"), 1)
            high(wf_hi, par("w_f", 0, 64), sem("wf_hi"))
            for _ in range(HI):
                split_weights()
            high_h(0)

            def inverse(v, bias=0.0):
                link(nc.scalar.activation(v, v, ACT.Ln, bias=1.0))
                return nc.scalar.activation(v, v, ACT.Exp, scale=-1.0, bias=bias)

            def silu(tag, m):
                ring, e = (F if tag == "b" else M), z_gate[:, m % 2, :]
                if tag == "b" or m >= 2:
                    act.wait_ge(sem("silu"), 4 * (tag == "b") + m - 1)
                move(("z" + tag, m), gated[tag][:, m, :], None, ring)
                ring.wait_out(act, ("z" + tag, m))
                link(nc.scalar.activation(e, gated[tag][:, m, :], ACT.Exp, scale=-1.0))
                inverse(e).then_inc(sem("silu_gate"), 1)
                split_after(m)

            def rows_out(key, dst, first=0, last=2 * NB):
                for i in range(first, last):
                    c, b = divmod(i, NB)
                    move((key, c, b), dst[:, b, 256 * c:256 * (c + 1)], lambda o: o[:, 0:256])
                    if b == NB - 1:
                        split_weights()

            for m in range(4):
                move(("qa", m), qa[:, m, :], scale=HEAD ** -0.5)
                split_after(m)
            for _ in range(2):
                split_weights()
            rows_out("va", va)
            for m in range(4):
                silu("a", m)
            for m in range(4):
                move(("qb", m), qb[:, m, :], scale=HEAD ** -0.5)
                split_after(m)
            for _ in range(2):
                split_weights()
            o = M.full(act, "f")
            fx, fa = nF_bc[0:HEADS, 0, :], nF_bc[0:HEADS, 1, :]
            nc.scalar.activation(fx, o[0:HEADS, :], ACT.Identity, scale=-1.0, bias=npar("b_forget")[0:HEADS, :])\
                .then_inc(M.out("f"), 1)
            M.wait_out(act, "f")
            link(nc.scalar.activation(fa, fx, ACT.Abs))
            link(nc.scalar.activation(fa, fa, ACT.Exp, scale=-1.0))
            nc.scalar.activation(fa, fa, ACT.Ln, bias=1.0).then_inc(sem("f_ln"), 1)

            N = HEADS * NB
            for i in range(N + 2):
                if i % 4 == 3 and 16 < i < N:
                    silu("b", (i - 16) // 4)
                if i < N:
                    end = P * (i % NB + 1)
                    e = ebuf[:, i % 3, 0:end]
                    o = M.full(act, ("a", i))
                    if i >= 3:
                        act.wait_ge(sem("stick_sp"), i - 2)
                    link(nc.scalar.activation(e, o[:, 0:end], ACT.Abs))
                    link(nc.scalar.activation(e, e, ACT.Exp, scale=-1.0))
                    nc.scalar.activation(e, e, ACT.Ln, bias=1.0).then_inc(sem("stick_ln"), 1)
                n = i - 2
                if 0 <= n < N:
                    end = P * (n % NB + 1)
                    M.wait_out(act, ("a", n))
                    w = wbuf[:, n % WBUF, 0:end]
                    nc.scalar.activation(w, w, ACT.Exp).then_inc(sem("stick_w"), 1)
                if i % 2 == 0 and 2 <= i <= 16:
                    rows_out("vb", vb, i // 2 - 1, i // 2)

            def gated_high(m):
                PV.wait_out(act, ("yb" if m >= 4 else "ya", m % 4))
                high(gated_hi[m], gated_raw[:, m, :], sem("gated_hi"))

            def gate_out(m):
                o = full(("g", m))
                nc.scalar.activation(gates[m], o, ACT.Exp, scale=-1.0, bias=npar("b_gate", m))\
                    .then_inc((F if m < SIDE_G else M).out(("g", m)), 1)

            def gate_inverse(m):
                (F if m < SIDE_G else M).wait_out(act, ("g", m))
                inverse(gates[m]).then_inc(sem("gates"), 1)
                split_after(m)

            for i in range(N + 3):
                if i == 0:
                    gate_out(0)
                if i == 1:
                    gate_out(1)
                    gate_inverse(0)
                    gate_inverse(1)
                if i % 4 == 3 and i < N:
                    gate_out(2 + i // 4)
                if i < N:
                    hd, b = divmod(i, NB)
                    end = P * (b + 1)
                    if b == 0:
                        if hd >= 2:
                            M.wait_out(act, ("b", NB * (hd - 1) - 1))
                        else:
                            act.wait_ge(sem("nF_ready"), 1)
                        move(("nF", hd), nF_bc[:, hd % 2, :])
                    M.wait_out(act, ("b", i))
                    if i >= 3:
                        TR.full(act, ("Tb", i - 3))
                        act.wait_ge(sem("fox_w"), i - 2)
                    nc.scalar.activation(expb[:, i % 3, 0:end], negb[:, i % 3, 0:end], ACT.Exp, scale=-1.0,
                                         bias=small[:, 8 + i % 3:9 + i % 3],
                                         accum_out=small[:, 11 + i % 3:12 + i % 3]).then_inc(sem("fox_exp"), 1)
                n = i - 2
                if 0 <= n < N:
                    end = P * (n % NB + 1)
                    move(("Tb", n), ptb[:, n % 3, 0:end], lambda o: o[:, 0:end], TR)
                if i % 4 == 3 and i < N:
                    gate_inverse(2 + i // 4)
                if i % 8 == 5 and i < N:
                    gated_high(i // 8)

            gate_out(SIDE_G - 1)
            gate_inverse(SIDE_G - 1)
            for m in range(4):
                gated_high(4 + m)
            for m in range(SIDE_G, 16):
                gate_out(m)
                gate_inverse(m)
            for _ in range(2):
                split_weights()
            for m in range(KD):
                act.wait_ge(sem("merged_raw"), m + 1)
                high(merged_hi[m], merged_raw[:, m, :], sem("merged_hi"))
                if m % 4 == 3:
                    split_weights()

            def between_blocks(k):
                split_after(k)
                act.wait_ge(sem("h_raw"), KD + k + 1)
                high(h_hi[:, k, :], h_raw[:, k, :], sem("h_hi"))

            squares(1, xres, T, lambda k: M.wait_out(act, ("wo", k)), between_blocks)
            act.dma_start(at(MIX_AT, DIFF_COL - MIX_COL), consts_in[:, MIX_COL:DIFF_COL]).then_inc(sem("mix_loaded"), 16)
            inverse_rms(1, T, PV)
            squares(2, xres, T, lambda k: act.wait_ge(sem("x2_ready"), k + 1))
            act.dma_start(x2_kept, xres).then_inc(sem("x2_stored"), 16)
            split_weights()
            inverse_rms(2, T, PV, rms2)

            for _ in range(4):
                split_weights()
            PV.full(act, "zcols")
            nc.scalar.activation(small[:, 44:48], bank[PV.ids["zcols"][1]][:, 0:NB], ACT.Copy)\
                .then_inc(PV.out("zcols"), 1)
            act.wait_ge(sem("zm"), 8)
            link(nc.scalar.activation(tA[0:64, :], zm[0:64, 6, :], ACT.Exp, scale=2.0))
            inverse(tA[0:64, :]).then_inc(sem("lora_exp"), 1)
            link(nc.scalar.activation(zm[:, 7, :], zm[:, 7, :], ACT.Exp, scale=-1.0))
            inverse(zm[:, 7, :]).then_inc(sem("lora_in"), 1)

            def dq_norm(lv):
                pair = (2 * lv - 2, 2 * lv - 1)
                for t in pair:
                    if t >= 2:
                        M.full(act, ("dn", t - 2))
                    M.wait_out(act, ("dq", t))
                    nc.scalar.activation(qk_sq[:, t % 2, :], dqk[:, t, :], ACT.Square).then_inc(sem("qk_squares"), 1)
                for t in pair:
                    o = M.full(act, ("dn", t))
                    if t >= 2:
                        act.wait_ge(sem("dqk_ready"), t - 1)
                    nc.scalar.activation(qk_rinv[t % 2], o, ACT.Ln, bias=con("eps")).then_inc(M.out(("dn", t)), 1)
                    M.wait_out(act, ("dn", t))
                    nc.scalar.activation(qk_rinv[t % 2], qk_rinv[t % 2], ACT.Exp, scale=-0.5).then_inc(sem("qk_inverse"), 1)

            def dq_out(first, last):
                for t in range(first, last):
                    split_after(t)

            def dv_out(first, last):
                for i in range(first, last):
                    c, b = divmod(i, NB)
                    move(("dv", c, b), dv[b][:, 256 * c:256 * (c + 1)], lambda o: o[:, 0:256], scale=small[:, 44 + b:45 + b])
                    if b == NB - 1:
                        split_weights()

            PV.wait_out(act, "zcols")
            dq_out(0, 2)
            for j in range(2):
                move(("pool", j), ycat03[:, j, :], scale=par("pool_scale", j))
            dq_out(2, 4)
            for j in range(2):
                for key, dst, bias, power in (("rw", decay, npar("w0", j), con("neg_half")),
                                              ("ra", avec, npar("a0", j), 0.0)):
                    o = M.full(act, (key, j))
                    nc.scalar.activation(dst, o, ACT.Exp, scale=-1.0, bias=bias).then_inc(M.out((key, j)), 1)
                    M.wait_out(act, (key, j))
                    inverse(dst, power).then_inc(sem("rates"), 1)
                move(("rg", j), gout)
                act.wait_ge(sem("kk0"), j + 1)
                nc.scalar.activation(tA, adec, ACT.Square).then_inc(sem("kk_squares"), 1)
                if j == 0:
                    dq_out(4, 5)
                else:
                    dv_out(0, 2)
                act.wait_ge(sem("kk_floor"), j + 1)
                link(nc.scalar.activation(tB, tB, ACT.Ln))
                nc.scalar.activation(tB, tB, ACT.Exp, scale=-0.5).then_inc(sem("kk_norm"), 1)
                act.wait_ge(sem("L_ready"), 2 * j + 2)
                nc.scalar.activation(rdec, tA, ACT.Exp).then_inc(sem("exps"), 1)
                nc.scalar.activation(kdec, tA, ACT.Exp, scale=-1.0).then_inc(sem("exps"), 1)
                nc.scalar.activation(decay, decay, ACT.Exp).then_inc(sem("exps"), 1)
                nc.scalar.activation(small[:, 24:32], tA[:, CHUNK - 1::CHUNK], ACT.Exp).then_inc(sem("exps"), 1)
                if j == 0:
                    dq_out(5, 8)
                else:
                    dv_out(2, 8)
                for i, dst in enumerate((vnat, knat, bnat, anat)):
                    move(("nat", j, i), dst, lambda o: o.rearrange("p (a b) -> p a b", a=4), TR)
                for lv in range(1, 5):
                    for hh in range(2):
                        M.full(act, ("ZT", j, lv, hh))
                        move(("Z", j, lv, hh), Om[hh], lambda o: o.rearrange("p (a b) -> p a b", a=4))
                    if j == 1:
                        dq_norm(lv)
                flat = lambda v: v.rearrange("p a b c -> p (a b c)")
                move(("X1", j), flat(X1))
                move(("U0", j), flat(U0))
                move(("yr", j), tA, None, PV)
                M.wait_out(act, ("ymean", j))
                nc.scalar.activation(tB, tA, ACT.Square).then_inc(sem("ysq_ready"), 1)
                o = M.full(act, ("yvar", j))
                nc.scalar.activation(tB, o, ACT.Ln, bias=con("gn_eps")).then_inc(M.out(("yvar", j)), 1)
                M.wait_out(act, ("yvar", j))
                nc.scalar.activation(tB, tB, ACT.Exp, scale=-0.5).then_inc(sem("y_rstd"), 1)

            act.wait_ge(sem("rwkv_out"), 2)
            act.dma_start(at(DIST_AT, NCONST - DIFF_COL), consts_in[:, DIFF_COL:]).then_inc(sem("dist_loaded"), 16)
            for m in range(4):
                high(h_hi[:, m, :], ycat03[:, m, :], sem("mixers_hi"))
            N = DIFF_HEADS * NB
            for i in range(N + 8):
                if i < N:
                    end = P * (i % NB + 1)
                    if i >= 3:
                        TR.full(act, ("Td", i - 3))
                    for cp in range(2):
                        M.wait_out(act, ("d", i, cp))
                        c = 2 * (i % 2) + cp
                        nc.scalar.activation(dexp[:, 2 * (i % 3) + cp, 0:end], dneg[:, c, 0:end], ACT.Exp, scale=-1.0,
                                             bias=small[:, 32 + c:33 + c], accum_out=small[:, 36 + c:37 + c])\
                            .then_inc(sem("diff_exp"), 1)
                if i == N - 1:
                    act.dma_start(xres, x2_kept).then_inc(sem("x2_back"), 16)
                n = i - 2
                if 0 <= n < N:
                    end = P * (n % NB + 1)
                    move(("Td", n), dpt[:, n % 3, 0:end], lambda o: o[:, 0:end], TR)
                n = i - 5
                if 0 <= n < N and n % NB == NB - 1:
                    hd = n // NB
                    o = PV.full(act, ("yd", hd))
                    nc.scalar.activation(dsq[:, hd % 2, :], o, ACT.Square).then_inc(sem("osq_ready"), 1)
                n = i - 6
                if 0 <= n < N and n % NB == NB - 1:
                    hd = n // NB
                    o = M.full(act, ("on", hd))
                    if hd >= 2:
                        PV.wait_out(act, ("yd", hd - 2))
                    nc.scalar.activation(drinv[:, hd % 2, :], o, ACT.Ln, scale=1.0 / P, bias=con("eps"))\
                        .then_inc(M.out(("on", hd)), 1)
                    M.wait_out(act, ("on", hd))
                    nc.scalar.activation(drinv[:, hd % 2, :], drinv[:, hd % 2, :], ACT.Exp, scale=-0.5)\
                        .then_inc(sem("oinv"), 1)
                n = i - 7
                if 0 <= n < N and n % NB == NB - 1:
                    hd = n // NB
                    PV.wait_out(act, ("yd", hd))
                    high(h_hi[:, 4 + hd, :], h_raw[:, 4 + hd, :], sem("mixers_hi"))

            act.dma_start(memx, mem_in).then_inc(sem("mem_loaded"), 16)
            act.wait_ge(sem("mem_loaded"), 16)
            squares(3, memx, MEM, lambda k: None)
            inverse_rms(3, MEM)

            def between(k):
                split_after(k)
                if k == 4:
                    for i in range(KD):
                        act.wait_ge(sem("h_raw"), KD * 2 + i + 1)
                        high(memn_hi[:, i, :], memn_raw[:, i, :], sem("h_hi"))

            squares(4, xres, T, lambda k: M.wait_out(act, ("wo2", k)), between)

            def heads_norm(name, dst, width):
                def inverse(hd):
                    if not 0 <= hd < XA_HEADS:
                        return
                    key = (name + "n", hd)
                    o = M.full(act, key)
                    if hd >= 2:
                        act.wait_ge(sem(f"{name}x_ready"), 2 * (hd - 1))
                    r = xrinv[:, hd % 2, 0:width]
                    nc.scalar.activation(r, o[:, 0:width], ACT.Ln, scale=1.0 / 256, bias=con("eps"))\
                        .then_inc(M.out(key), 1)
                    M.wait_out(act, key)
                    nc.scalar.activation(r, r, ACT.Exp, scale=-0.5).then_inc(sem(f"x{name}inv"), 1)

                for m in range(KD):
                    key = ({"k": "kx", "q": "xq"}[name], m)
                    move(key, dst[:, m, 0:width], lambda o: o[:, 0:width])
                    M.wait_out(act, key)
                    if m >= 4:
                        M.full(act, (name + "n", m // 2 - 2))
                    nc.scalar.activation(xsq[:, m % 4, 0:width], dst[:, m, 0:width], ACT.Square)\
                        .then_inc(sem(f"x{name}sq_ready"), 1)
                    split_after(m)
                    if m % 2 == 0:
                        inverse(m // 2 - 1)
                inverse(XA_HEADS - 1)

            heads_norm("k", kx, MEM)
            inverse_rms(4, T)
            for c in range(4):
                for b in range(2):
                    move(("vx", c, b), vx[:, b, 256 * c:256 * (c + 1)], lambda o: o[:, 0:256])
                split_weights()
                for k in (2 * c, 2 * c + 1):
                    act.wait_ge(sem("h_raw"), KD * 3 + k + 1)
                    high(h_hi[:, k, :], h_raw[:, k, :], sem("h_hi"))
            act.wait_ge(sem("kx_ready"), 8)
            heads_norm("q", qx, T)
            N = XA_HEADS * NB
            for i in range(N + 6):
                if i < N:
                    M.wait_out(act, ("x", i))
                    if i >= 3:
                        TR.full(act, ("Tx", i - 3))
                        act.wait_ge(sem("xa_w"), i - 2)
                    nc.scalar.activation(xexp[:, i % 3, :], xneg[:, i % 3, :], ACT.Exp, scale=-1.0,
                                         bias=small[:, 8 + i % 3:9 + i % 3],
                                         accum_out=small[:, 11 + i % 3:12 + i % 3]).then_inc(sem("xa_exp"), 1)
                n = i - 2
                if 0 <= n < N:
                    move(("Tx", n), xpt[:, n % 3, :], lambda o: o[:, 0:MEM], TR)
                n = i - 5
                if 0 <= n < N and n % NB == NB - 1:
                    PV.wait_out(act, ("yx", n))
                    for m in (2 * (n // NB), 2 * (n // NB) + 1):
                        high(h_hi[:, m, :], h_raw[:, m, :], sem("xa_hi"))
            squares(5, xres, T, lambda k: M.wait_out(act, ("xo", k)), split_after)
            inverse_rms(5, T)
            nc.scalar.preload_act_table_set("gelu_and_others")
            high_h(4)

            act.wait_ge(sem("conv_zero"), 1)
            for j in range(KF // 2 + 1):
                if j:
                    split_weights()
                if j < KF // 2:
                    for mi in range(2):
                        m = 2 * j + mi
                        if m >= 3:
                            act.wait_ge(sem("conv"), m - 2)
                        move(("up", m, 0), conv_in[:, m % 3, 2:T + 2])
                    split_weights()
                if j:
                    for m in (2 * j - 2, 2 * j - 1):
                        M.wait_out(act, ("up", m, 1))
                        high(gact_hi[:, m, :], gact_raw[:, m, :], sem("gact_hi"))
                if j < KF // 2:
                    for mi in range(2):
                        m = 2 * j + mi
                        act.wait_ge(sem("conv"), m + 1)
                        nc.scalar.activation(gact_raw[:, m, :], gact_raw[:, m, :], ACT.Gelu).then_inc(sem("gelu"), 1)
            for _ in range(DOWN):
                split_weights()
            assert chunks[0] == STREAM + DOWN + HI

        @block.vector
        def _(dve):
            links = [0]
            tt, ts, stt = nc.vector.tensor_tensor, nc.vector.tensor_scalar, nc.vector.scalar_tensor_tensor

            def link(ins):
                links[0] += 1
                ins.then_inc(sem("dve_link"), 1)
                dve.wait_ge(sem("dve_link"), links[0])

            def add_square(n, k, width):
                i = KD * n + k
                dve.wait_ge(sem("squares"), i + 1)
                s_ = sq[:, i % 2, 0:width]
                if k == 0:
                    if n:
                        (PV if n in (2, 3) else M).full(dve, ("norm", n - 1))
                    nc.vector.tensor_copy(acc[:, 0:width], s_).then_inc(sem("squares_added"), 1)
                else:
                    dve.wait_ge(sem("squares_added"), i)
                    tt(acc[:, 0:width], acc[:, 0:width], s_, ALU.add).then_inc(sem("squares_added"), 1)

            def low(lo, raw, hi, done):
                return tt(lo, raw, hi.bitcast(F32), ALU.subtract).then_inc(done, 1)

            def scaled(n, src, dst, g, width, done):
                dve.wait_ge(sem("rms_ready"), n + 1)
                for k in range(KD):
                    stt(dst[:, k, 0:width], src[:, k, 0:width], par(g, k), rms[:, 0:width], ALU.mult, ALU.mult)\
                        .then_inc(done, 1)

            def low_h(n, k, lo, raw, hi):
                dve.wait_ge(sem("h_hi"), KD * n + k + 1)
                low(lo[:, k, :], raw[:, k, :], hi[:, k, :], sem("h_ready"))

            def scaled_h(norm, n, g):
                dve.wait_ge(sem("rms_ready"), norm + 1)
                for k in range(KD + 2):
                    if k < KD:
                        stt(h_raw[:, k, :], xres[:, k, :], par(g, k), rms[:, :], ALU.mult, ALU.mult)\
                            .then_inc(sem("h_raw"), 1)
                    if k >= 2:
                        low_h(n, k - 2, h_lo, h_raw, h_hi)

            dve.wait_ge(sem("params_loaded"), 16)
            ts(nparams[:, :], params[:, 0:NCOLS], -1.0, None, ALU.mult).then_inc(sem("negated"), 1)
            tt(small[:, 0:2], par("lq", 0, 2), par("lk", 0, 2), ALU.mult).then_inc(sem("lam_products"), 1)
            ts(dq8[:, 0:1], par("dq_g"), HEAD ** -0.5, None, ALU.mult)
            link(ts(dq8[:, 1:2], par("subln"), 1.0 - LAMBDA_INIT, None, ALU.mult))
            for k in range(KD):
                add_square(0, k, T)
            def ada_sums(first, last):
                for i in range(first, last):
                    dve.wait_ge(sem(f"ada{i}_loaded"), 16)
                    total = ada_w[:, i, :, 0, :]
                    link(ts(total, total, par("c", 0), None, ALU.mult))
                    for k in range(1, KD):
                        ins = stt(total, ada_w[:, i, :, k, :], par("c", k), total, ALU.mult, ALU.add)
                        if k < KD - 1:
                            link(ins)
                    ins.then_inc(sem("ada_sums"), 1)

            ada_sums(0, ADA_FIRST)
            tt(gmix[:, :], par("final_g", 0, 8), par("mix_g", 0, 8), ALU.mult)
            dve.wait_ge(sem("wf_hi"), 1)
            tt(wf_lo, par("w_f", 0, 64), wf_hi.bitcast(F32), ALU.subtract).then_inc(sem("wf_split"), 1)
            M.wait_out(dve, "lam")
            link(tt(small[:, 4:5], small[:, 2:3], small[:, 3:4], ALU.subtract))
            link(ts(small[:, 5:6], small[:, 4:5], LAMBDA_INIT, -1.0, ALU.add, ALU.mult))
            nlam = small[:, 5:6]
            o = M.full(dve, "mod")
            tt(mod[:, 0:16], o[:, 0:16], par("b_ada", 0, 16), ALU.add).then_inc(M.out("mod"), 1)
            M.wait_out(dve, "mod")
            link(stt(gmod[:, :], mod[:, 8:16], 1.0, par("norm_g", 0, 8), ALU.add, ALU.mult))
            dve.wait_ge(sem("rms_ready"), 1)
            for k in range(KD + 3):
                if k < KD:
                    stt(h_raw[:, k, :], xres[:, k, :], gmod[:, k:k + 1], rms[:, :], ALU.mult, ALU.mult)\
                        .then_inc(sem("h_scaled"), 1)
                if 1 <= k <= KD:
                    dve.wait_ge(sem("h_scaled"), k)
                    ts(h_raw[:, k - 1, :], h_raw[:, k - 1, :], mod[:, k - 1:k], None, ALU.add).then_inc(sem("h_raw"), 1)
                if k >= 3:
                    low_h(0, k - 3, h_lo, h_raw, h_hi)
            for i, name in enumerate(("ident", "mask_strict", "mask_incl")):
                nc.vector.tensor_copy(masks[:, i, :], con(name)).then_inc(sem("masks"), 1)
            ada_sums(ADA_FIRST, ADA)
            o = M.full(dve, "gate")
            tt(mod[:, 16:24], o[:, 0:8], par("b_ada", 16, 8), ALU.add).then_inc(M.out("gate"), 1)

            def move(key, dst, src=None, ring_=M):
                o = ring_.full(dve, key)
                nc.vector.tensor_copy(dst, o if src is None else src(o)).then_inc(ring_.out(key), 1)

            def silu(tag, m):
                dve.wait_ge(sem("silu_gate"), 4 * (tag == "b") + m + 1)
                tt(gated[tag][:, m, :], gated[tag][:, m, :], z_gate[:, m % 2, :], ALU.mult).then_inc(sem("silu"), 1)

            for m in range(4):
                move(("ka", m), ka[:, m, :])
            for m in range(4):
                silu("a", m)
            for m in range(4):
                move(("kb", m), kb[:, m, :])
            fx, fa = nF_bc[0:HEADS, 0, :], nF_bc[0:HEADS, 1, :]
            dve.wait_ge(sem("f_ln"), 1)
            link(stt(fx, fx, 0.0, fa, ALU.max, ALU.add))
            nc.vector.tensor_tensor_scan(nF[0:HEADS, :], ones(T, HEADS), fx, 0.0, ALU.mult, ALU.add)\
                .then_inc(sem("nF_ready"), 1)

            N = HEADS * NB
            for i in range(N + 8):
                n = i - 4
                if 0 <= n < N:
                    end = P * (n % NB + 1)
                    move(("Ta", n), ptb[:, n % 3, 0:end], lambda o: o[:, 0:end], TR)
                if i < N:
                    end = P * (i % NB + 1)
                    o = M.full(dve, ("a", i))
                    sp, w = spb[:, i % 2, 0:end], wbuf[:, i % WBUF, 0:end]
                    dve.wait_ge(sem("stick_ln"), i + 1)
                    stt(sp, o[:, 0:end], 0.0, ebuf[:, i % 3, 0:end], ALU.max, ALU.add).then_inc(sem("stick_sp"), 1)
                    dve.wait_ge(sem("stick_sp"), i + 1)
                    if i >= WBUF:
                        TR.full(dve, ("Ta", i - WBUF))
                    link(nc.vector.tensor_tensor_scan(w[:, ::-1], ones(end), sp[:, ::-1], 0.0, ALU.mult, ALU.add))
                    tt(w, o[:, 0:end], w, ALU.subtract).then_inc(M.out(("a", i)), 1)
                if i % 4 == 3 and 16 < i < N:
                    silu("b", (i - 16) // 4)
                n = i - 7
                if 0 <= n < N and n % 8 == 7:
                    o = PV.full(dve, ("ya", n // 8))
                    g = gated["a"][:, n // 8, :]
                    tt(g, o, g, ALU.mult).then_inc(PV.out(("ya", n // 8)), 1)

            def soft(key, i, slot, width, bias, scale, neg, lowest):
                o = M.full(dve, key)
                nc.vector.tensor_tensor_reduce(neg[:, slot, 0:width], o[:, 0:width], bias, -scale, 3.0e38,
                                               ALU.add, ALU.min, lowest).then_inc(M.out(key), 1)

            for i in range(N + 6):
                if i < N:
                    hd, b = divmod(i, NB)
                    end = P * (b + 1)
                    if b == 0:
                        M.wait_out(dve, ("nF", hd))
                    if i >= 3:
                        dve.wait_ge(sem("fox_exp"), i - 2)
                    soft(("b", i), i, i % 3, end, nF_bc[:, hd % 2, 0:end], 1.0, negb, small[:, 8 + i % 3:9 + i % 3])
                n = i - 1
                if 0 <= n < N:
                    end = P * (n % NB + 1)
                    dve.wait_ge(sem("fox_exp"), n + 1)
                    link(nc.vector.reciprocal(small[:, 14 + n % 3:15 + n % 3], small[:, 11 + n % 3:12 + n % 3]))
                    w = expb[:, n % 3, 0:end]
                    ts(w, w, small[:, 14 + n % 3:15 + n % 3], None, ALU.mult).then_inc(sem("fox_w"), 1)
                n = i - 5
                if 0 <= n < N and n % 8 == 7:
                    o = PV.full(dve, ("yb", n // 8))
                    g = gated["b"][:, n // 8, :]
                    tt(g, o, g, ALU.mult).then_inc(PV.out(("yb", n // 8)), 1)

            for m in range(8):
                dve.wait_ge(sem("gated_hi"), m + 1)
                low(gated_lo[:, m, :], gated_raw[:, m, :], gated_hi[m], sem("gated_split"))
            dve.wait_ge(sem("gates"), 16)
            for m in range(KD):
                o = M.full(dve, ("oa", m))
                tt(gates[m], o, gates[m], ALU.mult).then_inc(M.out(("oa", m)), 1)
            for m in range(KD + 1):
                if m < KD:
                    o = M.full(dve, ("ob", m))
                    tt(gates[KD + m], o, gates[KD + m], ALU.mult).then_inc(M.out(("ob", m)), 1)
                    M.wait_out(dve, ("ob", m))
                    M.wait_out(dve, ("oa", m))
                    tt(merged_raw[:, m, :], gates[m], gates[KD + m], ALU.add).then_inc(sem("merged_raw"), 1)
                if m:
                    dve.wait_ge(sem("merged_hi"), m)
                    low(merged_lo[:, m - 1, :], merged_raw[:, m - 1, :], merged_hi[m - 1], sem("merged"))

            def residual(key, n, extra=None, gate=None):
                for m in range(KD + 1):
                    if m < KD:
                        o = M.full(dve, (key, m))
                        if gate is not None:
                            ins = stt(xres[:, m, :], o, gate(m), xres[:, m, :], ALU.mult, ALU.add)
                        else:
                            ins = tt(xres[:, m, :], o, xres[:, m, :], ALU.add)
                        ins.then_inc(M.out((key, m)), 1)
                        if extra is not None:
                            extra(m)
                    if m >= 1 and n is not None:
                        add_square(n, m - 1, T)
                if extra is not None:
                    extra(KD)

            def mixers_input(m):
                if m < KD:
                    M.wait_out(dve, ("wo", m))
                    ts(h_raw[:, m, :], xres[:, m, :], gmix[:, m:m + 1], None, ALU.mult).then_inc(sem("h_raw"), 1)
                if m >= 1:
                    low_h(1, m - 1, h_lo, h_raw, h_hi)

            residual("wo", 1, mixers_input, gate=lambda m: mod[:, 16 + m:17 + m])
            scaled(1, xres, xres, "final_g", T, sem("x2_ready"))
            for k in range(KD):
                add_square(2, k, T)
            dve.wait_ge(sem("rms_ready"), 3)
            tt(zscale, rms[:, :], rms2, ALU.mult).then_inc(sem("zscale"), 1)

            dve.wait_ge(sem("pads_zero"), 1)
            dve.wait_ge(sem("zscale"), 1)

            def token_scaled(key, dst):
                o = M.full(dve, key)
                tt(dst, o, zscale, ALU.mult).then_inc(M.out(key), 1)

            for m in range(8):
                if m:
                    dve.wait_ge(sem("zm"), m)
                z = zraw[:, m % 3, :]
                token_scaled(("zr", m), z[:, 1:T + 1])
                M.wait_out(dve, ("zr", m))
                link(tt(tA, z[:, 0:T], z[:, 1:T + 1], ALU.subtract))
                stt(zm[:, m, :], tA, par("mu", m), z[:, 1:T + 1], ALU.mult, ALU.add).then_inc(sem("zm"), 1)
            win = [at(MAT, POOL_W), at(MAT + 1024, POOL_W)]
            inv_count = con("inv_count", 2, T)
            dve.wait_ge(sem("mix_loaded"), 16)
            for j in range(2):
                token_scaled(("zp", j), pool_u[:, j, PAD:PAD + T])
                M.wait_out(dve, ("zp", j))
                u = pool_u[:, j, :]
                link(tt(win[0][:, 1:], u[:, 1:], u[:, :-1], ALU.add))
                link(tt(win[1][:, 3:], win[0][:, 3:], win[0][:, 1:-2], ALU.add))
                if j == 1:
                    link(tt(win[0][:, 7:], win[1][:, 7:], win[1][:, 3:-4], ALU.add))
                    link(tt(win[1][64:, 15:], win[0][64:, 15:], win[0][64:, 7:-8], ALU.add))
                for half in range(2):
                    rows = slice(64 * half, 64 * half + 64)
                    d = ycat03[rows, j, :]
                    link(tt(d, win[half][rows, PAD:], inv_count[rows, j, :], ALU.mult))
                    ins = tt(d, d, u[rows, PAD:], ALU.subtract)
                ins.then_inc(sem("pooled"), 1)
            def dq_out(first, last):
                for t in range(first, last):
                    token_scaled(("dq", t), dqk[:, t, :])

            dve.wait_ge(sem("x2_stored"), 16)
            dq_out(0, 2)
            dve.wait_ge(sem("lora_exp"), 1)
            ts(zm[0:64, 6, :], tA[0:64, :], -2.0, 1.0, ALU.mult, ALU.add).then_inc(sem("lora_in"), 1)

            dq_out(2, 4)
            for j in range(2):
                r_, k_, v_ = zm[:, j, :], zm[:, 2 + j, :], zm[:, 4 + j, :]
                ts(adec, k_, par("k_k", j), None, ALU.mult).then_inc(sem("kk0"), 1)
                dve.wait_ge(sem("rates"), 2 * j + 2)
                if j == 0:
                    dq_out(4, 5)
                o = M.full(dve, ("kk", j))
                ts(tB, o, float(HEAD), 1e-24, ALU.mult, ALU.max).then_inc(M.out(("kk", j)), 1)
                M.wait_out(dve, ("kk", j))
                nc.vector.engine_nop().then_inc(sem("kk_floor"), 1)
                link(ts(kvec, avec, 1.0, par("k_a", j), ALU.subtract, ALU.mult))
                link(stt(kvec, kvec, 1.0, k_, ALU.add, ALU.mult))
                stt(rst, r_, par("r_k", j), kvec, ALU.mult, ALU.mult).then_inc(sem("rk_ready"), 1)
                nc.vector.tensor_tensor_scan(tA, con("restart"), decay, 0.0, ALU.mult, ALU.subtract)\
                    .then_inc(sem("L_ready"), 1)
                dve.wait_ge(sem("L_ready"), 2 * j + 1)
                tt(decay, tA, decay, ALU.add).then_inc(sem("L_ready"), 1)
                dve.wait_ge(sem("kk_norm"), j + 1)
                link(tt(adec, adec, tB, ALU.mult))
                link(tt(bdec, avec, adec, ALU.mult))
                dve.wait_ge(sem("exps"), 4 * j + 4)
                tt(rdec, rdec, r_, ALU.mult).then_inc(sem("decayed"), 1)
                tt(bdec, bdec, kdec, ALU.mult).then_inc(sem("decayed"), 1)
                tt(kdec, kdec, kvec, ALU.mult).then_inc(sem("decayed"), 1)
                stt(adec, adec, -1.0, decay, ALU.mult, ALU.mult).then_inc(sem("decayed"), 1)
                o = M.full(dve, ("bonus", j))
                stt(bonus, o, float(HEAD), v_, ALU.mult, ALU.mult).then_inc(M.out(("bonus", j)), 1)
                if j == 0:
                    dq_out(5, 8)

                def spread(m):
                    return m.unsqueeze(1).broadcast_to([P, NB, P])

                four = lambda o: o.rearrange("p (a b) -> p a b", a=4)

                def masked(name, dst, mask):
                    for hh in range(2):
                        o = M.full(dve, (name, j, hh))
                        tt(dst[hh], four(o), spread(mask), ALU.mult).then_inc(M.out((name, j, hh)), 1)

                masked("A", Am, con("tri_lower"))
                masked("AT", AmT, con("tri_upper"))
                low0, up0 = con("lower", 6, P)[:, 0, :], con("upper", 6, P)[:, 0, :]
                for hh in range(2):
                    M.wait_out(dve, ("AT", j, hh))
                    tt(Tm[hh], Am[hh], spread(low0), ALU.mult)
                    link(tt(Wm[hh], AmT[hh], spread(up0), ALU.mult))
                    tt(Tm[hh], Tm[hh], spread(ident), ALU.add).then_inc(sem("inverse"), 1)
                    tt(Wm[hh], Wm[hh], spread(ident), ALU.add).then_inc(sem("inverse"), 1)
                for lv in range(1, 6):
                    for hh in range(2):
                        move(("ZT", j, lv, hh), OmT[hh], four)
                    for hh in range(2):
                        dw = M.full(dve, ("dW", j, lv, hh))
                        if lv == 1 and hh == 0:
                            dve.wait_ge(sem("inverse"), 4 * j + 4)
                        if lv > 1:
                            M.wait_out(dve, ("dT", j, lv - 1, hh))
                            M.wait_out(dve, ("dW", j, lv - 1, hh))
                        if lv < 5:
                            dt_ = M.full(dve, ("dT", j, lv, hh))
                            tt(Tm[hh], four(dt_), Tm[hh], ALU.add).then_inc(M.out(("dT", j, lv, hh)), 1)
                        tt(Wm[hh], four(dw), Wm[hh], ALU.add).then_inc(M.out(("dW", j, lv, hh)), 1)
                    if j == 1 and lv >= 2:
                        for t in (2 * lv - 4, 2 * lv - 3):
                            dve.wait_ge(sem("qk_inverse"), t + 1)
                            g = dq8[:, 0:1] if t < 4 else par("dk_g")
                            stt(dqk[:, t, :], dqk[:, t, :], g, qk_rinv[t % 2], ALU.mult, ALU.mult)\
                                .then_inc(sem("dqk_ready"), 1)
                masked("Aak", AakT, con("tri_upper"))
                masked("Arb", ArbT, con("tri_incl"))
                masked("Ark", ArkT, con("tri_incl"))
                move(("Q", j), Qm.rearrange("p a b c -> p (a b c)"))
                half = lambda o: o[:, 0:256].rearrange("p (a b) -> p a b", a=NB)
                for odd in range(2):
                    o = M.full(dve, ("Mt", j, odd))
                    tt(Mt[:, odd::2, :], half(o), con("ident64").unsqueeze(1).broadcast_to([P, NB, CHUNK]), ALU.add)\
                        .then_inc(M.out(("Mt", j, odd)), 1)
                for odd in range(2):
                    o = M.full(dve, ("H0", j, odd))
                    tt(H0[:, odd::2, :], half(o), small[:, 24 + odd:32:2].unsqueeze(2).broadcast_to([P, NB, CHUNK]),
                       ALU.mult).then_inc(M.out(("H0", j, odd)), 1)
                for odd in range(2):
                    M.wait_out(dve, ("H0", j, odd))
                nc.vector.tensor_copy(St[:, 1, :], H0[:, 0, :]).then_inc(sem("state"), 1)
                o = M.full(dve, ("R", j))
                tt(rst, o, rdec, ALU.add).then_inc(M.out(("R", j)), 1)
                for c in range(1, NCH - 1):
                    o = TR.full(dve, ("S", j, c))
                    stt(St[:, c + 1, :], o[:, 0:CHUNK], small[:, 24 + c:25 + c], H0[:, c, :], ALU.mult, ALU.add)\
                        .then_inc(TR.out(("S", j, c)), 1)
                o = M.full(dve, ("ymean", j))
                PV.wait_out(dve, ("yr", j))
                tt(tA, tA, o, ALU.subtract).then_inc(M.out(("ymean", j)), 1)
                dve.wait_ge(sem("y_rstd"), j + 1)
                link(tt(tA, tA, tB, ALU.mult))
                link(ts(tA, tA, par("ln_w", j), par("ln_b", j), ALU.mult, ALU.add))
                link(tt(tA, tA, bonus, ALU.add))
                tt(ycat03[:, 2 + j, :], tA, gout, ALU.mult).then_inc(sem("rwkv_out"), 1)

            dve.wait_ge(sem("dist_loaded"), 16)
            for m in range(4):
                dve.wait_ge(sem("mixers_hi"), m + 1)
                low(h_lo[:, m, :], ycat03[:, m, :], h_hi[:, m, :], sem("mixers_split"))
            dist = con("dist", DIFF_HEADS, T)
            N = DIFF_HEADS * NB
            for i in range(N + 8):
                if i < N:
                    hd, b = divmod(i, NB)
                    end = P * (b + 1)
                    for cp in range(2):
                        if i >= 2:
                            dve.wait_ge(sem("diff_exp"), 2 * (i - 2) + cp + 1)
                        c = 2 * (i % 2) + cp
                        soft(("d", i, cp), i, c, end, dist[:, hd, T - end:T], 1.0, dneg, small[:, 32 + c:33 + c])
                n = i - 1
                if 0 <= n < N:
                    end = P * (n % NB + 1)
                    dve.wait_ge(sem("diff_exp"), 2 * n + 2)
                    c = 2 * (n % 2)
                    e0, e1 = (dexp[:, 2 * (n % 3) + cp, 0:end] for cp in range(2))
                    link(nc.vector.reciprocal(small[:, 40:42], small[:, 36 + c:38 + c]))
                    ts(small[:, 42:43], small[:, 41:42], nlam, None, ALU.mult)
                    link(ts(e0, e0, small[:, 40:41], None, ALU.mult))
                    stt(e0, e1, small[:, 42:43], e0, ALU.mult, ALU.add).then_inc(sem("diff_w"), 1)
                n = i - 6
                if 0 <= n < N and n % NB == NB - 1:
                    hd = n // NB
                    o = PV.full(dve, ("yd", hd))
                    dve.wait_ge(sem("oinv"), hd + 1)
                    stt(h_raw[:, 4 + hd, :], o, dq8[:, 1:2], drinv[:, hd % 2, :], ALU.mult, ALU.mult)\
                        .then_inc(PV.out(("yd", hd)), 1)
                n = i - 7
                if 0 <= n < N and n % NB == NB - 1:
                    hd = n // NB
                    dve.wait_ge(sem("mixers_hi"), 5 + hd)
                    low(h_lo[:, 4 + hd, :], h_raw[:, 4 + hd, :], h_hi[:, 4 + hd, :], sem("mixers_split"))

            for k in range(KD):
                add_square(3, k, MEM)

            def mem_norm(m):
                if m == 3:
                    scaled(3, memx, memn_raw, "mem_g", MEM, sem("h_raw"))
                if m == 6:
                    for k in range(KD):
                        low_h(2, k, memn_lo, memn_raw, memn_hi)

            dve.wait_ge(sem("x2_back"), 16)
            residual("wo2", 4, mem_norm)

            def heads_scaled(name, dst, g, width):
                for m in range(KD):
                    dve.wait_ge(sem(f"x{name}inv"), m // 2 + 1)
                    stt(dst[:, m, 0:width], dst[:, m, 0:width], par(g, m % 2), xrinv[:, m // 2 % 2, 0:width],
                        ALU.mult, ALU.mult).then_inc(sem(f"{name}x_ready"), 1)

            heads_scaled("k", kx, "xk_g", MEM)
            scaled_h(4, 3, "xa_g")
            heads_scaled("q", qx, "xq_g", T)
            N = XA_HEADS * NB
            zeros = small[:, 63:64].broadcast_to([P, MEM])
            for i in range(N + 6):
                if i < N:
                    if i >= 3:
                        dve.wait_ge(sem("xa_exp"), i - 2)
                    soft(("x", i), i, i % 3, MEM, zeros, 256 ** -0.5, xneg, small[:, 8 + i % 3:9 + i % 3])
                n = i - 1
                if 0 <= n < N:
                    dve.wait_ge(sem("xa_exp"), n + 1)
                    link(nc.vector.reciprocal(small[:, 14 + n % 3:15 + n % 3], small[:, 11 + n % 3:12 + n % 3]))
                    w = xexp[:, n % 3, :]
                    ts(w, w, small[:, 14 + n % 3:15 + n % 3], None, ALU.mult).then_inc(sem("xa_w"), 1)
                n = i - 4
                if 0 <= n < N:
                    hd, b = divmod(n, NB)
                    move(("yx", n), h_raw[:, 2 * hd:2 * hd + 2, P * b:P * (b + 1)],
                         lambda o: o[:, 0:2 * P].rearrange("p (j n) -> p j n", j=2), PV)
                n = i - 5
                if 0 <= n < N and n % NB == NB - 1:
                    for m in (2 * (n // NB), 2 * (n // NB) + 1):
                        dve.wait_ge(sem("xa_hi"), m + 1)
                        low(h_lo[:, m, :], h_raw[:, m, :], h_hi[:, m, :], sem("xa_split"))
            residual("xo", 5)
            scaled_h(5, 4, "ffn_g")

            for j in range(KF // 2 + 1):
                if j < KF // 2:
                    for mi in range(2):
                        m = 2 * j + mi
                        M.wait_out(dve, ("up", m, 0))
                        a, c = conv_in[:, m % 3, :], gact_raw[:, m, :]
                        link(ts(c, a[:, 0:T], par("conv_w", m), par("conv_b", m), ALU.mult, ALU.add))
                        link(stt(c, a[:, 1:T + 1], par("conv_w", KF + m), c, ALU.mult, ALU.add))
                        stt(c, a[:, 2:T + 2], par("conv_w", 2 * KF + m), c, ALU.mult, ALU.add).then_inc(sem("conv"), 1)
                if j:
                    for m in (2 * j - 2, 2 * j - 1):
                        dve.wait_ge(sem("gact_hi"), m + 1)
                        low(gact_lo[:, m, :], gact_raw[:, m, :], gact_hi[:, m, :], sem("gact_split"))
                if j < KF // 2:
                    for mi in range(2):
                        m = 2 * j + mi
                        dve.wait_ge(sem("gelu"), m + 1)
                        o = M.full(dve, ("up", m, 1))
                        tt(gact_raw[:, m, :], o, gact_raw[:, m, :], ALU.mult).then_inc(M.out(("up", m, 1)), 1)
            residual("down", None)

        @block.gpsimd
        def _(pool):
            def low_weights(first, last):
                for c in range(first, last):
                    n = CHUNK_F if c < STREAM else DOWN_K * P
                    raw, lo = w_raw[:, c % RAW, 0:n], w_lo[:, c % RAW, 0:n]
                    pool.wait_ge(sem("weights_hi"), c + 1)
                    nc.gpsimd.tensor_tensor(lo, raw, w_hi[:, c % HI, 0:n].bitcast(F32), ALU.subtract)\
                        .then_inc(sem("weights_split"), 1)

            nc.gpsimd.memset(small[:, 63:64], 0.0).then_inc(sem("fills"), 1)
            mixers = chunk_end.index(("zr", 1))
            low_weights(0, mixers + HI)
            pool.wait_ge(sem("x2_ready"), 1)
            for s in range(3):
                nc.gpsimd.memset(zraw[:, s, 0:1], 0.0)
            for j in range(2):
                ins = nc.gpsimd.memset(pool_u[:, j, 0:PAD], 0.0)
            ins.then_inc(sem("pads_zero"), 1)
            diff = chunk_end.index(("dq", 7)) + 1
            low_weights(mixers + HI, diff + HI)
            pool.wait_ge(sem("mix_loaded"), 16)
            lower, upper = con("lower", 6, P), con("upper", 6, P)
            for j in range(2):
                if j == 1:
                    low_weights(diff + HI, diff + 2 * HI)
                for lv in range(1, 6):
                    for hh in range(2):
                        if lv == 1:
                            M.wait_out(pool, ("AT", j, hh))
                        else:
                            M.full(pool, ("dW", j, lv - 1, hh))
                        nc.gpsimd.tensor_tensor(Om[hh], Am[hh], lower[:, lv, :].unsqueeze(1).broadcast_to([P, NB, P]),
                                                ALU.mult).then_inc(sem("corner"), 1)
                        nc.gpsimd.tensor_tensor(OmT[hh], AmT[hh], upper[:, lv, :].unsqueeze(1).broadcast_to([P, NB, P]),
                                                ALU.mult).then_inc(sem("corner"), 1)
            up = chunk_end.index(("up", 1, 0))
            low_weights(diff + 2 * HI, up + HI)
            pool.wait_ge(sem("h_raw"), 4 * KD + 1)
            for s in range(3):
                ins = nc.gpsimd.memset(conv_in[:, s, 0:2], 0.0)
            ins.then_inc(sem("conv_zero"), 1)
            low_weights(up + HI, STREAM + DOWN)

        @block.sync
        def _(sp):
            sp.dma_start(xres[:, :, :], x_in).then_inc(sem("x_loaded"), 16)
            sp.dma_start(params[:, :], params_in).then_inc(sem("params_loaded"), 16)
            sp.dma_start(consts[:, :], consts_in[:, 0:MIX_COL]).then_inc(sem("consts_loaded"), 16)
            for i in range(ADA):
                sp.dma_start(at(4096 * i, 2, CHUNK_F), ada_in[2 * i:2 * i + 2].rearrange("c p n -> p c n"))\
                    .then_inc(sem(f"ada{i}_loaded"), 16)
                if i == ADA_FIRST - 1:
                    for c in range(RAW):
                        sp.dma_start(w_raw[:, c, :], stream_in[c]).then_inc(loaded[c], 16)
            rounds = STREAM // RAW
            with sp.Fori(1, rounds) as i:
                for s in range(RAW):
                    sp.wait_ge(used[s], i)
                    sp.dma_start(w_raw[:, s, :], stream_in[bass.ds(i * RAW + s, 1), :, :].rearrange("a p n -> p (a n)"))\
                        .then_inc(loaded[s], 16)
            for c in range(rounds * RAW, STREAM):
                sp.wait_ge(used[c % RAW], c // RAW)
                sp.dma_start(w_raw[:, c % RAW, :], stream_in[c]).then_inc(loaded[c % RAW], 16)
            width = DOWN_K * P
            rounds = DOWN // RAW
            with sp.Fori(0, rounds) as i:
                for s in range(RAW):
                    slot = (STREAM + s) % RAW
                    sp.wait_ge(used[slot], i + (STREAM + s) // RAW)
                    sp.dma_start(w_raw[:, slot, 0:width],
                                 down_in[bass.ds(i * RAW + s, 1), :, :].rearrange("a p n -> p (a n)"))\
                        .then_inc(loaded[slot], 16)
            for c in range(rounds * RAW, DOWN):
                slot = (STREAM + c) % RAW
                sp.wait_ge(used[slot], (STREAM + c) // RAW)
                sp.dma_start(w_raw[:, slot, 0:width], down_in[c]).then_inc(loaded[slot], 16)
            for m in range(KD):
                M.wait_out(sp, ("down", m))
                sp.dma_start(out[:, m, :], xres[:, m, :]).then_inc(sem("stored"), 16)
            sp.wait_ge(sem("stored"), 16 * KD)


def columns(v, n):
    return np.asarray(v, np.float32).reshape(n, P).T


def lay_params(a):
    out = np.zeros((P, NPARAM), np.float32)

    def put(name, value):
        i, n = PARAM_COLS[name]
        out[0:value.shape[0], i:i + n] = value

    for name, key in (("c", "c"), ("b_ada", "b_ada"), ("norm_g", "norm_g"), ("b_gate", "b_gate"),
                      ("final_g", "final_g"), ("mix_g", "mix_norm_g_2"), ("pool_scale", "pool_scale_2"),
                      ("mu", "rwkv_mu_2"), ("w0", "rwkv_w0_2"), ("a0", "rwkv_a0_2"), ("k_k", "rwkv_k_k_2"),
                      ("k_a", "rwkv_k_a_2"), ("r_k", "rwkv_r_k_2"), ("ln_w", "rwkv_ln_w_2"),
                      ("ln_b", "rwkv_ln_b_2"), ("dq_g", "diff_q_norm_2"), ("dk_g", "diff_k_norm_2"),
                      ("subln", "diff_subln_2"), ("xa_g", "xa_norm_g_2"), ("mem_g", "mem_norm_g_2"),
                      ("xq_g", "xa_q_norm_2"), ("xk_g", "xa_k_norm_2"), ("ffn_g", "ffn_norm_g_2"),
                      ("conv_w", "ffn_conv_w_2"), ("conv_b", "ffn_conv_b_2")):
        put(name, columns(a[key], PARAM_COLS[name][1]))
    for name, keys in (("lq", ("diff_lq1_2", "diff_lq2_2")), ("lk", ("diff_lk1_2", "diff_lk2_2"))):
        two = np.zeros((HEAD, 2), np.float32)
        for i, key in enumerate(keys):
            two[:, i] = np.asarray(a[key]).reshape(-1)
        put(name, two)
    put("b_forget", np.asarray(a["b_forget"]).reshape(HEADS, 1))
    w_f = np.asarray(a["w_in"])[0][:, 4096:4096 + HEADS]
    put("w_f", w_f.reshape(KD, P, HEADS).transpose(1, 0, 2).reshape(P, -1))
    put("lora", np.concatenate([np.asarray(a["rwkv_w2_2"])[0], np.asarray(a["rwkv_a2_2"])[0]], 0))
    put("g2", np.asarray(a["rwkv_g2_2"])[0])
    w = np.asarray(a["pool_w_2"])[0]
    blocks = np.zeros((P, 2, P), np.float32)
    for g in range(4):
        r = HEAD * (g % 2)
        blocks[r:r + HEAD, g // 2, r:r + HEAD] = w[g]
    put("pool_w", blocks.reshape(P, -1))
    return out


def lay_chunks(w, cols):
    k, n = w.shape
    return w.reshape(k // P, P, n // cols, cols).transpose(2, 1, 0, 3).reshape(n // cols, P, -1)


def lay_stream(a):
    w_in, w_in2, up = (np.asarray(a[k])[0] for k in ("w_in", "w_in_2", "ffn_w_up_2"))
    parts = []
    for i in (0, 1, 2, 3, 4, 5, 6, 7):
        parts.append(lay_chunks(w_in[:, 512 * i:512 * (i + 1)], 256))
    parts.append(lay_chunks(w_in[:, 4096 + HEADS:], 256))
    parts.append(lay_chunks(np.asarray(a["w_o_sb"])[0], 512))
    parts.append(lay_chunks(np.asarray(a["w_o_fox"])[0], 512))
    parts.append(lay_chunks(np.asarray(a["w_out"])[0], 256))
    parts.append(lay_chunks(w_in2[:, 256:1280], 256))
    parts.append(lay_chunks(w_in2[:, 0:256], 256))
    parts.append(lay_chunks(w_in2[:, 1280:], 256))
    for key in ("w_out_2", "xa_wk_2", "xa_wv_2", "xa_wq_2", "xa_wo_2"):
        parts.append(lay_chunks(np.asarray(a[key])[0], 256))
    halves = [lay_chunks(up[:, FFN * i:FFN * (i + 1)], 256) for i in range(2)]
    parts.append(np.stack(halves, 1).reshape(2 * halves[0].shape[0], P, -1))
    return np.ascontiguousarray(np.concatenate(parts, 0))


def lay_down(w):
    return np.ascontiguousarray(
        w.reshape(2, DOWN_K, P, KD, P).transpose(3, 0, 2, 1, 4).reshape(DOWN, P, DOWN_K * P))


def kernel(**inputs):
    from concourse import bacc as _bacc
    from concourse.bass_utils import run_bass_kernel_spmd as _run

    a = {k: np.asarray(v) for k, v in inputs.items()}
    rows = lambda v: np.ascontiguousarray(v.T.reshape(KD, P, -1).transpose(1, 0, 2))
    arrays = {
        "x": rows(a["x"][0]),
        "mem": rows(a["mem_2"][0]),
        "params": lay_params(a),
        "consts": shape_constants(),
        "ada": lay_chunks(np.asarray(a["w_ada"])[0], 256),
        "stream": lay_stream(a),
        "down": lay_down(a["ffn_w_down_2"][0]),
    }
    nc = _bacc.Bacc("TRN2", target_bir_lowering=False, num_devices=1)
    ins = [nc.dram_tensor("in_" + n, list(v.shape), F32, kind="ExternalInput").ap() for n, v in arrays.items()]
    out = nc.dram_tensor("out", [P, KD, T], F32, kind="ExternalOutput").ap()
    x2_kept = nc.dram_tensor("x2_kept", [P, KD, T], F32, kind="Internal").ap()
    build(nc, *ins, out, x2_kept)
    r = _run(nc, [{"in_" + n: v for n, v in arrays.items()}], core_ids=[0])
    got = r.results[0]["out"]
    return np.ascontiguousarray(got.transpose(1, 0, 2).reshape(D, T).T)[None]
```

```python
from contextlib import ExitStack

import numpy as np

import concourse.bass as bass
from concourse import mybir

F32 = mybir.dt.float32
F32R = mybir.dt.float32r
BF16 = mybir.dt.bfloat16
ACT = mybir.ActivationFunctionType
ALU = mybir.AluOpType

P = 128
T = 512
D = 1024
KD = D // P
NB = T // P
HEAD = 64
HEADS = 8
FFN = 2816
KF = FFN // P
MEM = 256
DIFF_HEADS = 4
MEM_SUM, KX_STEP = 9, 14
EARLY = 2
SIDE_G = 11
WBUF = 5
XA_HEADS = 4
CHUNK = 64
NCH = T // CHUNK
POOL_WINDOWS = (2, 4, 8, 16)
PAD = 16
EPS = 1e-6
GN_EPS = 64e-5
NEG = -1e30
ARENA = 24800
MIX_AT = 21536
LAMBDA_INIT = 0.2


RAW = 3
HI = 2
CHUNK_F = KD * 256
ADA, ADA_FIRST = 6, 4
STREAM = 85
DOWN_K = KF // 2
DOWN = 2 * KD

PARAM_COLS = {}
_at = 0
for _n, _c in (("c", 8), ("b_ada", 24), ("norm_g", 8), ("b_gate", 16), ("final_g", 8), ("mix_g", 8),
               ("pool_scale", 2), ("mu", 8), ("w0", 2), ("a0", 2), ("k_k", 2), ("k_a", 2), ("r_k", 2),
               ("ln_w", 2), ("ln_b", 2), ("dq_g", 1), ("dk_g", 1), ("lq", 2), ("lk", 2), ("subln", 1),
               ("xa_g", 8), ("mem_g", 8), ("xq_g", 2), ("xk_g", 2), ("ffn_g", 8), ("conv_w", 66),
               ("conv_b", 22), ("b_forget", 1), ("w_f", 64), ("lora", 256), ("g2", 256), ("pool_w", 256)):
    PARAM_COLS[_n] = (_at, _c)
    _at += _c
NPARAM = _at
NCOLS = PARAM_COLS["w_f"][0]
LATE_PARAM = PARAM_COLS["lora"][0]

CONST_COLS = {}
_at = 0
for _n, _c in (("ident", 128), ("ones", 128), ("blk", 128), ("mask_strict", 128), ("mask_incl", 128),
               ("tri_lower", 128), ("tri_upper", 128), ("tri_incl", 128), ("ident64", 64),
               ("eps", 1), ("gn_eps", 1), ("neg_half", 1), ("head_row", 1024),
               ("inv_count", 1024), ("lower", 5 * 128), ("upper0", 128), ("restart", 512),
               ("dist", 4 * 512)):
    CONST_COLS[_n] = (_at, _c)
    _at += _c
NCONST = _at
LATE_COL = CONST_COLS["head_row"][0]
MIX_COL, DIFF_COL = CONST_COLS["inv_count"][0], CONST_COLS["dist"][0]


def shape_constants():
    i = np.arange(P)
    t, s = i[:, None], i[None, :]
    same = (t // CHUNK) == (s // CHUNK)
    out = np.zeros((P, NCONST), np.float32)

    def put(name, value):
        a, n = CONST_COLS[name]
        out[:, a:a + n] = np.asarray(value, np.float32).reshape(P, n)

    put("ident", np.eye(P))
    put("ones", np.ones((P, P)))
    put("blk", same / HEAD)
    put("mask_strict", np.where(s < t, 0.0, NEG))
    put("mask_incl", np.where(s <= t, 0.0, NEG))
    lower = []
    for lv in range(6):
        b = 1 << lv
        lower.append((t // (2 * b) == s // (2 * b)) & (t // b % 2 == 1) & (s // b % 2 == 0))
    put("lower", np.stack(lower[1:], 1))
    put("upper0", lower[0].T)
    put("tri_lower", same & (s < t))
    put("tri_upper", same & (s > t))
    put("tri_incl", same & (s >= t))
    put("ident64", (t % CHUNK) == np.arange(CHUNK)[None, :])
    tok = np.arange(T)
    inv = np.zeros((P, 2, T))
    for g, w in enumerate(POOL_WINDOWS):
        inv[HEAD * (g % 2):HEAD * (g % 2 + 1), g // 2] = 1.0 / np.minimum(tok + 1, w).astype(np.float32)
    put("inv_count", inv)
    put("restart", np.broadcast_to(tok % CHUNK != 0, (P, T)))
    rows = np.zeros((P, HEADS, P))
    for h in range(HEADS):
        rows[h, h] = 1.0
    put("head_row", rows)
    put("eps", np.full((P, 1), EPS))
    put("gn_eps", np.full((P, 1), GN_EPS))
    put("neg_half", np.full((P, 1), -0.5))
    j = np.arange(T)[None, :] - (T - P)
    dist = -np.abs(t - j).astype(np.float64)
    seen = (j < 0) | (j // CHUNK <= t // CHUNK)
    put("dist", np.stack([np.where(seen, dist * 2.0 ** (-8.0 * (h + 1) / DIFF_HEADS), NEG)
                          for h in range(DIFF_HEADS)], 1))
    return out


def build(nc, x_in, mem_in, params_in, consts_in, ada_in, stream_in, down_in, out, x2_kept):
    with ExitStack() as ctx:

        sems = {}

        def sem(name):
            if name not in sems:
                sems[name] = ctx.enter_context(nc.semaphore(name))
            return sems[name]

        class Ring:

            def __init__(self, name, banks):
                self.filled = sem(f"{name}_filled")
                self.ids = {}
                self.use(banks)

            def use(self, banks):
                self.banks = banks
                self.turn = 0

            def take(self, pe, key):
                b = self.banks[self.turn % len(self.banks)]
                self.turn += 1
                if tiles[b]:
                    pe.wait_ge(moved[b], tiles[b])
                tiles[b] += 1
                self.ids[key] = len(self.ids), b, tiles[b]
                return bank[b]

            def full(self, eng, key):
                eng.wait_ge(self.filled, self.ids[key][0] + 1)
                return bank[self.ids[key][1]]

            def out(self, key):
                return moved[self.ids[key][1]]

            def wait_out(self, eng, key):
                eng.wait_ge(moved[self.ids[key][1]], self.ids[key][2])

        def view(v, dims):
            if len(dims) == 2:
                return v.rearrange("p (a b) -> p a b", a=dims[0])
            if len(dims) == 3:
                return v.rearrange("p (a b c) -> p a b c", a=dims[0], b=dims[1])
            return v

        def sb(name, *dims, kind=F32):
            n = int(np.prod(dims))
            return view(ctx.enter_context(nc.sbuf_tensor(name, [P, n], kind))[:, :], dims)

        def sb_both(name, *dims):
            with nc.sbuf_tensor(name, [P, int(np.prod(dims))], F32) as plain:
                pass
            return view(plain[:, :], dims), sb(name + "_low", *dims, kind=F32R)

        w_raw, w_lo = sb_both("weights", RAW, CHUNK_F)
        w_hi = sb("weights_high", HI, CHUNK_F, kind=F32R)
        consts = sb("consts", MIX_COL)
        params = sb("params", NPARAM)
        nparams = sb("nparams", NCOLS)
        wf_hi = sb("w_f_high", 64, kind=F32R)
        wf_lo = sb("w_f_low", 64, kind=F32R)
        xres = sb("xres", KD, T)
        h_raw, h_lo = sb_both("h", KD, T)
        h_hi = sb("h_high", KD, T, kind=F32R)
        sq = sb("sq", 2, T)
        acc = sb("acc", T)
        rms = sb("rms", T)
        mod = sb("mod", 24)
        gmod = sb("gmod", 8)
        gmix = sb("gmix", 8)
        small = sb("small", 64)
        dq8 = sb("dq8", 2)
        masks = sb("masks", 3, P, kind=BF16)
        with nc.sbuf_tensor("arena", [P, ARENA], F32) as arena:
            pass

        def at(a, *dims):
            n = int(np.prod(dims))
            assert a + n <= ARENA, (a, n)
            return view(arena[:, a:a + n], dims)

        def at_r(name, a, *dims):
            n = int(np.prod(dims))
            assert a + n <= ARENA, (a, n)
            with ExitStack() as held:
                if a:
                    held.enter_context(nc.sbuf_tensor(name + "_below", [P, a], F32))
                part = held.enter_context(nc.sbuf_tensor(name, [P, n], F32R))
            return view(part[:, :], dims)

        def par(name, j=0, n=1):
            a = PARAM_COLS[name][0] + j
            return params[:, a:a + n]

        def npar(name, j=0):
            a = PARAM_COLS[name][0] + j
            return nparams[:, a:a + 1]

        def con(name, *dims):
            a, n = CONST_COLS[name]
            if a >= MIX_COL:
                v = at(MIX_AT + a - MIX_COL, n)
            else:
                v = consts[:, a:a + n]
            return view(v, dims)

        ident, ones_m, blk = con("ident"), con("ones"), con("blk")

        def ones(n, rows=P):
            return ones_m[0:rows, 0:1].broadcast_to([rows, n])

        ada_w = at(0, ADA, 2, KD * 256).rearrange("p i c (k n) -> p i c k n", k=KD)
        qa, ka, va = at(0, 4, T), at(2048, 4, T), at(4096, 4, T)
        qb, kb, vb = at(6144, 4, T), at(8192, 4, T), at(10240, 4, T)
        W1 = 17920
        gated_raw = at(12288, 8, T)
        gated = {"a": gated_raw[:, 0:4, :], "b": gated_raw[:, 4:8, :]}
        gated_lo, gated_hi = at_r("gated_low", 12288, 8, T), \
            [v[:, m, :] for v in (at_r("gated_high_a", W1 + 3072, 4, T), at_r("gated_high_b", 6144, 4, T))
             for m in range(4)]
        gates = [at(512 * m if m < 12 else 10240 + 512 * (m - 12), T) for m in range(16)]
        merged_raw, merged_lo = at(16384, 8, T), at_r("merged_low", 16384, 8, T)
        merged_hi = [v[:, m, :] for v in (at_r("merged_high_a", 8192, 4, T), at_r("merged_high_b", W1 + 3072, 4, T))
                     for m in range(4)]
        nF = at(16384, T)
        nF_bc = at(16896, 2, T)
        ebuf, spb, wbuf, ptb = at(W1, 3, T), at(W1 + 1536, 2, T), at(W1 + 2560, WBUF, T), at(W1 + 5120, 3, T)
        z_gate = at(16896, 2, T)
        negb, expb = at(W1, 3, T), at(W1 + 1536, 3, T)
        zm = at(0, 8, T)
        POOL_AT = 4096
        pool_u = at(POOL_AT, 2, PAD + T)
        POOL_W = PAD + T
        ycat03 = at(5152, 4, T)
        dqk = xres
        qk_sq, qk_rinv = sq, [acc, rms]
        zscale, rms2 = sq[:, 0, :], sq[:, 1, :]
        dist = zm[:, 1::2, :]
        dv = [zm[:, 0, :], zm[:, 2, :], zm[:, 4, :], at(POOL_AT + 512, T)]
        W2 = 13344
        dneg, dexp, dpt = at(W2, 4, T), at(W2 + 2048, 6, T), at(W2 + 5120, 3, T)
        dsq, drinv = at(W2 + 6656, 3, T), at(W2 + 8192, 2, T)
        R0 = 7200
        kvec, avec, decay, rdec, kdec, bdec, adec, rst, bonus, gout = (at(R0 + 512 * i, T) for i in range(10))
        tA, tB = at(R0 + 5120, T), at(R0 + 5632, T)
        vnat, bnat, knat, anat = (at(R0 + 6144 + 512 * i, 4, P) for i in range(4))
        MAT = R0 + 8192
        Am, AmT, Tm, Wm, Om, OmT = ([at(MAT + 1024 * i + 512 * hh, 4, P) for hh in range(2)] for i in range(6))
        AakT, ArbT, ArkT = Am, AmT, Om
        U0 = at(POOL_AT, 2, 4, HEAD)
        Mt, H0 = view(kvec, (NCH, CHUNK)), view(avec, (NCH, CHUNK))
        Qm = view(at(R0 + 6144 + 512 * 3, 512), (2, 4, HEAD))
        X1, St = view(decay, (2, 4, HEAD)), view(decay, (NCH, CHUNK))
        zraw = at(R0, 3, T + 1)
        kx, vx = at(5152, 8, MEM), at(0, 2, D)
        memn_raw, memn_lo = at(7200, 8, MEM), at_r("memory_low", 7200, 8, MEM)
        memn_hi = at_r("memory_high", 9248, 8, MEM)
        xk_sq, xk_rinv = at(11296, 8, MEM), at(13344, 4, MEM)
        qx = at(17440, 8, T)
        ox_raw = [at(2048, 4, T), at(7200, 4, T)]
        ox_lo = [at_r("xa_low_a", 2048, 4, T), at_r("xa_low_b", 7200, 4, T)]
        ox_hi = at_r("xa_high", 11296, 8, T)
        W3 = 21536
        xneg, xexp, xpt = at(W3, 3, MEM), at(W3 + 768, 3, MEM), at(W3 + 1536, 3, MEM)
        xsq, xrinv = at(13344, 4, T), at(15392, 2, T)
        gact_raw, gact_lo, gact_hi = at(0, KF, T), at_r("gact_low", 0, KF, T), \
            at_r("gact_high", KF * T, KF, T)
        conv_in = at(2 * KF * T, 3, T + 2)

        bank = [ctx.enter_context(nc.psum_tensor(f"bank{b}", [P, T], F32))[:, :] for b in range(8)]
        moved = [sem(f"bank{b}_moved") for b in range(8)]
        tiles = [0] * 8
        M = Ring("main", [0, 1, 2, 3])
        F = Ring("side", [3])
        TR = Ring("turn", [4, 5])
        PV = Ring("mix", [6, 7])

        loaded = [sem(f"weights{s}_loaded") for s in range(RAW)]
        used = [sem(f"weights{s}_used") for s in range(RAW)]
        chunk_end = []

        block = ctx.enter_context(nc.Block())

        def rwkv_pe(pe, j, mm, turn, fill, level_done, state_done):
            lora, g2 = par("lora", P * j, P), par("g2", P * j, P)
            if j == 1:
                pe.wait_ge(sem("rwkv_out"), 1)
            o = M.take(pe, ("rw", j))
            mm(o, lora[0:64, :], zm[0:64, 6, :], True, True, M.filled)
            o = M.take(pe, ("ra", j))
            mm(o, lora[64:128, :], zm[64:128, 6, :], True, True, M.filled)
            o = M.take(pe, ("rg", j))
            mm(o, g2, zm[:, 7, :], True, True, M.filled)
            fill(0)
            pe.wait_ge(sem("kk_squares"), j + 1)
            o = M.take(pe, ("kk", j))
            mm(o, blk, tA, True, True, M.filled)
            fill(1)
            pe.wait_ge(sem("rk_ready"), j + 1)
            o = M.take(pe, ("bonus", j))
            mm(o, blk, rst, True, True, M.filled)
            fill(2)
            for i, src in enumerate((zm[:, 4 + j, :], kdec, bdec, adec)):
                pe.wait_ge(sem("decayed"), 4 * j + 4)
                o = TR.take(pe, ("nat", j, i))
                for c in range(NB):
                    turn(o[:, P * c:P * (c + 1)], src[:, P * c:P * (c + 1)], TR.filled if c == NB - 1 else None)

            def products(name, lhs, rhs):
                for hh in range(2):
                    lo = HEAD * hh
                    o = M.take(pe, (name, j, hh))
                    for c in range(NB):
                        cols = slice(P * c, P * (c + 1))
                        mm(o[:, cols], lhs[lo:lo + HEAD, cols], rhs[lo:lo + HEAD, cols], True, True,
                           M.filled if c == NB - 1 else None)

            def square(name, hh, lhs, rhs):
                o = M.take(pe, name)
                for c in range(NB):
                    mm(o[:, P * c:P * (c + 1)], lhs[hh][:, c, :], rhs[hh][:, c, :], True, True,
                       M.filled if c == NB - 1 else None)

            products("A", adec, bdec)
            products("AT", bdec, adec)
            for lv in range(1, 6):
                for hh in range(2):
                    pe.wait_ge(sem("corner"), 2 * (5 * j + lv - 1) + hh + 1)
                    if lv == 1:
                        pe.wait_ge(sem("inverse"), 2 * j + hh + 1)
                    else:
                        M.wait_out(pe, ("dW", j, lv - 1, hh))
                    square(("ZT", j, lv, hh), hh, Om, Wm)
                    o = TR.take(pe, ("T", j, lv, hh))
                    for c in range(NB):
                        turn(o[:, P * c:P * (c + 1)], Wm[hh][:, c, :], TR.filled if c == NB - 1 else None)
                for hh in range(2):
                    M.wait_out(pe, ("ZT", j, lv, hh))
                    TR.wait_out(pe, ("T", j, lv, hh))
                    square(("dW", j, lv, hh), hh, Tm, OmT)
                level_done(lv)
            products("Aak", kdec, adec)
            products("Arb", bdec, rdec)
            products("Ark", kdec, rdec)
            for i in range(4):
                TR.wait_out(pe, ("nat", j, i))
            o = M.take(pe, ("X1", j))
            for hh in range(2):
                M.wait_out(pe, ("Aak", j, hh))
                for c in range(NB):
                    mm(o[:, HEAD * (NB * hh + c):HEAD * (NB * hh + c + 1)], AakT[hh][:, c, :],
                       vnat[:, c, HEAD * hh:HEAD * (hh + 1)], True, True, M.filled if hh and c == NB - 1 else None)
            for hh in range(2):
                M.wait_out(pe, ("dW", j, 5, hh))
            o = M.take(pe, ("Q", j))
            for hh in range(2):
                for c in range(NB):
                    mm(o[:, HEAD * (NB * hh + c):HEAD * (NB * hh + c + 1)], Wm[hh][:, c, :],
                       anat[:, c, HEAD * hh:HEAD * (hh + 1)], True, True, M.filled if hh and c == NB - 1 else None)
            M.wait_out(pe, ("X1", j))
            o = M.take(pe, ("U0", j))
            for hh in range(2):
                for c in range(NB):
                    mm(o[:, HEAD * (NB * hh + c):HEAD * (NB * hh + c + 1)], Wm[hh][:, c, :],
                       X1[:, hh, c, :], True, True, M.filled if hh and c == NB - 1 else None)
            M.wait_out(pe, ("Q", j))
            for odd in range(2):
                rows = slice(CHUNK * odd, CHUNK * (odd + 1))
                o = M.take(pe, ("Mt", j, odd))
                for c in range(NB):
                    for hh in range(2):
                        cols = slice(HEAD * hh, HEAD * (hh + 1))
                        mm(o[cols, CHUNK * c:CHUNK * (c + 1)], Qm[rows, hh, c, :], bnat[rows, c, cols],
                           True, True, M.filled if (c == NB - 1 and hh) else None)
            M.wait_out(pe, ("U0", j))
            for odd in range(2):
                rows = slice(CHUNK * odd, CHUNK * (odd + 1))
                o = M.take(pe, ("H0", j, odd))
                for c in range(NB):
                    for hh in range(2):
                        cols = slice(HEAD * hh, HEAD * (hh + 1))
                        out_ = o[cols, CHUNK * c:CHUNK * (c + 1)]
                        mm(out_, bnat[rows, c, cols], U0[rows, hh, c, :], True, False)
                        mm(out_, knat[rows, c, cols], vnat[rows, c, cols], False, True,
                           M.filled if (c == NB - 1 and hh) else None)
            for hh in range(2):
                M.wait_out(pe, ("Arb", j, hh))
                M.wait_out(pe, ("Ark", j, hh))
            o = M.take(pe, ("R", j))
            for hh in range(2):
                rows = slice(HEAD * hh, HEAD * (hh + 1))
                for c in range(NB):
                    mm(o[rows, P * c:P * (c + 1)], Qm[:, hh, c, :], ArbT[hh][:, c, :], True, True,
                       M.filled if hh and c == NB - 1 else None)
            y = PV.take(pe, ("yr", j))
            for hh in range(2):
                rows = slice(HEAD * hh, HEAD * (hh + 1))
                for c in range(NB):
                    mm(y[rows, P * c:P * (c + 1)], U0[:, hh, c, :], ArbT[hh][:, c, :], c == 0, False, skip=True)
                    mm(y[rows, P * c:P * (c + 1)], vnat[:, c, rows], ArkT[hh][:, c, :], False, False, skip=True)
            for odd in range(2):
                M.wait_out(pe, ("Mt", j, odd))
            M.wait_out(pe, ("R", j))
            for c in range(1, NCH):
                if c == 1:
                    pe.wait_ge(sem("state"), j + 1)
                else:
                    TR.wait_out(pe, ("S", j, c - 1))
                if c < NCH - 1:
                    o = TR.take(pe, ("S", j, c))
                    for hh in range(2):
                        rows = slice(HEAD * hh, HEAD * (hh + 1))
                        mm(o[rows, 0:CHUNK], Mt[rows, c, :], St[rows, c, :], True, True, TR.filled if hh else None)
                for hh in range(2):
                    rows = slice(HEAD * hh, HEAD * (hh + 1))
                    mm(y[rows, CHUNK * c:CHUNK * (c + 1)], St[rows, c, :], rst[rows, CHUNK * c:CHUNK * (c + 1)],
                       False, c == NCH - 1, PV.filled if (c == NCH - 1 and hh) else None, skip=True)
                state_done(c)

        def rwkv_norm_pe(pe, j, mm, part):
            if part == 0:
                PV.wait_out(pe, ("yr", j))
                o = M.take(pe, ("ymean", j))
                mm(o, blk, tA, True, True, M.filled)
            else:
                pe.wait_ge(sem("ysq_ready"), j + 1)
                o = M.take(pe, ("yvar", j))
                mm(o, blk, tB, True, True, M.filled)

        @block.tensor
        def _(pe):
            free_slot = []

            def mm(o, lhsT, rhs, start, stop, signal=None, skip=False):
                ins = nc.tensor.matmul(o, lhsT, rhs, start=start, stop=stop, skip_group_check=skip)
                if signal is not None:
                    ins.then_inc(signal, 1)
                elif free_slot:
                    ins.then_inc(used[free_slot.pop()], 1)

            def turn(o, i, signal=None):
                ins = nc.tensor.transpose(o, i, ident)
                if signal is not None:
                    ins.then_inc(signal, 1)

            def next_chunk(k, cols):
                c = len(chunk_end)
                pe.wait_ge(sem("weights_split"), c + 1)
                chunk_end.append(("used", c % RAW, c // RAW + 1))
                return c % RAW, [v[:, 0:k * cols].rearrange("p (k n) -> p k n", k=k)
                                 for v in (w_hi[:, c % HI, :], w_lo[:, c % RAW, :])]

            def mm3(o, left, right, first, last, signal=None):
                mm(o, left[0], right[0], first, False)
                mm(o, left[0], right[1], False, False)
                mm(o, left[1], right[0], False, last, signal)

            chunk = [None]

            def project(key, tiles, nk, rhs, n, ready=None, cols=256, after=None, first=0):
                for m in range(first, first + tiles):
                    per = cols // P
                    if m % per == 0:
                        chunk[0] = next_chunk(nk, cols)
                    slot, w = chunk[0]
                    o = M.take(pe, (key, m))
                    for k in range(nk):
                        if m == first and ready is not None:
                            ready(k)
                        mm3(o[:, 0:n], [p_[:, k, P * (m % per):P * (m % per + 1)] for p_ in w], rhs(k),
                            k == 0, k == nk - 1, M.filled if k == nk - 1 else None)
                    if m % per == per - 1:
                        free_slot.append(slot)
                        chunk_end[-1] = (key, m)
                    if after is not None:
                        after(m)

            part_bank = [None]

            def project_part(key, m, first, last):
                if first == 0:
                    if m % 2 == 0:
                        chunk[0] = next_chunk(KD, 256)
                    part_bank[0] = F.take(pe, (key, m))
                slot, w = chunk[0]
                for k in range(first, last):
                    mm3(part_bank[0], [p_[:, k, P * (m % 2):P * (m % 2 + 1)] for p_ in w], h(k),
                        k == 0, k == KD - 1, F.filled if k == KD - 1 else None)
                if last == KD and m % 2 == 1:
                    free_slot.append(slot)
                    chunk_end[-1] = (key, m)

            def project_rows(key, first, last, lhs, blocks):
                for i in range(first, last):
                    c, b = divmod(i, blocks)
                    if b == 0:
                        chunk[0] = next_chunk(KD, 256)
                    slot, w = chunk[0]
                    o = M.take(pe, (key, c, b))
                    for k in range(KD):
                        mm3(o[:, 0:256], lhs(k, b), [p_[:, k, :] for p_ in w], k == 0, k == KD - 1,
                            M.filled if k == KD - 1 else None)
                    if b == blocks - 1:
                        free_slot.append(slot)
                        chunk_end[-1] = (key, c, b)

            def norm_sum(n, width, ring=M):
                pe.wait_ge(sem("squares_added"), KD * (n + 1))
                o = ring.take(pe, ("norm", n))
                mm(o[:, 0:width], ones_m, acc[:, 0:width], True, True, ring.filled)

            def h_ready(n):
                return lambda k: pe.wait_ge(sem("h_ready"), KD * n + k + 1)

            pe.wait_ge(sem("consts_loaded"), 16)
            pe.wait_ge(sem("params_loaded"), 16)
            norm_sum(0, T)
            pe.wait_ge(sem("lam_products"), 1)
            o = M.take(pe, "lam")
            mm(o[:, 0:2], ones_m, small[:, 0:2], True, True, M.filled)
            o = M.take(pe, "mod")

            def ada_columns(o, first, last):
                for i in range(first, last):
                    pe.wait_ge(sem("ada_sums"), i + 1)
                    for c in range(2):
                        for mi in range(2):
                            m = 2 * c + mi
                            at_ = 4 * (i - first) + m
                            mm(o[:, at_:at_ + 1], ada_w[:, i, c, 0, P * mi:P * (mi + 1)], ones_m[:, 0:1], True, True,
                               M.filled if i == last - 1 and m == 3 else None)

            ada_columns(o, 0, ADA_FIRST)

            h = lambda k: (h_hi[:, k, :], h_lo[:, k, :])
            hrow = lambda k, b: (h_hi[:, k, P * b:P * (b + 1)], h_lo[:, k, P * b:P * (b + 1)])
            project("qa", 4, KD, h, T, h_ready(0))
            o = M.take(pe, "gate")
            ada_columns(o, ADA_FIRST, ADA)
            project("ka", 4, KD, h, T)
            project_rows("va", 0, 2 * NB, hrow, NB)
            project("za", 4, KD, h, T)
            project("qb", 4, KD, h, T)
            project("kb", 4, KD, h, T)
            o = M.take(pe, "f")
            pe.wait_ge(sem("wf_split"), 1)
            wf = [v.rearrange("p (k n) -> p k n", k=KD) for v in (wf_hi, wf_lo)]
            for k in range(KD):
                mm3(o[0:HEADS, :], [v[:, k, :] for v in wf], h(k), k == 0, k == KD - 1,
                    M.filled if k == KD - 1 else None)

            def head_rows(hd):
                return HEAD * (hd % 2), HEAD * (hd % 2) + HEAD

            def transposes(key, src, blocks):
                o = TR.take(pe, key)
                for i in range(blocks):
                    turn(o[:, P * i:P * (i + 1)], src[:, P * i:P * (i + 1)], TR.filled if i == blocks - 1 else None)

            def attend(tag, q, kk, v, mask, lag, weights_done, weights, fill):
                N = HEADS * NB
                for c in range(2):
                    for b in range(NB):
                        M.wait_out(pe, ("v" + tag, c, b))
                if tag == "a":
                    pe.wait_ge(sem("masks"), 3)
                for i in range(N + lag + 2):
                    if i < N:
                        hd, b = divmod(i, NB)
                        if tag == "b" and b == 0:
                            if hd == 0:
                                pe.wait_ge(sem("nF_ready"), 1)
                                pe.wait_ge(sem("late_loaded"), 32)
                            o = M.take(pe, ("nF", hd))
                            mm(o, con("head_row", HEADS, P)[0:HEADS, hd, :], nF[0:HEADS, :], True, True, M.filled)
                        if b == 0 and hd % 2 == 0:
                            M.wait_out(pe, ("q" + tag, hd // 2))
                            M.wait_out(pe, ("k" + tag, hd // 2))
                        lo, hi = head_rows(hd)
                        o = M.take(pe, (tag, i))
                        end = P * (b + 1)
                        mm(o[:, 0:end], q[lo:hi, hd // 2, P * b:end], kk[lo:hi, hd // 2, 0:end], True, False)
                        mm(o[:, P * b:end], masks[:, 0, :], mask, False, True, M.filled)
                    n = i - lag
                    if 0 <= n < N:
                        pe.wait_ge(weights_done, n + 1)
                        transposes(("T" + tag, n), weights(n), n % NB + 1)
                    n = i - lag - 2
                    if 0 <= n < N:
                        hd, b = divmod(n, NB)
                        lo, hi = head_rows(hd)
                        TR.wait_out(pe, ("T" + tag, n))
                        if b == 0 and hd % 2 == 0:
                            y = PV.take(pe, ("y" + tag, hd // 2))
                        last = b == NB - 1 and hd % 2 == 1
                        for s in range(b + 1):
                            mm(y[lo:hi, P * b:P * (b + 1)], v[:, s, HEAD * hd:HEAD * (hd + 1)],
                               ptb[:, n % 3, P * s:P * (s + 1)], s == 0, s == b,
                               PV.filled if last and s == b else None)
                    fill(i)

            PARTS = ((0, 3), (3, 6), (6, KD))

            def fill_a(i):
                if i % 2 == 1 and i < 16:
                    project_rows("vb", i // 2, i // 2 + 1, hrow, NB)
                elif 16 <= i < 32 and i % 4 < 3:
                    project_part("zb", (i - 16) // 4, *PARTS[i % 4])
                elif i >= 32:
                    project_part("g", (i - 32) // 3, *PARTS[(i - 32) % 3])

            def fill_b(i):
                if i % 4 < 3:
                    project_part("g", 2 + i // 4, *PARTS[i % 4])

            M.use([0, 1, 2])
            attend("a", qa, ka, va, masks[:, 1, :], 4, sem("stick_w"), lambda n: wbuf[:, n % WBUF, :], fill_a)
            attend("b", qb, kb, vb, masks[:, 2, :], 2, sem("fox_w"), lambda n: expb[:, n % 3, :], fill_b)

            M.use([0, 1, 2, 3])
            project("g", 16 - SIDE_G, KD, h, T, first=SIDE_G)
            for tag, first in (("oa", 0), ("ob", 4)):
                project(tag, KD, 4, lambda k: (gated_hi[first + k], gated_lo[:, first + k, :]), T,
                        lambda k: pe.wait_ge(sem("gated_split"), first + k + 1), cols=512)
            project("wo", KD, KD, lambda k: (merged_hi[k], merged_lo[:, k, :]), T,
                    lambda k: pe.wait_ge(sem("merged"), k + 1))

            project("zr", 1, KD, h, T, h_ready(1))
            norm_sum(1, T, PV)
            project("zr", 2, KD, h, T, first=1)
            norm_sum(2, T, PV)
            project("zr", 5, KD, h, T, first=3)
            project("zp", 2, KD, h, T)
            pe.wait_ge(sem("zscale"), 1)
            o = PV.take(pe, "zcols")
            for b in range(NB):
                mm(o[:, b:b + 1], zscale[:, P * b:P * (b + 1)], ident[:, 0:1], True, True,
                   PV.filled if b == NB - 1 else None)
            project("dq", 2, KD, h, T)
            for j in range(2):
                pe.wait_ge(sem("pooled"), j + 1)
                o = M.take(pe, ("pool", j))
                mm(o, par("pool_w", P * j, P), ycat03[:, j, :], True, True, M.filled)
            project("dq", 2, KD, h, T, first=2)
            pe.wait_ge(sem("lora_in"), 2)

            def dq_sums(lv):
                for t in range(2 * lv - 2, 2 * lv):
                    if t < 8:
                        pe.wait_ge(sem("qk_squares"), t + 1)
                        o = M.take(pe, ("dn", t))
                        mm(o, blk, qk_sq[:, t % 2, :], True, True, M.filled)

            def diff_scores(i):
                hd, b = divmod(i, NB)
                end = P * (b + 1)
                if i == 0:
                    pe.wait_ge(sem("dqk_ready"), 8)
                for cp in range(2):
                    lo, hi = head_rows(cp)
                    o = M.take(pe, ("d", i, cp))
                    mm(o[:, 0:end], dqk[lo:hi, hd, P * b:end], dqk[lo:hi, 4 + hd, 0:end], True, True, M.filled)

            def early_scores(c):
                if c % 2 == 0 and c // 2 <= EARLY:
                    diff_scores(c // 2 - 1)

            rwkv_pe(pe, 0, mm, turn, lambda i: project("dq", (1, 2, 1)[i], KD, h, T, first=(4, 5, 7)[i]),
                    lambda lv: None, lambda c: None)
            for part in range(2):
                project_rows("dv", part, part + 1, hrow, NB)
                rwkv_norm_pe(pe, 0, mm, part)
            rwkv_pe(pe, 1, mm, turn, lambda i: project_rows("dv", 2 + 2 * i, 4 + 2 * i, hrow, NB), dq_sums,
                    early_scores)
            N = DIFF_HEADS * NB
            for i in range(N + 7):
                if EARLY <= i < N:
                    diff_scores(i)
                if i in (2, 4):
                    rwkv_norm_pe(pe, 1, mm, 0 if i == 2 else 1)
                n = i - 2
                if 0 <= n < N:
                    pe.wait_ge(sem("diff_w"), n + 1)
                    transposes(("Td", n), dexp[:, 2 * (n % 3), :], n % NB + 1)
                n = i - 4
                if 0 <= n < N:
                    hd, b = divmod(n, NB)
                    TR.wait_out(pe, ("Td", n))
                    if b == 0:
                        y = PV.take(pe, ("yd", hd))
                    for s in range(b + 1):
                        mm(y[:, P * b:P * (b + 1)], dv[s][:, P * hd:P * (hd + 1)], dpt[:, n % 3, P * s:P * (s + 1)],
                           s == 0, s == b, PV.filled if (b == NB - 1 and s == b) else None)
                n = i - 6
                if 0 <= n < N and n % NB == NB - 1:
                    hd = n // NB
                    pe.wait_ge(sem("osq_ready"), hd + 1)
                    o = M.take(pe, ("on", hd))
                    mm(o, ones_m, dsq[:, hd % 2, :], True, True, M.filled)
                if i == MEM_SUM:
                    norm_sum(3, MEM)
                if KX_STEP <= i < KX_STEP + KD:
                    project("kx", 1, KD, lambda k: (memn_hi[:, k, :], memn_lo[:, k, :]), MEM,
                            h_ready(2) if i == KX_STEP else None, first=i - KX_STEP)
            def key_sums(m):
                if m == 1:
                    pe.wait_ge(sem("xksq_ready"), 8)
                    for hd in range(XA_HEADS):
                        o = M.take(pe, ("kn", hd))
                        for i in range(2):
                            mm(o[:, 0:MEM], ones_m, xk_sq[:, 2 * hd + i, :], i == 0, i == 1, M.filled if i else None)

            project("wo2", KD, KD, h, T, lambda k: pe.wait_ge(sem("mixers_split"), k + 1), after=key_sums)

            def head_sum(hd):
                if 0 <= hd < XA_HEADS:
                    pe.wait_ge(sem("xqsq_ready"), 2 * hd + 2)
                    o = M.take(pe, ("qn", hd))
                    for i in range(2):
                        mm(o, ones_m, xsq[:, (2 * hd + i) % 4, :], i == 0, i == 1, M.filled if i else None)

            norm_sum(4, T)
            project_rows("vx", 0, 4 * 2, lambda k, b: [v[:, k, P * b:P * (b + 1)] for v in (memn_hi, memn_lo)], 2)
            project("xq", KD, KD, h, T, h_ready(3), after=lambda m: head_sum(m // 2 - 1) if m % 2 == 0 else None)
            head_sum(XA_HEADS - 1)
            pe.wait_ge(sem("kx_ready"), 8)
            for c in range(4):
                for b in range(2):
                    M.wait_out(pe, ("vx", c, b))
            N = XA_HEADS * NB
            for i in range(N + 4):
                if i < N:
                    hd, b = divmod(i, NB)
                    if b == 0:
                        pe.wait_ge(sem("qx_ready"), 2 * hd + 2)
                    o = M.take(pe, ("x", i))
                    for k in range(2):
                        mm(o[:, 0:MEM], qx[:, 2 * hd + k, P * b:P * (b + 1)], kx[:, 2 * hd + k, :], k == 0, k == 1,
                           M.filled if k else None)
                n = i - 2
                if 0 <= n < N:
                    pe.wait_ge(sem("xa_w"), n + 1)
                    transposes(("Tx", n), xexp[:, n % 3, :], 2)
                n = i - 4
                if 0 <= n < N:
                    hd, b = divmod(n, NB)
                    TR.wait_out(pe, ("Tx", n))
                    o = PV.take(pe, ("yx", n))
                    for j in range(2):
                        for s in range(2):
                            mm(o[:, P * j:P * (j + 1)], vx[:, s, 256 * hd + P * j:256 * hd + P * (j + 1)],
                               xpt[:, n % 3, P * s:P * (s + 1)], s == 0, s == 1, PV.filled if j and s else None)
            project("xo", KD, KD, lambda k: (ox_hi[:, k, :], ox_lo[k // 4][:, k % 4, :]), T,
                    lambda k: pe.wait_ge(sem("xa_split"), k + 1))

            for j in range(KF // 2):
                for half in range(2):
                    slot, w = next_chunk(KD, 256)
                    for mi in range(2):
                        o = M.take(pe, ("up", 2 * j + mi, half))
                        for k in range(KD):
                            if j == 0 and half == 0 and mi == 0:
                                h_ready(4)(k)
                            mm3(o, [p_[:, k, P * mi:P * (mi + 1)] for p_ in w], h(k), k == 0, k == KD - 1,
                                M.filled if k == KD - 1 else None)
                        if j == 0 and half == 0 and mi == 0:
                            norm_sum(5, T, PV)
                    free_slot.append(slot)
                    chunk_end[-1] = ("up", 2 * j + 1, half)
            for m in range(KD):
                o = M.take(pe, ("down", m))
                for part in range(2):
                    slot, w = next_chunk(DOWN_K, P)
                    for k in range(DOWN_K):
                        kf = DOWN_K * part + k
                        if m == 0:
                            pe.wait_ge(sem("gact_split"), kf + 1)
                        mm3(o, [p_[:, k, :] for p_ in w], (gact_hi[:, kf, :], gact_lo[:, kf, :]),
                            kf == 0, kf == KF - 1, M.filled if kf == KF - 1 else None)
                    free_slot.append(slot)
            assert len(chunk_end) == STREAM + DOWN

        @block.scalar
        def _(act):
            links = [0]

            def link(ins):
                links[0] += 1
                ins.then_inc(sem("act_link"), 1)
                act.wait_ge(sem("act_link"), links[0])

            chunks = [0]

            def full(key):
                return (F if key in F.ids else M).full(act, key)

            def split_weights(part=0, parts=1):
                c = chunks[0]
                if part == parts - 1:
                    chunks[0] += 1
                if c >= len(chunk_end):
                    return
                n = (CHUNK_F if c < STREAM else DOWN_K * P) // parts
                cols = slice(n * part, n * (part + 1))
                if part:
                    ins = nc.scalar.activation(w_hi[:, c % HI, cols], w_raw[:, c % RAW, cols], ACT.Copy)
                    if part == parts - 1:
                        ins.then_inc(sem("weights_hi"), 1)
                    return
                act.wait_ge(loaded[c % RAW], 16 * (c // RAW + 1))
                if c >= HI:
                    end = chunk_end[c - HI]
                    if end[0] == "used":
                        act.wait_ge(used[end[1]], end[2])
                    else:
                        full(end)
                ins = nc.scalar.activation(w_hi[:, c % HI, cols], w_raw[:, c % RAW, cols], ACT.Copy)
                if parts == 1:
                    ins.then_inc(sem("weights_hi"), 1)

            def split_after(m):
                if m % 2 == 1:
                    split_weights()

            def high(hi, raw, done):
                nc.scalar.activation(hi, raw, ACT.Copy).then_inc(done, 1)

            def high_h(n):
                for k in range(KD):
                    act.wait_ge(sem("h_raw"), KD * n + k + 1)
                    high(h_hi[:, k, :], h_raw[:, k, :], sem("h_hi"))

            def squares(n, src, width, ready, after=None, tiles_=range(KD)):
                for k in tiles_:
                    i = KD * n + k
                    if k and after is not None:
                        after(k - 1)
                    ready(k)
                    if i >= 2:
                        act.wait_ge(sem("squares_added"), i - 1)
                    nc.scalar.activation(sq[:, i % 2, 0:width], src[:, k, 0:width], ACT.Square)\
                        .then_inc(sem("squares"), 1)
                if after is not None:
                    after(KD - 1)

            def inverse_rms(n, width, ring=M, to=rms):
                o = ring.full(act, ("norm", n))
                nc.scalar.activation(to[:, 0:width], o[:, 0:width], ACT.Ln, scale=1.0 / D, bias=con("eps"))\
                    .then_inc(ring.out(("norm", n)), 1)
                ring.wait_out(act, ("norm", n))
                nc.scalar.activation(to[:, 0:width], to[:, 0:width], ACT.Exp, scale=-0.5).then_inc(sem("rms_ready"), 1)

            def move(key, dst, src=None, ring_=M, scale=None):
                o = ring_.full(act, key)
                s_ = o if src is None else src(o)
                if scale is None:
                    nc.scalar.activation(dst, s_, ACT.Copy).then_inc(ring_.out(key), 1)
                elif isinstance(scale, float):
                    nc.scalar.activation(dst, s_, ACT.Copy, scale=scale).then_inc(ring_.out(key), 1)
                else:
                    nc.scalar.activation(dst, s_, ACT.Identity, scale=scale).then_inc(ring_.out(key), 1)

            nc.scalar.preload_act_table_set("natural_log_exp_and_others")
            act.wait_ge(sem("x_loaded"), 16)
            squares(0, xres, T, lambda k: None)
            act.wait_ge(sem("consts_loaded"), 16)
            inverse_rms(0, T)
            o = M.full(act, "lam")
            nc.scalar.activation(small[:, 2:4], o[:, 0:2], ACT.Exp).then_inc(M.out("lam"), 1)

            act.wait_ge(sem("negated"), 1)
            high(wf_hi, par("w_f", 0, 64), sem("wf_hi"))
            for _ in range(HI):
                split_weights()
            for k in range(KD):
                act.wait_ge(sem("h_raw"), k + 1)
                nc.scalar.activation(h_hi[:, k, :], h_raw[:, k, :], ACT.Identity, bias=mod[:, k:k + 1])\
                    .then_inc(sem("h_hi"), 1)

            def inverse(v, bias=0.0):
                link(nc.scalar.activation(v, v, ACT.Ln, bias=1.0))
                return nc.scalar.activation(v, v, ACT.Exp, scale=-1.0, bias=bias)

            def silu(tag, m):
                ring, e = (F if tag == "b" else M), z_gate[:, m % 2, :]
                if tag == "b" or m >= 2:
                    act.wait_ge(sem("silu"), 4 * (tag == "b") + m - 1)
                move(("z" + tag, m), gated[tag][:, m, :], None, ring)
                ring.wait_out(act, ("z" + tag, m))
                link(nc.scalar.activation(e, gated[tag][:, m, :], ACT.Exp, scale=-1.0))
                inverse(e).then_inc(sem("silu_gate"), 1)
                split_after(m)

            def rows_out(key, dst, first=0, last=2 * NB):
                for i in range(first, last):
                    c, b = divmod(i, NB)
                    move((key, c, b), dst[:, b, 256 * c:256 * (c + 1)], lambda o: o[:, 0:256])
                    if b == NB - 1:
                        split_weights()

            for m in range(4):
                move(("qa", m), qa[:, m, :], scale=HEAD ** -0.5)
                split_after(m)
            for _ in range(2):
                split_weights()
            rows_out("va", va)
            for m in range(4):
                silu("a", m)
            for m in range(4):
                move(("qb", m), qb[:, m, :], scale=HEAD ** -0.5)
                split_after(m)
            for _ in range(2):
                split_weights()
            o = M.full(act, "f")
            fx, fa = nF_bc[0:HEADS, 0, :], nF_bc[0:HEADS, 1, :]
            nc.scalar.activation(fx, o[0:HEADS, :], ACT.Identity, scale=-1.0, bias=npar("b_forget")[0:HEADS, :])\
                .then_inc(M.out("f"), 1)
            M.wait_out(act, "f")
            link(nc.scalar.activation(fa, fx, ACT.Abs))
            link(nc.scalar.activation(fa, fa, ACT.Exp, scale=-1.0))
            nc.scalar.activation(fa, fa, ACT.Ln, bias=1.0).then_inc(sem("f_ln"), 1)

            N = HEADS * NB
            for i in range(N + 2):
                if i % 4 == 3 and 16 < i < N:
                    silu("b", (i - 16) // 4)
                if i < N:
                    end = P * (i % NB + 1)
                    e = ebuf[:, i % 3, 0:end]
                    o = M.full(act, ("a", i))
                    if i >= 3:
                        act.wait_ge(sem("stick_sp"), i - 2)
                    link(nc.scalar.activation(e, o[:, 0:end], ACT.Abs))
                    link(nc.scalar.activation(e, e, ACT.Exp, scale=-1.0))
                    nc.scalar.activation(e, e, ACT.Ln, bias=1.0).then_inc(sem("stick_ln"), 1)
                n = i - 2
                if 0 <= n < N:
                    end = P * (n % NB + 1)
                    M.wait_out(act, ("a", n))
                    w = wbuf[:, n % WBUF, 0:end]
                    nc.scalar.activation(w, w, ACT.Exp).then_inc(sem("stick_w"), 1)
                if i % 2 == 0 and 2 <= i <= 16:
                    rows_out("vb", vb, i // 2 - 1, i // 2)

            def gated_high(m):
                PV.wait_out(act, ("yb" if m >= 4 else "ya", m % 4))
                high(gated_hi[m], gated_raw[:, m, :], sem("gated_hi"))

            def gate_out(m):
                o = full(("g", m))
                nc.scalar.activation(gates[m], o, ACT.Exp, scale=-1.0, bias=npar("b_gate", m))\
                    .then_inc((F if m < SIDE_G else M).out(("g", m)), 1)

            def gate_inverse(m):
                (F if m < SIDE_G else M).wait_out(act, ("g", m))
                inverse(gates[m]).then_inc(sem("gates"), 1)
                if m >= SIDE_G - 2:
                    split_after(m)

            for i in range(N + 3):
                if i == 0:
                    gate_out(0)
                if i == 1:
                    gate_out(1)
                    gate_inverse(0)
                    gate_inverse(1)
                if i % 4 == 3 and i < N:
                    gate_out(2 + i // 4)
                if i < N:
                    hd, b = divmod(i, NB)
                    end = P * (b + 1)
                    if b == 0:
                        if hd >= 2:
                            M.wait_out(act, ("b", NB * (hd - 1) - 1))
                        else:
                            act.wait_ge(sem("nF_ready"), 1)
                        move(("nF", hd), nF_bc[:, hd % 2, :])
                    M.wait_out(act, ("b", i))
                    if i >= 3:
                        TR.full(act, ("Tb", i - 3))
                        act.wait_ge(sem("fox_w"), i - 2)
                    nc.scalar.activation(expb[:, i % 3, 0:end], negb[:, i % 3, 0:end], ACT.Exp, scale=-1.0,
                                         bias=small[:, 8 + i % 3:9 + i % 3],
                                         accum_out=small[:, 11 + i % 3:12 + i % 3]).then_inc(sem("fox_exp"), 1)
                n = i - 2
                if 0 <= n < N:
                    end = P * (n % NB + 1)
                    move(("Tb", n), ptb[:, n % 3, 0:end], lambda o: o[:, 0:end], TR)
                if i % 4 == 3 and i < N:
                    gate_inverse(2 + i // 4)
                if i % 8 in (1, 2) and i < N:
                    split_weights((1, 2).index(i % 8), 2)
                if i % 8 == 5 and i < N:
                    gated_high(i // 8)

            gate_out(SIDE_G - 1)
            gate_inverse(SIDE_G - 1)
            for m in range(4):
                gated_high(4 + m)
            for m in range(SIDE_G, 16):
                gate_out(m)
                gate_inverse(m)
            for _ in range(2):
                split_weights()
            for m in range(KD):
                act.wait_ge(sem("merged_raw"), m + 1)
                high(merged_hi[m], merged_raw[:, m, :], sem("merged_hi"))
                if m % 4 == 3:
                    split_weights()

            def between_blocks(k):
                split_after(k)
                act.wait_ge(sem("h_raw"), KD + k + 1)
                high(h_hi[:, k, :], h_raw[:, k, :], sem("h_hi"))

            squares(1, xres, T, lambda k: M.wait_out(act, ("wo", k)), between_blocks)
            act.dma_start(at(MIX_AT, DIFF_COL - MIX_COL), consts_in[:, MIX_COL:DIFF_COL]).then_inc(sem("mix_loaded"), 16)
            inverse_rms(1, T, PV)
            squares(2, xres, T, lambda k: act.wait_ge(sem("x2_ready"), k + 1))
            act.dma_start(x2_kept, xres).then_inc(sem("x2_stored"), 16)
            split_weights()
            inverse_rms(2, T, PV, rms2)

            for _ in range(4):
                split_weights()
            PV.full(act, "zcols")
            nc.scalar.activation(small[:, 44:48], bank[PV.ids["zcols"][1]][:, 0:NB], ACT.Copy)\
                .then_inc(PV.out("zcols"), 1)
            act.wait_ge(sem("zm"), 8)
            link(nc.scalar.activation(tA[0:64, :], zm[0:64, 6, :], ACT.Exp, scale=2.0))
            inverse(tA[0:64, :]).then_inc(sem("lora_exp"), 1)
            link(nc.scalar.activation(zm[:, 7, :], zm[:, 7, :], ACT.Exp, scale=-1.0))
            inverse(zm[:, 7, :]).then_inc(sem("lora_in"), 1)

            def dq_norm(lv):
                pair = (2 * lv - 2, 2 * lv - 1)
                for t in pair:
                    if t >= 2:
                        M.full(act, ("dn", t - 2))
                    M.wait_out(act, ("dq", t))
                    nc.scalar.activation(qk_sq[:, t % 2, :], dqk[:, t, :], ACT.Square).then_inc(sem("qk_squares"), 1)
                for t in pair:
                    o = M.full(act, ("dn", t))
                    if t >= 2:
                        act.wait_ge(sem("dqk_ready"), t - 1)
                    nc.scalar.activation(qk_rinv[t % 2], o, ACT.Ln, bias=con("eps")).then_inc(M.out(("dn", t)), 1)
                    M.wait_out(act, ("dn", t))
                    nc.scalar.activation(qk_rinv[t % 2], qk_rinv[t % 2], ACT.Exp, scale=-0.5).then_inc(sem("qk_inverse"), 1)

            def dq_out(first, last):
                for t in range(first, last):
                    split_after(t)

            def rwkv_square(j):
                M.wait_out(act, ("ymean", j))
                nc.scalar.activation(tB, tA, ACT.Square).then_inc(sem("ysq_ready"), 1)

            def rwkv_inverse(j):
                o = M.full(act, ("yvar", j))
                nc.scalar.activation(tB, o, ACT.Ln, bias=con("gn_eps")).then_inc(M.out(("yvar", j)), 1)
                M.wait_out(act, ("yvar", j))
                nc.scalar.activation(tB, tB, ACT.Exp, scale=-0.5).then_inc(sem("y_rstd"), 1)

            def dv_out(first, last):
                for i in range(first, last):
                    c, b = divmod(i, NB)
                    move(("dv", c, b), dv[b][:, 256 * c:256 * (c + 1)], lambda o: o[:, 0:256], scale=small[:, 44 + b:45 + b])
                    if b == NB - 1:
                        split_weights()

            def diff_exp(i):
                end = P * (i % NB + 1)
                if i >= 3:
                    TR.full(act, ("Td", i - 3))
                for cp in range(2):
                    M.wait_out(act, ("d", i, cp))
                    c = 2 * (i % 2) + cp
                    nc.scalar.activation(dexp[:, 2 * (i % 3) + cp, 0:end], dneg[:, c, 0:end], ACT.Exp, scale=-1.0,
                                         bias=small[:, 32 + c:33 + c], accum_out=small[:, 36 + c:37 + c])\
                        .then_inc(sem("diff_exp"), 1)

            PV.wait_out(act, "zcols")
            dq_out(0, 2)
            for j in range(2):
                move(("pool", j), ycat03[:, j, :], scale=par("pool_scale", j))
            dq_out(2, 4)
            for j in range(2):
                for key, dst, bias, power in (("rw", decay, npar("w0", j), con("neg_half")),
                                              ("ra", avec, npar("a0", j), 0.0)):
                    o = M.full(act, (key, j))
                    nc.scalar.activation(dst, o, ACT.Exp, scale=-1.0, bias=bias).then_inc(M.out((key, j)), 1)
                    M.wait_out(act, (key, j))
                    inverse(dst, power).then_inc(sem("rates"), 1)
                move(("rg", j), gout)
                act.wait_ge(sem("kk0"), j + 1)
                nc.scalar.activation(tA, adec, ACT.Square).then_inc(sem("kk_squares"), 1)
                if j == 0:
                    dq_out(4, 5)
                else:
                    dv_out(2, 4)
                act.wait_ge(sem("kk_floor"), j + 1)
                link(nc.scalar.activation(tB, tB, ACT.Ln))
                nc.scalar.activation(tB, tB, ACT.Exp, scale=-0.5).then_inc(sem("kk_norm"), 1)
                act.wait_ge(sem("L_ready"), 2 * j + 2)
                nc.scalar.activation(rdec, tA, ACT.Exp).then_inc(sem("exps"), 1)
                nc.scalar.activation(kdec, tA, ACT.Exp, scale=-1.0).then_inc(sem("exps"), 1)
                nc.scalar.activation(decay, decay, ACT.Exp).then_inc(sem("exps"), 1)
                nc.scalar.activation(small[:, 24:32], tA[:, CHUNK - 1::CHUNK], ACT.Exp).then_inc(sem("exps"), 1)
                if j == 0:
                    dq_out(5, 8)
                else:
                    dv_out(4, 8)
                for i, dst in enumerate((vnat, knat, bnat, anat)):
                    move(("nat", j, i), dst, lambda o: o.rearrange("p (a b) -> p a b", a=4), TR)
                for lv in range(1, 6):
                    for hh in range(2):
                        move(("T", j, lv, hh), Tm[hh], lambda o: o.rearrange("p (a b) -> p a b", a=4), TR)
                    if j == 1 and lv < 5:
                        dq_norm(lv)
                if j == 1:
                    act.dma_start(dist, consts_in[:, DIFF_COL:].rearrange("p (a b) -> p a b", a=DIFF_HEADS))\
                        .then_inc(sem("dist_loaded"), 16)
                flat = lambda v: v.rearrange("p a b c -> p (a b c)")
                move(("X1", j), flat(X1))
                move(("U0", j), flat(U0))
                if j == 1:
                    for i in range(EARLY):
                        diff_exp(i)
                move(("yr", j), tA, None, PV)
                if j == 0:
                    dv_out(0, 1)
                    rwkv_square(0)
                    dv_out(1, 2)
                    rwkv_inverse(0)

            N = DIFF_HEADS * NB
            for i in range(N + 8):
                if EARLY <= i < N:
                    diff_exp(i)
                if i == 2:
                    rwkv_square(1)
                if i == 4:
                    rwkv_inverse(1)
                if 6 <= i < 10:
                    if i == 6:
                        act.wait_ge(sem("rwkv_out"), 2)
                    high(h_hi[:, i - 6, :], ycat03[:, i - 6, :], sem("mixers_hi"))
                if i == N - 1:
                    act.dma_start(xres, x2_kept).then_inc(sem("x2_back"), 16)
                if i == 0:
                    act.dma_start(memn_raw, mem_in).then_inc(sem("mem_loaded"), 16)
                if 3 <= i < 7:
                    act.wait_ge(sem("mem_loaded"), 16)
                    squares(3, memn_raw, MEM, lambda k: None, tiles_=range(2 * (i - 3), 2 * (i - 3) + 2))
                if i == MEM_SUM + 1:
                    inverse_rms(3, MEM)
                if MEM_SUM + 2 <= i < MEM_SUM + 4:
                    for k in range(4 * (i - MEM_SUM - 2), 4 * (i - MEM_SUM - 1)):
                        act.wait_ge(sem("h_raw"), KD * 2 + k + 1)
                        high(memn_hi[:, k, :], memn_raw[:, k, :], sem("h_hi"))
                if KX_STEP < i <= KX_STEP + KD:
                    m = i - KX_STEP - 1
                    act.wait_ge(sem("mixers_split"), 4)
                    move(("kx", m), kx[:, m, :], lambda o: o[:, 0:MEM])
                    M.wait_out(act, ("kx", m))
                    nc.scalar.activation(xk_sq[:, m, :], kx[:, m, :], ACT.Square).then_inc(sem("xksq_ready"), 1)
                    split_after(m)
                n = i - 2
                if 0 <= n < N:
                    end = P * (n % NB + 1)
                    move(("Td", n), dpt[:, n % 3, 0:end], lambda o: o[:, 0:end], TR)
                n = i - 5
                if 0 <= n < N and n % NB == NB - 1:
                    hd = n // NB
                    o = PV.full(act, ("yd", hd))
                    nc.scalar.activation(dsq[:, hd % 2, :], o, ACT.Square).then_inc(sem("osq_ready"), 1)
                n = i - 6
                if 0 <= n < N and n % NB == NB - 1:
                    hd = n // NB
                    o = M.full(act, ("on", hd))
                    if hd >= 2:
                        PV.wait_out(act, ("yd", hd - 2))
                    nc.scalar.activation(drinv[:, hd % 2, :], o, ACT.Ln, scale=1.0 / P, bias=con("eps"))\
                        .then_inc(M.out(("on", hd)), 1)
                    M.wait_out(act, ("on", hd))
                    nc.scalar.activation(drinv[:, hd % 2, :], drinv[:, hd % 2, :], ACT.Exp, scale=-0.5)\
                        .then_inc(sem("oinv"), 1)
                n = i - 7
                if 0 <= n < N and n % NB == NB - 1:
                    hd = n // NB
                    PV.wait_out(act, ("yd", hd))
                    high(h_hi[:, 4 + hd, :], h_raw[:, 4 + hd, :], sem("mixers_hi"))

            def head_inverse(key, r, width, done):
                o = M.full(act, key)
                nc.scalar.activation(r, o[:, 0:width], ACT.Ln, scale=1.0 / 256, bias=con("eps")).then_inc(M.out(key), 1)
                M.wait_out(act, key)
                nc.scalar.activation(r, r, ACT.Exp, scale=-0.5).then_inc(done, 1)

            def between(k):
                split_after(k)
                if k == 1:
                    for hd in range(XA_HEADS):
                        head_inverse(("kn", hd), xk_rinv[:, hd, :], MEM, sem("xkinv"))

            squares(4, xres, T, lambda k: M.wait_out(act, ("wo2", k)), between)
            inverse_rms(4, T)
            for c in range(4):
                for b in range(2):
                    move(("vx", c, b), vx[:, b, 256 * c:256 * (c + 1)], lambda o: o[:, 0:256])
                split_weights()
                for k in (2 * c, 2 * c + 1):
                    act.wait_ge(sem("h_raw"), KD * 3 + k + 1)
                    high(h_hi[:, k, :], h_raw[:, k, :], sem("h_hi"))
            act.wait_ge(sem("kx_ready"), 8)

            def query_inverse(hd):
                if hd >= 2:
                    act.wait_ge(sem("qx_ready"), 2 * (hd - 1))
                head_inverse(("qn", hd), xrinv[:, hd % 2, :], T, sem("xqinv"))

            for m in range(KD):
                move(("xq", m), qx[:, m, :])
                M.wait_out(act, ("xq", m))
                if m >= 4:
                    M.full(act, ("qn", m // 2 - 2))
                nc.scalar.activation(xsq[:, m % 4, :], qx[:, m, :], ACT.Square).then_inc(sem("xqsq_ready"), 1)
                split_after(m)
                if m % 2 == 0 and m:
                    query_inverse(m // 2 - 1)
            query_inverse(XA_HEADS - 1)
            N = XA_HEADS * NB
            for i in range(N + 6):
                if i < N:
                    M.wait_out(act, ("x", i))
                    if i >= 3:
                        TR.full(act, ("Tx", i - 3))
                        act.wait_ge(sem("xa_w"), i - 2)
                    nc.scalar.activation(xexp[:, i % 3, :], xneg[:, i % 3, :], ACT.Exp, scale=-1.0,
                                         bias=small[:, 8 + i % 3:9 + i % 3],
                                         accum_out=small[:, 11 + i % 3:12 + i % 3]).then_inc(sem("xa_exp"), 1)
                n = i - 2
                if 0 <= n < N:
                    move(("Tx", n), xpt[:, n % 3, :], lambda o: o[:, 0:MEM], TR)
                n = i - 5
                if 0 <= n < N and n % NB == NB - 1:
                    PV.wait_out(act, ("yx", n))
                    for m in (2 * (n // NB), 2 * (n // NB) + 1):
                        high(ox_hi[:, m, :], ox_raw[m // 4][:, m % 4, :], sem("xa_hi"))

            def before_ffn(k):
                split_after(k)
                act.wait_ge(sem("h_raw"), 4 * KD + k + 1)
                high(h_hi[:, k, :], h_raw[:, k, :], sem("h_hi"))

            squares(5, xres, T, lambda k: M.wait_out(act, ("xo", k)), before_ffn)
            inverse_rms(5, T, PV)
            nc.scalar.preload_act_table_set("gelu_and_others")

            for j in range(KF // 2 + 1):
                if j:
                    split_weights()
                if j < KF // 2:
                    split_weights()
                if j:
                    for m in (2 * j - 2, 2 * j - 1):
                        M.wait_out(act, ("up", m, 1))
                        high(gact_hi[:, m, :], gact_raw[:, m, :], sem("gact_hi"))
                if j < KF // 2:
                    for mi in range(2):
                        m = 2 * j + mi
                        act.wait_ge(sem("conv"), m + 1)
                        nc.scalar.activation(gact_raw[:, m, :], gact_raw[:, m, :], ACT.Gelu).then_inc(sem("gelu"), 1)
            for _ in range(DOWN):
                split_weights()
            assert chunks[0] == STREAM + DOWN + HI

        @block.vector
        def _(dve):
            links = [0]
            tt, ts, stt = nc.vector.tensor_tensor, nc.vector.tensor_scalar, nc.vector.scalar_tensor_tensor

            def link(ins):
                links[0] += 1
                ins.then_inc(sem("dve_link"), 1)
                dve.wait_ge(sem("dve_link"), links[0])

            def add_square(n, k, width):
                i = KD * n + k
                dve.wait_ge(sem("squares"), i + 1)
                s_ = sq[:, i % 2, 0:width]
                if k == 0:
                    if n:
                        (PV if n in (2, 3) else M).full(dve, ("norm", n - 1))
                    nc.vector.tensor_copy(acc[:, 0:width], s_).then_inc(sem("squares_added"), 1)
                else:
                    dve.wait_ge(sem("squares_added"), i)
                    tt(acc[:, 0:width], acc[:, 0:width], s_, ALU.add).then_inc(sem("squares_added"), 1)

            def low(lo, raw, hi, done):
                return tt(lo, raw, hi.bitcast(F32), ALU.subtract).then_inc(done, 1)

            def scaled(n, src, dst, g, width, done):
                dve.wait_ge(sem("rms_ready"), n + 1)
                for k in range(KD):
                    stt(dst[:, k, 0:width], src[:, k, 0:width], par(g, k), rms[:, 0:width], ALU.mult, ALU.mult)\
                        .then_inc(done, 1)

            def low_h(n, k, lo, raw, hi):
                dve.wait_ge(sem("h_hi"), KD * n + k + 1)
                low(lo[:, k, :], raw[:, k, :], hi[:, k, :], sem("h_ready"))

            def scaled_h(norm, n, g):
                dve.wait_ge(sem("rms_ready"), norm + 1)
                for k in range(KD + 2):
                    if k < KD:
                        stt(h_raw[:, k, :], xres[:, k, :], par(g, k), rms[:, :], ALU.mult, ALU.mult)\
                            .then_inc(sem("h_raw"), 1)
                    if k >= 2:
                        low_h(n, k - 2, h_lo, h_raw, h_hi)

            dve.wait_ge(sem("params_loaded"), 16)
            ts(nparams[:, :], params[:, 0:NCOLS], -1.0, None, ALU.mult).then_inc(sem("negated"), 1)
            tt(small[:, 0:2], par("lq", 0, 2), par("lk", 0, 2), ALU.mult).then_inc(sem("lam_products"), 1)
            ts(dq8[:, 0:1], par("dq_g"), HEAD ** -0.5, None, ALU.mult)
            link(ts(dq8[:, 1:2], par("subln"), 1.0 - LAMBDA_INIT, None, ALU.mult))
            for k in range(KD):
                add_square(0, k, T)
            def ada_sums(first, last):
                for i in range(first, last):
                    dve.wait_ge(sem(f"ada{i}_loaded"), 16)
                    total = ada_w[:, i, :, 0, :]
                    link(ts(total, total, par("c", 0), None, ALU.mult))
                    for k in range(1, KD):
                        ins = stt(total, ada_w[:, i, :, k, :], par("c", k), total, ALU.mult, ALU.add)
                        if k < KD - 1:
                            link(ins)
                    ins.then_inc(sem("ada_sums"), 1)

            ada_sums(0, ADA_FIRST)
            tt(gmix[:, :], par("final_g", 0, 8), par("mix_g", 0, 8), ALU.mult)
            dve.wait_ge(sem("wf_hi"), 1)
            tt(wf_lo, par("w_f", 0, 64), wf_hi.bitcast(F32), ALU.subtract).then_inc(sem("wf_split"), 1)
            M.wait_out(dve, "lam")
            link(tt(small[:, 4:5], small[:, 2:3], small[:, 3:4], ALU.subtract))
            link(ts(small[:, 5:6], small[:, 4:5], LAMBDA_INIT, -1.0, ALU.add, ALU.mult))
            nlam = small[:, 5:6]
            o = M.full(dve, "mod")
            tt(mod[:, 0:16], o[:, 0:16], par("b_ada", 0, 16), ALU.add).then_inc(M.out("mod"), 1)
            M.wait_out(dve, "mod")
            link(stt(gmod[:, :], mod[:, 8:16], 1.0, par("norm_g", 0, 8), ALU.add, ALU.mult))
            dve.wait_ge(sem("rms_ready"), 1)
            for k in range(KD + 2):
                if k < KD:
                    stt(h_raw[:, k, :], xres[:, k, :], gmod[:, k:k + 1], rms[:, :], ALU.mult, ALU.mult)\
                        .then_inc(sem("h_raw"), 1)
                if k >= 2:
                    dve.wait_ge(sem("h_hi"), k - 1)
                    stt(h_lo[:, k - 2, :], h_raw[:, k - 2, :], mod[:, k - 2:k - 1], h_hi[:, k - 2, :].bitcast(F32),
                        ALU.add, ALU.subtract).then_inc(sem("h_ready"), 1)
            for i, name in enumerate(("ident", "mask_strict", "mask_incl")):
                nc.vector.tensor_copy(masks[:, i, :], con(name)).then_inc(sem("masks"), 1)
            ada_sums(ADA_FIRST, ADA)
            o = M.full(dve, "gate")
            tt(mod[:, 16:24], o[:, 0:8], par("b_ada", 16, 8), ALU.add).then_inc(M.out("gate"), 1)

            def move(key, dst, src=None, ring_=M):
                o = ring_.full(dve, key)
                nc.vector.tensor_copy(dst, o if src is None else src(o)).then_inc(ring_.out(key), 1)

            def silu(tag, m):
                dve.wait_ge(sem("silu_gate"), 4 * (tag == "b") + m + 1)
                tt(gated[tag][:, m, :], gated[tag][:, m, :], z_gate[:, m % 2, :], ALU.mult).then_inc(sem("silu"), 1)

            for m in range(4):
                move(("ka", m), ka[:, m, :])
            for m in range(4):
                silu("a", m)
            for m in range(4):
                move(("kb", m), kb[:, m, :])
            fx, fa = nF_bc[0:HEADS, 0, :], nF_bc[0:HEADS, 1, :]
            dve.wait_ge(sem("f_ln"), 1)
            link(stt(fx, fx, 0.0, fa, ALU.max, ALU.add))
            nc.vector.tensor_tensor_scan(nF[0:HEADS, :], ones(T, HEADS), fx, 0.0, ALU.mult, ALU.add)\
                .then_inc(sem("nF_ready"), 1)

            N = HEADS * NB
            for i in range(N + 8):
                n = i - 4
                if 0 <= n < N:
                    end = P * (n % NB + 1)
                    move(("Ta", n), ptb[:, n % 3, 0:end], lambda o: o[:, 0:end], TR)
                if i < N:
                    end = P * (i % NB + 1)
                    o = M.full(dve, ("a", i))
                    sp, w = spb[:, i % 2, 0:end], wbuf[:, i % WBUF, 0:end]
                    dve.wait_ge(sem("stick_ln"), i + 1)
                    stt(sp, o[:, 0:end], 0.0, ebuf[:, i % 3, 0:end], ALU.max, ALU.add).then_inc(sem("stick_sp"), 1)
                    dve.wait_ge(sem("stick_sp"), i + 1)
                    if i >= WBUF:
                        TR.full(dve, ("Ta", i - WBUF))
                    link(nc.vector.tensor_tensor_scan(w[:, ::-1], ones(end), sp[:, ::-1], 0.0, ALU.mult, ALU.add))
                    tt(w, o[:, 0:end], w, ALU.subtract).then_inc(M.out(("a", i)), 1)
                if i % 4 == 3 and 16 < i < N:
                    silu("b", (i - 16) // 4)
                n = i - 7
                if 0 <= n < N and n % 8 == 7:
                    o = PV.full(dve, ("ya", n // 8))
                    g = gated["a"][:, n // 8, :]
                    tt(g, o, g, ALU.mult).then_inc(PV.out(("ya", n // 8)), 1)

            def soft(key, i, slot, width, bias, scale, neg, lowest):
                o = M.full(dve, key)
                nc.vector.tensor_tensor_reduce(neg[:, slot, 0:width], o[:, 0:width], bias, -scale, 3.0e38,
                                               ALU.add, ALU.min, lowest).then_inc(M.out(key), 1)

            for i in range(N + 6):
                if i < N:
                    hd, b = divmod(i, NB)
                    end = P * (b + 1)
                    if b == 0:
                        M.wait_out(dve, ("nF", hd))
                    if i >= 3:
                        dve.wait_ge(sem("fox_exp"), i - 2)
                    soft(("b", i), i, i % 3, end, nF_bc[:, hd % 2, 0:end], 1.0, negb, small[:, 8 + i % 3:9 + i % 3])
                n = i - 1
                if 0 <= n < N:
                    end = P * (n % NB + 1)
                    dve.wait_ge(sem("fox_exp"), n + 1)
                    link(nc.vector.reciprocal(small[:, 14 + n % 3:15 + n % 3], small[:, 11 + n % 3:12 + n % 3]))
                    w = expb[:, n % 3, 0:end]
                    ts(w, w, small[:, 14 + n % 3:15 + n % 3], None, ALU.mult).then_inc(sem("fox_w"), 1)
                n = i - 5
                if 0 <= n < N and n % 8 == 7:
                    o = PV.full(dve, ("yb", n // 8))
                    g = gated["b"][:, n // 8, :]
                    tt(g, o, g, ALU.mult).then_inc(PV.out(("yb", n // 8)), 1)

            for m in range(8):
                dve.wait_ge(sem("gated_hi"), m + 1)
                low(gated_lo[:, m, :], gated_raw[:, m, :], gated_hi[m], sem("gated_split"))
            dve.wait_ge(sem("gates"), 16)
            for m in range(KD):
                o = M.full(dve, ("oa", m))
                tt(gates[m], o, gates[m], ALU.mult).then_inc(M.out(("oa", m)), 1)
            for m in range(KD + 1):
                if m < KD:
                    o = M.full(dve, ("ob", m))
                    tt(gates[KD + m], o, gates[KD + m], ALU.mult).then_inc(M.out(("ob", m)), 1)
                    M.wait_out(dve, ("ob", m))
                    M.wait_out(dve, ("oa", m))
                    tt(merged_raw[:, m, :], gates[m], gates[KD + m], ALU.add).then_inc(sem("merged_raw"), 1)
                if m:
                    dve.wait_ge(sem("merged_hi"), m)
                    low(merged_lo[:, m - 1, :], merged_raw[:, m - 1, :], merged_hi[m - 1], sem("merged"))

            def residual(key, n, extra=None, gate=None):
                for m in range(KD + 1):
                    if m < KD:
                        o = M.full(dve, (key, m))
                        if gate is not None:
                            ins = stt(xres[:, m, :], o, gate(m), xres[:, m, :], ALU.mult, ALU.add)
                        else:
                            ins = tt(xres[:, m, :], o, xres[:, m, :], ALU.add)
                        ins.then_inc(M.out((key, m)), 1)
                        if extra is not None:
                            extra(m)
                    if m >= 1 and n is not None:
                        add_square(n, m - 1, T)
                if extra is not None:
                    extra(KD)

            def mixers_input(m):
                if m < KD:
                    M.wait_out(dve, ("wo", m))
                    ts(h_raw[:, m, :], xres[:, m, :], gmix[:, m:m + 1], None, ALU.mult).then_inc(sem("h_raw"), 1)
                if m >= 1:
                    low_h(1, m - 1, h_lo, h_raw, h_hi)

            residual("wo", 1, mixers_input, gate=lambda m: mod[:, 16 + m:17 + m])
            scaled(1, xres, xres, "final_g", T, sem("x2_ready"))
            for k in range(KD):
                add_square(2, k, T)
            dve.wait_ge(sem("rms_ready"), 3)
            tt(zscale, rms[:, :], rms2, ALU.mult).then_inc(sem("zscale"), 1)

            dve.wait_ge(sem("pads_zero"), 1)
            dve.wait_ge(sem("zscale"), 1)

            def token_scaled(key, dst):
                o = M.full(dve, key)
                tt(dst, o, zscale, ALU.mult).then_inc(M.out(key), 1)

            for m in range(8):
                if m:
                    dve.wait_ge(sem("zm"), m)
                z = zraw[:, m % 3, :]
                token_scaled(("zr", m), z[:, 1:T + 1])
                M.wait_out(dve, ("zr", m))
                link(tt(tA, z[:, 0:T], z[:, 1:T + 1], ALU.subtract))
                stt(zm[:, m, :], tA, par("mu", m), z[:, 1:T + 1], ALU.mult, ALU.add).then_inc(sem("zm"), 1)
            win = [at(MAT, POOL_W), at(MAT + 1024, POOL_W)]
            inv_count = con("inv_count", 2, T)
            dve.wait_ge(sem("mix_loaded"), 16)
            for j in range(2):
                token_scaled(("zp", j), pool_u[:, j, PAD:PAD + T])
                M.wait_out(dve, ("zp", j))
                u = pool_u[:, j, :]
                link(tt(win[0][:, 1:], u[:, 1:], u[:, :-1], ALU.add))
                link(tt(win[1][:, 3:], win[0][:, 3:], win[0][:, 1:-2], ALU.add))
                if j == 1:
                    link(tt(win[0][:, 7:], win[1][:, 7:], win[1][:, 3:-4], ALU.add))
                    link(tt(win[1][64:, 15:], win[0][64:, 15:], win[0][64:, 7:-8], ALU.add))
                for half in range(2):
                    rows = slice(64 * half, 64 * half + 64)
                    d = ycat03[rows, j, :]
                    link(tt(d, win[half][rows, PAD:], inv_count[rows, j, :], ALU.mult))
                    ins = tt(d, d, u[rows, PAD:], ALU.subtract)
                ins.then_inc(sem("pooled"), 1)
            def dq_out(first, last):
                for t in range(first, last):
                    token_scaled(("dq", t), dqk[:, t, :])

            dve.wait_ge(sem("x2_stored"), 16)
            dq_out(0, 2)
            dve.wait_ge(sem("lora_exp"), 1)
            ts(zm[0:64, 6, :], tA[0:64, :], -2.0, 1.0, ALU.mult, ALU.add).then_inc(sem("lora_in"), 1)

            dq_out(2, 4)
            def diff_soft(i):
                hd, b = divmod(i, NB)
                end = P * (b + 1)
                if i == 0:
                    dve.wait_ge(sem("dist_loaded"), 16)
                for cp in range(2):
                    if i >= 2:
                        dve.wait_ge(sem("diff_exp"), 2 * (i - 2) + cp + 1)
                    c = 2 * (i % 2) + cp
                    soft(("d", i, cp), i, c, end, dist[:, hd, T - end:T], 1.0, dneg, small[:, 32 + c:33 + c])

            def rwkv_center(j):
                o = M.full(dve, ("ymean", j))
                PV.wait_out(dve, ("yr", j))
                tt(tA, tA, o, ALU.subtract).then_inc(M.out(("ymean", j)), 1)

            def rwkv_out(j):
                dve.wait_ge(sem("y_rstd"), j + 1)
                link(tt(tA, tA, tB, ALU.mult))
                link(ts(tA, tA, par("ln_w", j), par("ln_b", j), ALU.mult, ALU.add))
                link(tt(tA, tA, bonus, ALU.add))
                tt(ycat03[:, 2 + j, :], tA, gout, ALU.mult).then_inc(sem("rwkv_out"), 1)

            for j in range(2):
                r_, k_, v_ = zm[:, j, :], zm[:, 2 + j, :], zm[:, 4 + j, :]
                ts(adec, k_, par("k_k", j), None, ALU.mult).then_inc(sem("kk0"), 1)
                dve.wait_ge(sem("rates"), 2 * j + 2)
                if j == 0:
                    dq_out(4, 5)
                o = M.full(dve, ("kk", j))
                ts(tB, o, float(HEAD), 1e-24, ALU.mult, ALU.max).then_inc(M.out(("kk", j)), 1)
                M.wait_out(dve, ("kk", j))
                nc.vector.engine_nop().then_inc(sem("kk_floor"), 1)
                link(ts(kvec, avec, 1.0, par("k_a", j), ALU.subtract, ALU.mult))
                link(stt(kvec, kvec, 1.0, k_, ALU.add, ALU.mult))
                stt(rst, r_, par("r_k", j), kvec, ALU.mult, ALU.mult).then_inc(sem("rk_ready"), 1)
                nc.vector.tensor_tensor_scan(tA, con("restart"), decay, 0.0, ALU.mult, ALU.subtract)\
                    .then_inc(sem("L_ready"), 1)
                dve.wait_ge(sem("L_ready"), 2 * j + 1)
                tt(decay, tA, decay, ALU.add).then_inc(sem("L_ready"), 1)
                dve.wait_ge(sem("kk_norm"), j + 1)
                link(tt(adec, adec, tB, ALU.mult))
                link(tt(bdec, avec, adec, ALU.mult))
                dve.wait_ge(sem("exps"), 4 * j + 4)
                tt(rdec, rdec, r_, ALU.mult).then_inc(sem("decayed"), 1)
                tt(bdec, bdec, kdec, ALU.mult).then_inc(sem("decayed"), 1)
                tt(kdec, kdec, kvec, ALU.mult).then_inc(sem("decayed"), 1)
                stt(adec, adec, -1.0, decay, ALU.mult, ALU.mult).then_inc(sem("decayed"), 1)
                o = M.full(dve, ("bonus", j))
                stt(bonus, o, float(HEAD), v_, ALU.mult, ALU.mult).then_inc(M.out(("bonus", j)), 1)
                if j == 0:
                    dq_out(5, 8)

                def spread(m):
                    return m.unsqueeze(1).broadcast_to([P, NB, P])

                four = lambda o: o.rearrange("p (a b) -> p a b", a=4)

                def masked(name, dst, mask):
                    for hh in range(2):
                        o = M.full(dve, (name, j, hh))
                        tt(dst[hh], four(o), spread(mask), ALU.mult).then_inc(M.out((name, j, hh)), 1)

                masked("A", Am, con("tri_lower"))
                masked("AT", AmT, con("tri_upper"))
                for hh in range(2):
                    M.wait_out(dve, ("AT", j, hh))
                    link(tt(Wm[hh], AmT[hh], spread(con("upper0")), ALU.mult))
                    tt(Wm[hh], Wm[hh], spread(ident), ALU.add).then_inc(sem("inverse"), 1)
                for lv in range(1, 6):
                    for hh in range(2):
                        move(("ZT", j, lv, hh), OmT[hh], four)
                    for hh in range(2):
                        dw = M.full(dve, ("dW", j, lv, hh))
                        if lv > 1:
                            M.wait_out(dve, ("dW", j, lv - 1, hh))
                        elif hh == 0:
                            dve.wait_ge(sem("inverse"), 2 * j + 2)
                        tt(Wm[hh], four(dw), Wm[hh], ALU.add).then_inc(M.out(("dW", j, lv, hh)), 1)
                    if j == 1 and lv >= 2:
                        for t in (2 * lv - 4, 2 * lv - 3):
                            dve.wait_ge(sem("qk_inverse"), t + 1)
                            g = dq8[:, 0:1] if t < 4 else par("dk_g")
                            stt(dqk[:, t, :], dqk[:, t, :], g, qk_rinv[t % 2], ALU.mult, ALU.mult)\
                                .then_inc(sem("dqk_ready"), 1)
                masked("Aak", AakT, con("tri_upper"))
                masked("Arb", ArbT, con("tri_incl"))
                masked("Ark", ArkT, con("tri_incl"))
                move(("Q", j), Qm.rearrange("p a b c -> p (a b c)"))
                half = lambda o: o[:, 0:256].rearrange("p (a b) -> p a b", a=NB)
                for odd in range(2):
                    o = M.full(dve, ("Mt", j, odd))
                    tt(Mt[:, odd::2, :], half(o), con("ident64").unsqueeze(1).broadcast_to([P, NB, CHUNK]), ALU.add)\
                        .then_inc(M.out(("Mt", j, odd)), 1)
                for odd in range(2):
                    o = M.full(dve, ("H0", j, odd))
                    tt(H0[:, odd::2, :], half(o), small[:, 24 + odd:32:2].unsqueeze(2).broadcast_to([P, NB, CHUNK]),
                       ALU.mult).then_inc(M.out(("H0", j, odd)), 1)
                for odd in range(2):
                    M.wait_out(dve, ("H0", j, odd))
                nc.vector.tensor_copy(St[:, 1, :], H0[:, 0, :]).then_inc(sem("state"), 1)
                o = M.full(dve, ("R", j))
                tt(rst, o, rdec, ALU.add).then_inc(M.out(("R", j)), 1)
                for c in range(1, NCH - 1):
                    o = TR.full(dve, ("S", j, c))
                    stt(St[:, c + 1, :], o[:, 0:CHUNK], small[:, 24 + c:25 + c], H0[:, c, :], ALU.mult, ALU.add)\
                        .then_inc(TR.out(("S", j, c)), 1)
                    if j == 1 and c % 2 == 1 and 0 <= (c - 3) // 2 < EARLY:
                        diff_soft((c - 3) // 2)
                if j == 0:
                    rwkv_center(0)
                    rwkv_out(0)

            N = DIFF_HEADS * NB
            for i in range(N + 8):
                if EARLY <= i < N:
                    diff_soft(i)
                if 4 <= i < 8:
                    for k in (2 * i - 8, 2 * i - 7):
                        add_square(3, k, MEM)
                if MEM_SUM + 1 <= i < MEM_SUM + 3:
                    dve.wait_ge(sem("rms_ready"), 4)
                    for k in range(4 * (i - MEM_SUM - 1), 4 * (i - MEM_SUM)):
                        stt(memn_raw[:, k, :], memn_raw[:, k, :], par("mem_g", k), rms[:, 0:MEM], ALU.mult, ALU.mult)\
                            .then_inc(sem("h_raw"), 1)
                if MEM_SUM + 3 <= i < MEM_SUM + 5:
                    for k in range(4 * (i - MEM_SUM - 3), 4 * (i - MEM_SUM - 2)):
                        low_h(2, k, memn_lo, memn_raw, memn_hi)
                if i == 2:
                    rwkv_center(1)
                n = i - 1
                if 0 <= n < N:
                    end = P * (n % NB + 1)
                    dve.wait_ge(sem("diff_exp"), 2 * n + 2)
                    c = 2 * (n % 2)
                    e0, e1 = (dexp[:, 2 * (n % 3) + cp, 0:end] for cp in range(2))
                    link(nc.vector.reciprocal(small[:, 40:42], small[:, 36 + c:38 + c]))
                    ts(small[:, 42:43], small[:, 41:42], nlam, None, ALU.mult)
                    link(ts(e0, e0, small[:, 40:41], None, ALU.mult))
                    stt(e0, e1, small[:, 42:43], e0, ALU.mult, ALU.add).then_inc(sem("diff_w"), 1)
                if i == 5:
                    rwkv_out(1)
                if 7 <= i < 11:
                    dve.wait_ge(sem("mixers_hi"), i - 6)
                    low(h_lo[:, i - 7, :], ycat03[:, i - 7, :], h_hi[:, i - 7, :], sem("mixers_split"))
                n = i - 6
                if 0 <= n < N and n % NB == NB - 1:
                    hd = n // NB
                    o = PV.full(dve, ("yd", hd))
                    dve.wait_ge(sem("oinv"), hd + 1)
                    stt(h_raw[:, 4 + hd, :], o, dq8[:, 1:2], drinv[:, hd % 2, :], ALU.mult, ALU.mult)\
                        .then_inc(PV.out(("yd", hd)), 1)
                n = i - 7
                if 0 <= n < N and n % NB == NB - 1:
                    hd = n // NB
                    dve.wait_ge(sem("mixers_hi"), 5 + hd)
                    low(h_lo[:, 4 + hd, :], h_raw[:, 4 + hd, :], h_hi[:, 4 + hd, :], sem("mixers_split"))

            def keys_scaled(m):
                if m == 4:
                    for k in range(KD):
                        dve.wait_ge(sem("xkinv"), k // 2 + 1)
                        stt(kx[:, k, :], kx[:, k, :], par("xk_g", k % 2), xk_rinv[:, k // 2, :], ALU.mult, ALU.mult)\
                            .then_inc(sem("kx_ready"), 1)

            dve.wait_ge(sem("x2_back"), 16)
            residual("wo2", 4, keys_scaled)

            scaled_h(4, 3, "xa_g")
            for m in range(KD):
                dve.wait_ge(sem("xqinv"), m // 2 + 1)
                stt(qx[:, m, :], qx[:, m, :], par("xq_g", m % 2), xrinv[:, m // 2 % 2, :], ALU.mult, ALU.mult)\
                    .then_inc(sem("qx_ready"), 1)
            N = XA_HEADS * NB
            zeros = small[:, 63:64].broadcast_to([P, MEM])
            for i in range(N + 6):
                if i < N:
                    if i >= 3:
                        dve.wait_ge(sem("xa_exp"), i - 2)
                    soft(("x", i), i, i % 3, MEM, zeros, 256 ** -0.5, xneg, small[:, 8 + i % 3:9 + i % 3])
                n = i - 1
                if 0 <= n < N:
                    dve.wait_ge(sem("xa_exp"), n + 1)
                    link(nc.vector.reciprocal(small[:, 14 + n % 3:15 + n % 3], small[:, 11 + n % 3:12 + n % 3]))
                    w = xexp[:, n % 3, :]
                    ts(w, w, small[:, 14 + n % 3:15 + n % 3], None, ALU.mult).then_inc(sem("xa_w"), 1)
                n = i - 4
                if 0 <= n < N:
                    hd, b = divmod(n, NB)
                    move(("yx", n), ox_raw[hd // 2][:, 2 * (hd % 2):2 * (hd % 2) + 2, P * b:P * (b + 1)],
                         lambda o: o[:, 0:2 * P].rearrange("p (j n) -> p j n", j=2), PV)
                n = i - 5
                if 0 <= n < N and n % NB == NB - 1:
                    for m in (2 * (n // NB), 2 * (n // NB) + 1):
                        dve.wait_ge(sem("xa_hi"), m + 1)
                        low(ox_lo[m // 4][:, m % 4, :], ox_raw[m // 4][:, m % 4, :], ox_hi[:, m, :], sem("xa_split"))

            def ffn_input(m):
                if m < KD:
                    M.wait_out(dve, ("xo", m))
                    ts(h_raw[:, m, :], xres[:, m, :], par("ffn_g", m), None, ALU.mult).then_inc(sem("h_raw"), 1)
                if m >= 1:
                    low_h(4, m - 1, h_lo, h_raw, h_hi)

            residual("xo", 5, ffn_input)

            dve.wait_ge(sem("conv_zero"), 1)
            dve.wait_ge(sem("rms_ready"), 6)
            for j in range(KF // 2 + 1):
                if j < KF // 2:
                    for mi in range(2):
                        m = 2 * j + mi
                        a, c = conv_in[:, m % 3, :], gact_raw[:, m, :]
                        if m >= 3:
                            dve.wait_ge(sem("conv"), m - 2)
                        o = M.full(dve, ("up", m, 0))
                        tt(a[:, 2:T + 2], o, rms[:, :], ALU.mult).then_inc(M.out(("up", m, 0)), 1)
                        M.wait_out(dve, ("up", m, 0))
                        link(ts(c, a[:, 0:T], par("conv_w", m), par("conv_b", m), ALU.mult, ALU.add))
                        link(stt(c, a[:, 1:T + 1], par("conv_w", KF + m), c, ALU.mult, ALU.add))
                        stt(c, a[:, 2:T + 2], par("conv_w", 2 * KF + m), c, ALU.mult, ALU.add).then_inc(sem("conv"), 1)
                if j:
                    for m in (2 * j - 2, 2 * j - 1):
                        dve.wait_ge(sem("gact_hi"), m + 1)
                        low(gact_lo[:, m, :], gact_raw[:, m, :], gact_hi[:, m, :], sem("gact_split"))
                if j < KF // 2:
                    for mi in range(2):
                        m = 2 * j + mi
                        dve.wait_ge(sem("gelu"), m + 1)
                        link(tt(gact_raw[:, m, :], gact_raw[:, m, :], rms[:, :], ALU.mult))
                        o = M.full(dve, ("up", m, 1))
                        tt(gact_raw[:, m, :], o, gact_raw[:, m, :], ALU.mult).then_inc(M.out(("up", m, 1)), 1)
            residual("down", None)

        @block.gpsimd
        def _(pool):
            def low_weights(first, last):
                for c in range(first, last):
                    n = CHUNK_F if c < STREAM else DOWN_K * P
                    raw, lo = w_raw[:, c % RAW, 0:n], w_lo[:, c % RAW, 0:n]
                    pool.wait_ge(sem("weights_hi"), c + 1)
                    nc.gpsimd.tensor_tensor(lo, raw, w_hi[:, c % HI, 0:n].bitcast(F32), ALU.subtract)\
                        .then_inc(sem("weights_split"), 1)

            nc.gpsimd.memset(small[:, 63:64], 0.0).then_inc(sem("fills"), 1)
            mixers = chunk_end.index(("zr", 1))
            low_weights(0, mixers + HI)
            pool.wait_ge(sem("x2_ready"), 1)
            for s in range(3):
                nc.gpsimd.memset(zraw[:, s, 0:1], 0.0)
            for j in range(2):
                ins = nc.gpsimd.memset(pool_u[:, j, 0:PAD], 0.0)
            ins.then_inc(sem("pads_zero"), 1)
            diff = chunk_end.index(("dq", 7)) + 1
            low_weights(mixers + HI, diff + HI)
            pool.wait_ge(sem("mix_loaded"), 16)
            lower = con("lower", 5, P)
            for j in range(2):
                if j == 1:
                    low_weights(diff + HI, diff + 2 * HI)
                for lv in range(1, 6):
                    for hh in range(2):
                        if lv == 1:
                            M.wait_out(pool, ("A", j, hh))
                        else:
                            M.full(pool, ("ZT", j, lv - 1, hh))
                        nc.gpsimd.tensor_tensor(Om[hh], Am[hh], lower[:, lv - 1, :].unsqueeze(1).broadcast_to([P, NB, P]),
                                                ALU.mult).then_inc(sem("corner"), 1)
            up = chunk_end.index(("up", 1, 0))
            low_weights(diff + 2 * HI, up + HI)
            pool.wait_ge(sem("h_raw"), 4 * KD + 1)
            for s in range(3):
                ins = nc.gpsimd.memset(conv_in[:, s, 0:2], 0.0)
            ins.then_inc(sem("conv_zero"), 1)
            low_weights(up + HI, STREAM + DOWN)

        @block.sync
        def _(sp):
            sp.dma_start(xres[:, :, :], x_in).then_inc(sem("x_loaded"), 16)
            sp.dma_start(params[:, 0:LATE_PARAM], params_in[:, 0:LATE_PARAM]).then_inc(sem("params_loaded"), 16)
            sp.dma_start(consts[:, 0:LATE_COL], consts_in[:, 0:LATE_COL]).then_inc(sem("consts_loaded"), 16)
            for i in range(ADA):
                sp.dma_start(at(4096 * i, 2, CHUNK_F), ada_in[2 * i:2 * i + 2].rearrange("c p n -> p c n"))\
                    .then_inc(sem(f"ada{i}_loaded"), 16)
                if i == ADA_FIRST - 1:
                    for c in range(RAW):
                        sp.dma_start(w_raw[:, c, :], stream_in[c]).then_inc(loaded[c], 16)
            sp.dma_start(params[:, LATE_PARAM:], params_in[:, LATE_PARAM:]).then_inc(sem("late_loaded"), 16)
            sp.dma_start(consts[:, LATE_COL:], consts_in[:, LATE_COL:MIX_COL]).then_inc(sem("late_loaded"), 16)
            rounds = STREAM // RAW
            with sp.Fori(1, rounds) as i:
                for s in range(RAW):
                    sp.wait_ge(used[s], i)
                    sp.dma_start(w_raw[:, s, :], stream_in[bass.ds(i * RAW + s, 1), :, :].rearrange("a p n -> p (a n)"))\
                        .then_inc(loaded[s], 16)
            for c in range(rounds * RAW, STREAM):
                sp.wait_ge(used[c % RAW], c // RAW)
                sp.dma_start(w_raw[:, c % RAW, :], stream_in[c]).then_inc(loaded[c % RAW], 16)
            width = DOWN_K * P
            rounds = DOWN // RAW
            with sp.Fori(0, rounds) as i:
                for s in range(RAW):
                    slot = (STREAM + s) % RAW
                    sp.wait_ge(used[slot], i + (STREAM + s) // RAW)
                    sp.dma_start(w_raw[:, slot, 0:width],
                                 down_in[bass.ds(i * RAW + s, 1), :, :].rearrange("a p n -> p (a n)"))\
                        .then_inc(loaded[slot], 16)
            for c in range(rounds * RAW, DOWN):
                slot = (STREAM + c) % RAW
                sp.wait_ge(used[slot], (STREAM + c) // RAW)
                sp.dma_start(w_raw[:, slot, 0:width], down_in[c]).then_inc(loaded[slot], 16)
            for m in range(KD):
                M.wait_out(sp, ("down", m))
                sp.dma_start(out[:, m, :], xres[:, m, :]).then_inc(sem("stored"), 16)
            sp.wait_ge(sem("stored"), 16 * KD)


def columns(v, n):
    return np.asarray(v, np.float32).reshape(n, P).T


def lay_params(a):
    out = np.zeros((P, NPARAM), np.float32)

    def put(name, value):
        i, n = PARAM_COLS[name]
        out[0:value.shape[0], i:i + n] = value

    for name, key in (("c", "c"), ("b_ada", "b_ada"), ("norm_g", "norm_g"), ("b_gate", "b_gate"),
                      ("final_g", "final_g"), ("mix_g", "mix_norm_g_2"), ("pool_scale", "pool_scale_2"),
                      ("mu", "rwkv_mu_2"), ("w0", "rwkv_w0_2"), ("a0", "rwkv_a0_2"), ("k_k", "rwkv_k_k_2"),
                      ("k_a", "rwkv_k_a_2"), ("r_k", "rwkv_r_k_2"), ("ln_w", "rwkv_ln_w_2"),
                      ("ln_b", "rwkv_ln_b_2"), ("dq_g", "diff_q_norm_2"), ("dk_g", "diff_k_norm_2"),
                      ("subln", "diff_subln_2"), ("xa_g", "xa_norm_g_2"), ("mem_g", "mem_norm_g_2"),
                      ("xq_g", "xa_q_norm_2"), ("xk_g", "xa_k_norm_2"), ("ffn_g", "ffn_norm_g_2"),
                      ("conv_w", "ffn_conv_w_2"), ("conv_b", "ffn_conv_b_2")):
        put(name, columns(a[key], PARAM_COLS[name][1]))
    for name, keys in (("lq", ("diff_lq1_2", "diff_lq2_2")), ("lk", ("diff_lk1_2", "diff_lk2_2"))):
        two = np.zeros((HEAD, 2), np.float32)
        for i, key in enumerate(keys):
            two[:, i] = np.asarray(a[key]).reshape(-1)
        put(name, two)
    put("b_forget", np.asarray(a["b_forget"]).reshape(HEADS, 1))
    w_f = np.asarray(a["w_in"])[0][:, 4096:4096 + HEADS]
    put("w_f", w_f.reshape(KD, P, HEADS).transpose(1, 0, 2).reshape(P, -1))
    put("lora", np.concatenate([np.asarray(a["rwkv_w2_2"])[0], np.asarray(a["rwkv_a2_2"])[0]], 0))
    put("g2", np.asarray(a["rwkv_g2_2"])[0])
    w = np.asarray(a["pool_w_2"])[0]
    blocks = np.zeros((P, 2, P), np.float32)
    for g in range(4):
        r = HEAD * (g % 2)
        blocks[r:r + HEAD, g // 2, r:r + HEAD] = w[g]
    put("pool_w", blocks.reshape(P, -1))
    return out


def lay_chunks(w, cols):
    k, n = w.shape
    return w.reshape(k // P, P, n // cols, cols).transpose(2, 1, 0, 3).reshape(n // cols, P, -1)


def lay_stream(a):
    w_in, w_in2, up = (np.asarray(a[k])[0] for k in ("w_in", "w_in_2", "ffn_w_up_2"))
    parts = []
    for i in (0, 1, 2, 3, 4, 5, 6, 7):
        parts.append(lay_chunks(w_in[:, 512 * i:512 * (i + 1)], 256))
    parts.append(lay_chunks(w_in[:, 4096 + HEADS:], 256))
    parts.append(lay_chunks(np.asarray(a["w_o_sb"])[0], 512))
    parts.append(lay_chunks(np.asarray(a["w_o_fox"])[0], 512))
    parts.append(lay_chunks(np.asarray(a["w_out"])[0], 256))
    parts.append(lay_chunks(w_in2[:, 256:1280], 256))
    parts.append(lay_chunks(w_in2[:, 0:256], 256))
    parts.append(lay_chunks(w_in2[:, 1280:], 256))
    for key in ("xa_wk_2", "w_out_2", "xa_wv_2", "xa_wq_2", "xa_wo_2"):
        parts.append(lay_chunks(np.asarray(a[key])[0], 256))
    halves = [lay_chunks(up[:, FFN * i:FFN * (i + 1)], 256) for i in range(2)]
    parts.append(np.stack(halves, 1).reshape(2 * halves[0].shape[0], P, -1))
    return np.ascontiguousarray(np.concatenate(parts, 0))


def lay_down(w):
    return np.ascontiguousarray(
        w.reshape(2, DOWN_K, P, KD, P).transpose(3, 0, 2, 1, 4).reshape(DOWN, P, DOWN_K * P))


def kernel(**inputs):
    from concourse import bacc as _bacc
    from concourse.bass_utils import run_bass_kernel_spmd as _run

    a = {k: np.asarray(v) for k, v in inputs.items()}
    rows = lambda v: np.ascontiguousarray(v.T.reshape(KD, P, -1).transpose(1, 0, 2))
    arrays = {
        "x": rows(a["x"][0]),
        "mem": rows(a["mem_2"][0]),
        "params": lay_params(a),
        "consts": shape_constants(),
        "ada": lay_chunks(np.asarray(a["w_ada"])[0], 256),
        "stream": lay_stream(a),
        "down": lay_down(a["ffn_w_down_2"][0]),
    }
    nc = _bacc.Bacc("TRN2", target_bir_lowering=False, num_devices=1)
    ins = [nc.dram_tensor("in_" + n, list(v.shape), F32, kind="ExternalInput").ap() for n, v in arrays.items()]
    out = nc.dram_tensor("out", [P, KD, T], F32, kind="ExternalOutput").ap()
    x2_kept = nc.dram_tensor("x2_kept", [P, KD, T], F32, kind="Internal").ap()
    build(nc, *ins, out, x2_kept)
    r = _run(nc, [{"in_" + n: v for n, v in arrays.items()}], core_ids=[0])
    got = r.results[0]["out"]
    return np.ascontiguousarray(got.transpose(1, 0, 2).reshape(D, T).T)[None]
```
